# Optimizing a Trainium2 kernel written in Bass

```python
import jax, jax.numpy as jnp
from jax import lax
import numpy as np

D_MODEL = 1024
BATCH = 1
SEQ = 1024
DEPTH = 1

N_MEM = 256
D_MIX = D_MODEL
D_A = D_MIX // 4
D_B = D_MIX // 4
D_C = D_MIX // 2
H_A = 4
H_B = 4
H_C = 4
DH_A = D_A // H_A
DH_B = D_B // H_B
DH_C = D_C // H_C
CHUNK = 128
CONV_B = 31
CONV_C = 4
CONV_F = 3
N_XHEADS = 4
DH_X = D_MODEL // N_XHEADS
D_FF = ((8 * D_MODEL // 3 + 255) // 256) * 256
D_IN = 2 * D_A + 2 * D_B + 2 * D_C + 2 * H_C
RMS_EPS = 1e-6
LN_EPS = 1e-5


def rmsnorm(x, g):
    xf = x.astype(jnp.float32)
    y = xf * lax.rsqrt(jnp.mean(xf * xf, axis=-1, keepdims=True) + RMS_EPS)
    return (y * g.astype(jnp.float32)).astype(x.dtype)

def standardize(x):
    xf = x.astype(jnp.float32)
    mu = jnp.mean(xf, axis=-1, keepdims=True)
    var = jnp.mean(jnp.square(xf - mu), axis=-1, keepdims=True)
    return (xf - mu) * lax.rsqrt(var + LN_EPS)

def causal_dwconv(x, w, b):
    K, C = w.shape
    y = lax.conv_general_dilated(
        x, w[:, None, :].astype(x.dtype), window_strides=(1,),
        padding=[(K - 1, 0)], dimension_numbers=('NWC', 'WIO', 'NWC'),
        feature_group_count=C)
    return y + b.astype(x.dtype)

def gmlp_spatial_gating(u, v, ln_g, ln_b, w_s, b_s):
    Bsz, S, _ = v.shape
    vn = (standardize(v) * ln_g + ln_b).astype(v.dtype)
    vn = vn.reshape(Bsz, S // CHUNK, CHUNK, H_A, DH_A)
    mask = jnp.tril(jnp.ones((CHUNK, CHUNK), dtype=bool))
    w = jnp.where(mask, w_s, 0.0).astype(v.dtype)
    s = jnp.einsum('hts,bcshd->bcthd', w, vn) + b_s.T.astype(v.dtype)[None, None, :, :, None]
    return u * s.reshape(Bsz, S, D_A)

def conformer_conv(a, g, conv_w, conv_b, gn_g, gn_b):
    Bsz, S, _ = a.shape
    y = a * jax.nn.sigmoid(g)
    y = causal_dwconv(y, conv_w, conv_b)
    yn = standardize(y.reshape(Bsz, S, H_B, DH_B)).reshape(Bsz, S, D_B)
    y = (yn * gn_g + gn_b).astype(a.dtype)
    return jax.nn.silu(y)

def mlstm_chunkwise(q, k, v, logi, logf):
    Bsz, H, S, DH = q.shape
    NC = S // CHUNK
    q = q * (DH ** -0.5)

    def to_chunks(a):
        a = a.reshape((Bsz, H, NC, CHUNK) + a.shape[3:])
        return jnp.moveaxis(a, 2, 0)

    qc, kc, vc, ic, fc = (to_chunks(t) for t in (q, k, v, logi, logf))
    mask = jnp.tril(jnp.ones((CHUNK, CHUNK), dtype=bool))

    def step(carry, inp):
        C, n, m = carry
        qt, kt, vt, it, ft = inp
        bcum = jnp.cumsum(ft, axis=-1)
        dmat = bcum[..., :, None] - bcum[..., None, :] + it[..., None, :]
        dmat = jnp.where(mask, dmat, -jnp.inf)
        inter = bcum + m[..., None]
        m_t = jnp.maximum(inter, jnp.max(dmat, axis=-1))
        w_intra = jnp.exp(dmat - m_t[..., None])
        w_inter = jnp.exp(inter - m_t)
        scores = jnp.einsum('bhtd,bhsd->bhts', qt, kt) * w_intra
        num = (w_inter[..., None] * jnp.einsum('bhtd,bhde->bhte', qt, C)
               + jnp.einsum('bhts,bhse->bhte', scores, vt))
        den = w_inter * jnp.einsum('bhtd,bhd->bht', qt, n) + jnp.sum(scores, axis=-1)
        h = num / jnp.maximum(jnp.abs(den), jnp.exp(-m_t))[..., None]
        btot = bcum[..., -1]
        gdec = btot[..., None] - bcum + it
        m_new = jnp.maximum(btot + m, jnp.max(gdec, axis=-1))
        decay = jnp.exp(btot + m - m_new)
        wg = jnp.exp(gdec - m_new[..., None])
        C_new = decay[..., None, None] * C + jnp.einsum('bhs,bhsd,bhse->bhde', wg, kt, vt)
        n_new = decay[..., None] * n + jnp.einsum('bhs,bhsd->bhd', wg, kt)
        return (C_new, n_new, m_new), h

    init = (jnp.zeros((Bsz, H, DH, DH), jnp.float32),
            jnp.zeros((Bsz, H, DH), jnp.float32),
            jnp.zeros((Bsz, H), jnp.float32))
    _, hs = lax.scan(step, init, (qc, kc, vc, ic, fc))
    return jnp.moveaxis(hs, 0, 2).reshape(Bsz, H, S, DH)

def mlstm_group(xc, oc, gi, gf, b_igate, b_fgate, conv_w, conv_b, w_q, w_k, w_v, hn_g, skip):
    Bsz, S, _ = xc.shape
    xconv = jax.nn.silu(causal_dwconv(xc, conv_w, conv_b))
    xh = xconv.reshape(Bsz, S, H_C, DH_C)
    xv = xc.reshape(Bsz, S, H_C, DH_C)
    q = jnp.einsum('bshd,hde->bhse', xh, w_q).astype(jnp.float32)
    k = jnp.einsum('bshd,hde->bhse', xh, w_k).astype(jnp.float32)
    v = jnp.einsum('bshd,hde->bhse', xv, w_v).astype(jnp.float32)
    logi = jnp.transpose(gi.astype(jnp.float32) + b_igate.astype(jnp.float32), (0, 2, 1))
    logf = jax.nn.log_sigmoid(jnp.transpose(gf.astype(jnp.float32) + b_fgate.astype(jnp.float32), (0, 2, 1)))
    hcell = mlstm_chunkwise(q, k, v, logi, logf)
    hcell = jnp.transpose(hcell, (0, 2, 1, 3))
    hnorm = (standardize(hcell) * hn_g.reshape(H_C, DH_C)).reshape(Bsz, S, D_C).astype(xc.dtype)
    return jax.nn.sigmoid(oc) * (hnorm + skip * xconv)

def hybrid_mixer(hn, w_in, b_igate, b_fgate, ln_a_g, ln_a_b, w_s, b_s,
                 conv_b_w, conv_b_b, gn_b_g, gn_b_b, conv_c_w, conv_c_b,
                 w_q_c, w_k_c, w_v_c, hn_c_g, skip_c, w_out):
    z = hn @ w_in
    o0 = 2 * D_A
    o1 = o0 + 2 * D_B
    o2 = o1 + D_C
    o3 = o2 + D_C
    o4 = o3 + H_C
    za = jax.nn.gelu(z[..., :o0], approximate=False)
    y_a = gmlp_spatial_gating(za[..., :D_A], za[..., D_A:], ln_a_g, ln_a_b, w_s, b_s)
    zb = z[..., o0:o1]
    y_b = conformer_conv(zb[..., :D_B], zb[..., D_B:], conv_b_w, conv_b_b, gn_b_g, gn_b_b)
    y_c = mlstm_group(z[..., o1:o2], z[..., o2:o3], z[..., o3:o4], z[..., o4:],
                      b_igate, b_fgate, conv_c_w, conv_c_b, w_q_c, w_k_c, w_v_c, hn_c_g, skip_c)
    return jnp.concatenate([y_a, y_b, y_c], axis=-1) @ w_out

def cross_attention(hn, mn, w_xq, w_xkv, w_xo):
    Bsz, S, _ = hn.shape
    M = mn.shape[1]
    q = (hn @ w_xq).reshape(Bsz, S, N_XHEADS, DH_X)
    kv = mn @ w_xkv
    k = kv[..., :D_MODEL].reshape(Bsz, M, N_XHEADS, DH_X)
    v = kv[..., D_MODEL:].reshape(Bsz, M, N_XHEADS, DH_X)
    s = jnp.einsum('bshd,bmhd->bhsm', q, k).astype(jnp.float32) * (DH_X ** -0.5)
    p = jax.nn.softmax(s, axis=-1).astype(v.dtype)
    o = jnp.einsum('bhsm,bmhd->bshd', p, v).reshape(Bsz, S, D_MODEL)
    return o @ w_xo

def conv_glu(hn, w_up, conv_f_w, conv_f_b, w_down):
    up = hn @ w_up
    gate = jax.nn.gelu(causal_dwconv(up[..., :D_FF], conv_f_w, conv_f_b), approximate=False)
    return (gate * up[..., D_FF:]) @ w_down

def first_inputs(seed: int = 0) -> dict:
    key = jax.random.key(seed)
    ks = iter(jax.random.split(key, 48))

    def nrm(shape, scale):
        return jax.random.normal(next(ks), shape, jnp.float32) * scale

    L = DEPTH
    return {
        "x": nrm((BATCH, SEQ, D_MODEL), 1.0),
        "mem": nrm((BATCH, N_MEM, D_MODEL), 1.0),
        "norm_mix_g": 1.0 + nrm((L, D_MODEL), 0.02),
        "w_in": nrm((L, D_MODEL, D_IN), D_MODEL ** -0.5),
        "b_igate": nrm((L, H_C), 0.1),
        "b_fgate": jax.random.uniform(next(ks), (L, H_C), jnp.float32, 3.0, 6.0),
        "ln_a_g": 1.0 + nrm((L, D_A), 0.02),
        "ln_a_b": nrm((L, D_A), 0.02),
        "w_s": nrm((L, H_A, CHUNK, CHUNK), CHUNK ** -0.5),
        "b_s": 1.0 + nrm((L, H_A, CHUNK), 0.1),
        "conv_b_w": nrm((L, CONV_B, D_B), CONV_B ** -0.5),
        "conv_b_b": nrm((L, D_B), 0.02),
        "gn_b_g": 1.0 + nrm((L, D_B), 0.02),
        "gn_b_b": nrm((L, D_B), 0.02),
        "conv_c_w": nrm((L, CONV_C, D_C), CONV_C ** -0.5),
        "conv_c_b": nrm((L, D_C), 0.02),
        "w_q_c": nrm((L, H_C, DH_C, DH_C), DH_C ** -0.5),
        "w_k_c": nrm((L, H_C, DH_C, DH_C), DH_C ** -0.5),
        "w_v_c": nrm((L, H_C, DH_C, DH_C), DH_C ** -0.5),
        "hn_c_g": 1.0 + nrm((L, D_C), 0.02),
        "skip_c": 1.0 + nrm((L, D_C), 0.02),
        "w_out": nrm((L, D_MIX, D_MODEL), D_MIX ** -0.5),
        "norm_x_g": 1.0 + nrm((L, D_MODEL), 0.02),
        "norm_mem_g": 1.0 + nrm((L, D_MODEL), 0.02),
        "w_xq": nrm((L, D_MODEL, D_MODEL), D_MODEL ** -0.5),
        "w_xkv": nrm((L, D_MODEL, 2 * D_MODEL), D_MODEL ** -0.5),
        "w_xo": nrm((L, D_MODEL, D_MODEL), D_MODEL ** -0.5),
        "norm_ffn_g": 1.0 + nrm((L, D_MODEL), 0.02),
        "w_up": nrm((L, D_MODEL, 2 * D_FF), D_MODEL ** -0.5),
        "conv_f_w": nrm((L, CONV_F, D_FF), CONV_F ** -0.5),
        "conv_f_b": nrm((L, D_FF), 0.02),
        "w_down": nrm((L, D_FF, D_MODEL), D_FF ** -0.5),
        "final_g": 1.0 + nrm((D_MODEL,), 0.02),
    }

def first_block(x, mem, norm_mix_g, w_in, b_igate, b_fgate, ln_a_g, ln_a_b, w_s, b_s,
              conv_b_w, conv_b_b, gn_b_g, gn_b_b, conv_c_w, conv_c_b,
              w_q_c, w_k_c, w_v_c, hn_c_g, skip_c, w_out,
              norm_x_g, norm_mem_g, w_xq, w_xkv, w_xo,
              norm_ffn_g, w_up, conv_f_w, conv_f_b, w_down, final_g):
    h = x
    for l in range(DEPTH):
        hn = rmsnorm(h, norm_mix_g[l])
        h = h + hybrid_mixer(hn, w_in[l], b_igate[l], b_fgate[l], ln_a_g[l], ln_a_b[l],
                             w_s[l], b_s[l], conv_b_w[l], conv_b_b[l], gn_b_g[l], gn_b_b[l],
                             conv_c_w[l], conv_c_b[l], w_q_c[l], w_k_c[l], w_v_c[l],
                             hn_c_g[l], skip_c[l], w_out[l])
        hn = rmsnorm(h, norm_x_g[l])
        mn = rmsnorm(mem, norm_mem_g[l])
        h = h + cross_attention(hn, mn, w_xq[l], w_xkv[l], w_xo[l])
        hn = rmsnorm(h, norm_ffn_g[l])
        h = h + conv_glu(hn, w_up[l], conv_f_w[l], conv_f_b[l], w_down[l])
    return rmsnorm(h, final_g)


CHUNK_2 = 64
D_MIX_2 = D_MODEL
SWA_HEAD_DIM = 64
SWA_HEADS = (D_MIX_2 // 2) // SWA_HEAD_DIM
SWA_KV_HEADS = 2
SWA_WIDTH = SWA_HEADS * SWA_HEAD_DIM
SWA_KV_WIDTH = SWA_KV_HEADS * SWA_HEAD_DIM
WINDOW = 128
WINDOW_CHUNKS = WINDOW // CHUNK_2
HGRN_HEAD_DIM = 128
HGRN_WIDTH = D_MIX_2 - SWA_WIDTH
HGRN_HEADS = HGRN_WIDTH // HGRN_HEAD_DIM
IN_SIZES = (SWA_WIDTH, SWA_KV_WIDTH, SWA_KV_WIDTH,
            HGRN_WIDTH, HGRN_WIDTH, HGRN_WIDTH, HGRN_WIDTH)
D_IN_2 = sum(IN_SIZES)
IN_SPLITS = [int(v) for v in np.cumsum(IN_SIZES)[:-1]]
MEM_LEN = 256
XATTN_HEADS = 4
XATTN_HEAD_DIM = D_MODEL // XATTN_HEADS
D_FF_2 = ((8 * D_MODEL // 3 + 255) // 256) * 256
NEG_INF = -1e30


def rms_norm(x, g):
    xf = x.astype(jnp.float32)
    y = xf * lax.rsqrt(jnp.mean(xf * xf, axis=-1, keepdims=True) + RMS_EPS)
    return (y * g.astype(jnp.float32)).astype(x.dtype)

def swa_with_sinks(q, k, v, sinks):
    B, T, Hq, Dh = q.shape
    Hkv = k.shape[2]
    G = Hq // Hkv
    NC = T // CHUNK_2
    WC = WINDOW_CHUNKS
    L = (WC + 1) * CHUNK_2
    qc = q.reshape(B, NC, CHUNK_2, Hkv, G, Dh)
    pad = ((0, 0), (WC * CHUNK_2, 0), (0, 0), (0, 0))
    kc = jnp.pad(k, pad).reshape(B, NC + WC, CHUNK_2, Hkv, Dh)
    vc = jnp.pad(v, pad).reshape(B, NC + WC, CHUNK_2, Hkv, Dh)
    kband = jnp.concatenate([kc[:, j:j + NC] for j in range(WC + 1)], axis=2)
    vband = jnp.concatenate([vc[:, j:j + NC] for j in range(WC + 1)], axis=2)
    band_chunk = jnp.arange(NC)[:, None] - WC + jnp.arange(WC + 1)[None, :]
    valid = jnp.repeat(band_chunk >= 0, CHUNK_2, axis=1)
    s = jnp.einsum('bnqhgd,bnkhd->bnhgqk', qc, kband).astype(jnp.float32) * (Dh ** -0.5)
    s = jnp.where(valid[None, :, None, None, None, :], s, NEG_INF)
    sink = jnp.broadcast_to(sinks.astype(jnp.float32).reshape(1, 1, Hkv, G, 1, 1),
                            (B, NC, Hkv, G, CHUNK_2, 1))
    p = jax.nn.softmax(jnp.concatenate([s, sink], axis=-1), axis=-1)[..., :L]
    o = jnp.einsum('bnhgqk,bnkhd->bnqhgd', p.astype(v.dtype), vband)
    return o.reshape(B, T, Hq * Dh)

def hgrn2(q, f_logit, i, g, lb, onorm_g):
    B, T, H, Dk = q.shape
    Dv = i.shape[-1]
    NC = T // CHUNK_2
    f32 = jnp.float32
    qf = jax.nn.silu(q.astype(f32)) * (Dk ** -0.5)
    lbf = lb.astype(f32)
    f = lbf + (1.0 - lbf) * jax.nn.sigmoid(f_logit.astype(f32))
    kf = 1.0 - f
    logf = jnp.log(f)

    def chunks(a):
        return a.reshape(B, NC, CHUNK_2, H, a.shape[-1]).transpose(0, 3, 1, 2, 4)

    qc, kc, vc, lc = chunks(qf), chunks(kf), chunks(i.astype(f32)), chunks(logf)
    b = jnp.cumsum(lc, axis=3)
    b_mid = b[:, :, :, CHUNK_2 // 2 - 1:CHUNK_2 // 2]
    b_last = b[:, :, :, CHUNK_2 - 1:CHUNK_2]
    A = jnp.einsum('bhnqd,bhnkd->bhnqk', qc * jnp.exp(b - b_mid), kc * jnp.exp(b_mid - b))
    causal = jnp.tril(jnp.ones((CHUNK_2, CHUNK_2), dtype=bool))
    A = jnp.where(causal, A, 0.0)
    o_intra = jnp.einsum('bhnqk,bhnkv->bhnqv', A, vc)
    kv = jnp.einsum('bhnkd,bhnkv->bhndv', kc * jnp.exp(b_last - b), vc)
    decay = jnp.exp(b_last[:, :, :, 0, :])

    def step(S, inp):
        d, u = inp
        return d[..., None] * S + u, S

    S0 = jnp.zeros((B, H, Dk, Dv), f32)
    _, S_prev = lax.scan(step, S0, (jnp.moveaxis(decay, 2, 0), jnp.moveaxis(kv, 2, 0)))
    S_prev = jnp.moveaxis(S_prev, 0, 2)
    o_inter = jnp.einsum('bhnqd,bhndv->bhnqv', qc * jnp.exp(b), S_prev)
    o = (o_intra + o_inter).transpose(0, 2, 3, 1, 4).reshape(B, T, H, Dv)
    o = rms_norm(o, onorm_g) * jax.nn.silu(g.astype(f32))
    return o.reshape(B, T, H * Dv).astype(q.dtype)

def cross_attention_2(u, m, wq, wk, wv, wo):
    B, T, _ = u.shape
    M = m.shape[1]
    q = (u @ wq).reshape(B, T, XATTN_HEADS, XATTN_HEAD_DIM)
    k = (m @ wk).reshape(B, M, XATTN_HEADS, XATTN_HEAD_DIM)
    v = (m @ wv).reshape(B, M, XATTN_HEADS, XATTN_HEAD_DIM)
    s = jnp.einsum('bthd,bmhd->bhtm', q, k).astype(jnp.float32) * (XATTN_HEAD_DIM ** -0.5)
    p = jax.nn.softmax(s, axis=-1).astype(v.dtype)
    o = jnp.einsum('bhtm,bmhd->bthd', p, v).reshape(B, T, D_MODEL)
    return o @ wo

def second_inputs(seed: int = 0) -> dict:
    key = jax.random.key(seed)
    ks = jax.random.split(key, 24)
    f32 = jnp.float32

    def nrm(k, shape, scale):
        return jax.random.normal(k, shape, f32) * scale

    def gain(k, shape):
        return 1.0 + 0.05 * jax.random.normal(k, shape, f32)

    return {
        "x": nrm(ks[0], (BATCH, SEQ, D_MODEL), 1.0),
        "mem": nrm(ks[1], (BATCH, MEM_LEN, D_MODEL), 1.0),
        "w_in": nrm(ks[2], (DEPTH, D_MODEL, D_IN_2), D_MODEL ** -0.5),
        "sinks": nrm(ks[3], (DEPTH, SWA_HEADS), 0.5),
        "hgrn_lb": nrm(ks[4], (DEPTH + 1, HGRN_WIDTH), 0.1),
        "hgrn_onorm": gain(ks[5], (DEPTH, HGRN_HEAD_DIM)),
        "w_out": nrm(ks[6], (DEPTH, D_MIX_2, D_MODEL), D_MIX_2 ** -0.5),
        "g_mix_pre": gain(ks[7], (DEPTH, D_MODEL)),
        "g_mix_post": gain(ks[8], (DEPTH, D_MODEL)),
        "g_mem": gain(ks[9], (DEPTH, D_MODEL)),
        "g_x_pre": gain(ks[10], (DEPTH, D_MODEL)),
        "g_x_post": gain(ks[11], (DEPTH, D_MODEL)),
        "wq_x": nrm(ks[12], (DEPTH, D_MODEL, D_MODEL), D_MODEL ** -0.5),
        "wk_x": nrm(ks[13], (DEPTH, D_MODEL, D_MODEL), D_MODEL ** -0.5),
        "wv_x": nrm(ks[14], (DEPTH, D_MODEL, D_MODEL), D_MODEL ** -0.5),
        "wo_x": nrm(ks[15], (DEPTH, D_MODEL, D_MODEL), D_MODEL ** -0.5),
        "g_ffn_pre": gain(ks[16], (DEPTH, D_MODEL)),
        "g_ffn_post": gain(ks[17], (DEPTH, D_MODEL)),
        "w_gate": nrm(ks[18], (DEPTH, D_MODEL, D_FF_2), D_MODEL ** -0.5),
        "w_up": nrm(ks[19], (DEPTH, D_MODEL, D_FF_2), D_MODEL ** -0.5),
        "w_down": nrm(ks[20], (DEPTH, D_FF_2, D_MODEL), D_FF_2 ** -0.5),
    }

def second_block(x, mem, w_in, sinks, hgrn_lb, hgrn_onorm, w_out, g_mix_pre, g_mix_post,
              g_mem, g_x_pre, g_x_post, wq_x, wk_x, wv_x, wo_x, g_ffn_pre, g_ffn_post,
              w_gate, w_up, w_down):
    B, T, _ = x.shape
    lb_all = jnp.cumsum(jax.nn.softmax(hgrn_lb.astype(jnp.float32), axis=0), axis=0)
    h = x
    for l in range(DEPTH):
        u = rms_norm(h, g_mix_pre[l])
        z = u @ w_in[l]
        qa, ka, va, qh, fh, ih, gh = jnp.split(z, IN_SPLITS, axis=-1)
        ya = swa_with_sinks(qa.reshape(B, T, SWA_HEADS, SWA_HEAD_DIM),
                            ka.reshape(B, T, SWA_KV_HEADS, SWA_HEAD_DIM),
                            va.reshape(B, T, SWA_KV_HEADS, SWA_HEAD_DIM),
                            sinks[l])
        hv = HGRN_WIDTH // HGRN_HEADS
        yh = hgrn2(qh.reshape(B, T, HGRN_HEADS, HGRN_HEAD_DIM),
                   fh.reshape(B, T, HGRN_HEADS, HGRN_HEAD_DIM),
                   ih.reshape(B, T, HGRN_HEADS, hv),
                   gh.reshape(B, T, HGRN_HEADS, hv),
                   lb_all[l].reshape(HGRN_HEADS, HGRN_HEAD_DIM),
                   hgrn_onorm[l])
        y = jnp.concatenate([ya, yh.astype(ya.dtype)], axis=-1) @ w_out[l]
        h = h + rms_norm(y, g_mix_post[l])
        u = rms_norm(h, g_x_pre[l])
        m = rms_norm(mem, g_mem[l])
        y = cross_attention_2(u, m, wq_x[l], wk_x[l], wv_x[l], wo_x[l])
        h = h + rms_norm(y, g_x_post[l])
        u = rms_norm(h, g_ffn_pre[l])
        y = (jax.nn.silu(u @ w_gate[l]) * (u @ w_up[l])) @ w_down[l]
        h = h + rms_norm(y, g_ffn_post[l])
    return h


def setup_inputs(seed=0):
    out = dict(first_inputs(seed))
    for name, value in second_inputs(seed + 1).items():
        if name != "x":
            out[name + "_2"] = value
    return out


def reference(
    x, mem, norm_mix_g, w_in, b_igate, b_fgate, ln_a_g, ln_a_b, w_s, b_s, conv_b_w, conv_b_b,
    gn_b_g, gn_b_b, conv_c_w, conv_c_b, w_q_c, w_k_c, w_v_c, hn_c_g, skip_c, w_out, norm_x_g,
    norm_mem_g, w_xq, w_xkv, w_xo, norm_ffn_g, w_up, conv_f_w, conv_f_b, w_down, final_g, mem_2,
    w_in_2, sinks_2, hgrn_lb_2, hgrn_onorm_2, w_out_2, g_mix_pre_2, g_mix_post_2, g_mem_2,
    g_x_pre_2, g_x_post_2, wq_x_2, wk_x_2, wv_x_2, wo_x_2, g_ffn_pre_2, g_ffn_post_2, w_gate_2,
    w_up_2, w_down_2,
):
    x = first_block(
        x, mem, norm_mix_g, w_in, b_igate, b_fgate, ln_a_g, ln_a_b, w_s, b_s, conv_b_w,
        conv_b_b, gn_b_g, gn_b_b, conv_c_w, conv_c_b, w_q_c, w_k_c, w_v_c, hn_c_g, skip_c,
        w_out, norm_x_g, norm_mem_g, w_xq, w_xkv, w_xo, norm_ffn_g, w_up, conv_f_w, conv_f_b,
        w_down, final_g,
    )
    return second_block(
        x, mem_2, w_in_2, sinks_2, hgrn_lb_2, hgrn_onorm_2, w_out_2, g_mix_pre_2, g_mix_post_2,
        g_mem_2, g_x_pre_2, g_x_post_2, wq_x_2, wk_x_2, wv_x_2, wo_x_2, g_ffn_pre_2,
        g_ffn_post_2, w_gate_2, w_up_2, w_down_2,
    )


_drawn_inputs = setup_inputs


def setup_inputs(seed=0):
    import zlib

    import numpy as np

    out = dict(_drawn_inputs(seed))
    spreads = {}
    factors = {'b_igate': 42.587,
     'ln_a_g': 8.0,
     'ln_a_b': 8.0,
     'conv_b_b': 2.668,
     'gn_b_g': 5.74,
     'gn_b_b': 4.96,
     'conv_c_b': 2.8,
     'hn_c_g': 5.831,
     'skip_c': 8.0,
     'norm_x_g': 8.0,
     'norm_mem_g': 8.0,
     'norm_ffn_g': 3.353,
     'conv_f_b': 4.245,
     'sinks_2': 64.0,
     'hgrn_lb_2': 6.256}
    for name, (base, spread) in spreads.items():
        noise = np.random.default_rng([zlib.crc32(name.encode()), seed]).standard_normal(out[name].shape)
        drawn = base * np.exp(spread * noise) if base else spread * noise
        out[name] = __import__('jax').numpy.asarray(drawn.astype(out[name].dtype))
    for name, factor in factors.items():
        out[name] = (out[name] * factor).astype(out[name].dtype)
    return out
```

```python
from contextlib import ExitStack

import numpy as np

import concourse.bass as bass
from concourse import mybir

F32 = mybir.dt.float32
F32R = mybir.dt.float32r
U32 = mybir.dt.uint32
ACT = mybir.ActivationFunctionType
ALU = mybir.AluOpType
AX = mybir.AxisListType.X

P = 128
T = 1024
D = 1024
KT = D // P
HALF = 512
CH = 128
NCH = T // CH
MEM = 256
FT = 22
FC = FT // 2
NH = 4
BIG = 3.0e38
NEG = -1.0e30
RMS_EPS = 1e-6
LN_EPS = 1e-5

STAGES = [("z1", 17, 17), ("out1", 8, 8), ("k1", 8, 8), ("v1", 8, 8), ("q1", 8, 8), ("xo1", 8, 8),
          ("ffn1", 6 * FC, 12 * FC),
          ("z2", 22, 22), ("out2", 8, 8), ("k2", 8, 8), ("v2", 8, 8), ("q2", 8, 8), ("xo2", 8, 8),
          ("ffn2", 6 * FC, 12 * FC)]
BLOCK0, PROD0 = {}, {}
_b = _p = 0
for _name, _nb, _np_ in STAGES:
    BLOCK0[_name], PROD0[_name] = _b, _p
    _b, _p = _b + _nb, _p + _np_
NBLOCKS = _b

COLS = [("mix1", 8), ("lna_g", 2), ("lna_b", 2), ("cb_w", 62), ("cb_b", 2), ("gnb_g", 2), ("gnb_b", 2),
        ("cc_w", 16), ("cc_b", 4), ("hn_g", 4), ("skip", 4), ("x1", 8), ("mem1", 8), ("ffn1", 8),
        ("cf", 4 * FT), ("final", 8), ("mix2", 8), ("post_mix", 8), ("mem2", 8), ("x2", 8),
        ("post_x", 8), ("ffn2", 8), ("post_ffn", 8), ("lb", 8), ("onorm", 1), ("sinks", 8), ("gate_b", 1)]
COL = {}
_c = 0
for _name, _n in COLS:
    COL[_name] = _c
    _c += _n
NCOLS = _c

CONSTS = [("ident", 128), ("ones", 128), ("blk", 128), ("ml_mask", 128), ("swa_rest", 256),
          ("swa_first", 256), ("hg_mask", 128), ("hg_reset", 512), ("sel", 512)]
CST = {}
_c = 0
for _name, _n in CONSTS:
    CST[_name] = _c
    _c += _n
NCONST = _c
NKEPT = CST["hg_reset"]


NORMS = ["z1", "q1", "ffn1", "final", "z2", "pm", "q2", "px", "ffn2", "pf"]
OPERANDS = ["z1", "q1", "ffn1", "z2", "q2", "ffn2"]
XA0 = {"1": 0, "2": NCH}
STD0 = {"cf": (0, 0), "ln": (2, 2), "hn": (3, 4)}
FF0 = {"ffn1": 0, "ffn2": FT}


class Chain:

    def __init__(self, eng, sem):
        self.eng, self.sem, self.n, self.turn = eng, sem, 0, 0

    def link(self, ins):
        ins.then_inc(self.sem, 1)
        self.n += 1
        self.eng.wait_ge(self.sem, self.turn + self.n)

    def enter(self, i, first, per):
        self.turn, self.start, self.per = (i - first) * per, self.n, per

    def leave(self, trips):
        assert self.n - self.start == self.per, self.n - self.start
        self.n, self.turn = self.start + trips * self.per, 0


def program(nc, ap):
    ctx = ExitStack()
    with ctx:
        semaphores = {}

        def s(name):
            if name not in semaphores:
                semaphores[name] = ctx.enter_context(nc.semaphore(name))
            return semaphores[name]

        def norm(what, name, n, per=KT):
            return s(what), per * NORMS.index(name) + n

        def operand_count(what, name, n):
            if name in ("m1", "m2"):
                return s("mem_lo"), KT * (name == "m2") + n
            return s(what), KT * OPERANDS.index(name) + n

        arena_cols = 53200
        ctx.enter_context(nc.sbuf_tensor("arena", [P, arena_cols], F32))
        first_byte = nc.sbuf_base - 4 * arena_cols
        place_of = {}
        used = [0]

        def place(name, shape, dt=F32, over=None, offset=0):
            size = -(-int(np.prod(shape[1:])) // 8) * 8
            if over is None:
                start = used[0]
                used[0] += size
            else:
                start = place_of[over] + offset
            place_of[name] = start
            assert used[0] <= arena_cols, used
            return nc.alloc_sbuf_tensor_at(name, shape, dt, offset=first_byte + 4 * start)

        act_hi = place("act_hi", [P, KT, T], F32R)
        act_lo = place("act_lo", [P, KT, T], F32R)
        w_raw = place("w_raw", [P, 2, KT * P])
        w_hi = place("w_hi", [P, 2, KT * P], F32R)
        w_lo = place("w_lo", [P, 2, KT * P], F32R)
        W = place("work", [P, FT, T])
        TMP = place("tmp", [P, 4, T])
        rstd = place("rstd", [P, T])
        cst = place("cst", [P, NKEPT])
        phase = place("phase", [P, 512])
        cols = place("cols", [P, NCOLS])
        small = place("small", [P, 64])
        epsc = place("epsc", [P, 2])
        g_hi = place("g_hi", [P, 2, T], F32R, over="work", offset=18 * T)
        g_lo = place("g_lo", [P, 2, T], F32R, over="work", offset=20 * T)
        m_hi = place("m_hi", [P, KT, MEM], F32R, over="work", offset=8 * T)
        m_lo = place("m_lo", [P, KT, MEM], F32R, over="work", offset=10 * T)
        hi_as_f32 = act_hi[:, :, :].bitcast(F32)
        lo_free = place("lo_free", [P, 4, T], over="act_lo", offset=4 * T)
        hi_free = place("hi_free", [P, 4, T], over="act_hi", offset=4 * T)

        G = ctx.enter_context(nc.psum_tensor("products", [P, 2, T], F32))
        N = ctx.enter_context(nc.psum_tensor("others", [P, 2, T], F32))

        def const(name, n=None):
            c = CST[name]
            return cst[:, c:c + (n or 128)]

        def col(name, k):
            return cols[:, COL[name] + k:COL[name] + k + 1]

        Wc = W[:, :, :].rearrange("p k (c t) -> p k c t", t=CH)
        hic = act_hi[:, :, :].rearrange("p k (c t) -> p k c t", t=CH)
        loc = act_lo[:, :, :].rearrange("p k (c t) -> p k c t", t=CH)
        hicf = hi_as_f32.rearrange("p k (c t) -> p k c t", t=CH)
        Tc = TMP[:, :, :].rearrange("p k (c t) -> p k c t", t=CH)
        flat = W[:, :, :].rearrange("p k t -> p (k t)")
        tflat = TMP[:, :, :].rearrange("p k t -> p (k t)")
        sq = [TMP[:, 0, :], TMP[:, 1, :]]
        ssum, root = TMP[:, 2, :], TMP[:, 3, :]
        ident, ones, blk = const("ident"), const("ones"), const("blk")

        rowA, rowF, rowE, rowM = (TMP[:, n, :] for n in range(4))
        wq, wk, wv, wsT = (flat[:, 20 * T + 512 * n:20 * T + 512 * n + 512] for n in range(4))
        ml = lambda n, k=1: (flat[:, 512 * n:512 * (n + k)] if n < 8 else
                             flat[:, 8 * T + 512 * (n - 8):8 * T + 512 * (n - 8 + k)])
        heads = lambda v: v.rearrange("p (h t) -> p h t", h=NH)
        xcs, xvs, qT, qw, kT, kw, Wt, Pm = (heads(ml(n)) for n in range(8))
        winter, emm, Et, dn = (heads(ml(8 + n)) for n in range(4))
        vt = ml(12, 2).rearrange("p (h t) -> p h t", h=NH)
        Cst = ml(14, 2).rearrange("p (h t) -> p h t", h=NH)
        sel = phase[:, :].rearrange("p (h t) -> p h t", h=NH)
        bsb = place("bsb", [P, 2 * P])
        arow = place("arow", [P, P])
        bsv = bsb[:, :].rearrange("p (k t) -> p k t", k=2)
        Gf = G[:, :, :].rearrange("p a t -> p (a t)")
        Nf = N[:, :, :].rearrange("p a t -> p (a t)")
        Gb = [heads(Gf[:, 512 * n:512 * n + 512]) for n in range(4)]
        Nb = [heads(Nf[:, 512 * n:512 * n + 512]) for n in range(4)]

        hg_names = "lf b D1 E1 E1n Eb D2 E2 Q1 Q2 K1 K2 vs vtok k2tok AT S".split()

        def hg(names):
            out = []
            for name in names.split():
                n = hg_names.index(name)
                v = flat[:, 16 * T + 512 * n:16 * T + 512 * n + 512] if n < 12 else tflat[:, 512 * (n - 12):512 * (n - 11)]
                out.append(heads(v))
            return out

        block = ctx.enter_context(nc.Block())

        @block.sync
        def _(sp):
            def load(b, slot):
                sp.dma_start(w_raw[:, slot, :], ap["wstream"][b]).then_inc(s(f"weights_loaded{slot}"), 16)

            load(0, 0)
            load(1, 1)
            with sp.Fori(2, NBLOCKS - 1, 2) as b:
                for slot in range(2):
                    sp.wait_ge(s("weights_split"), b + slot - 1)
                    load(b + slot, slot)
            if NBLOCKS % 2:
                sp.wait_ge(s("weights_split"), NBLOCKS - 2)
                load(NBLOCKS - 1, 0)

        @block.gpsimd
        def _(pool):
            pool.memset(small[:, 63:64], 0.0).then_inc(s("pool_zero"), 1)
            pool.wait_ge(s("pool_zero"), 1)
            zeros = small[:, 63:64].to_broadcast([P, KT * P])

            def split(b, turn, slot, first=False):
                pool.wait_ge(s(f"weights_loaded{slot}"), 16 * (turn + 1))
                if not first:
                    pool.wait_ge(s("product_quarters"), 4 * (b - 1))
                pool.tensor_tensor(w_hi[:, slot, :], w_raw[:, slot, :], zeros, ALU.add).then_inc(s("weights_high"), 1)
                pool.wait_ge(s("weights_high"), b + 1)
                pool.tensor_tensor(w_lo[:, slot, :], w_raw[:, slot, :], w_hi[:, slot, :].bitcast(F32),
                                   ALU.subtract).then_inc(s("weights_split"), 1)

            split(0, 0, 0, True)
            split(1, 0, 1, True)
            with pool.Fori(1, NBLOCKS // 2) as turn:
                for slot in range(2):
                    split(turn * 2 + slot, turn, slot)
            if NBLOCKS % 2:
                split(NBLOCKS - 1, NBLOCKS // 2, 0)

        @block.tensor
        def _(pe):
            def room(p):
                if not isinstance(p, int) or p >= 2:
                    pe.wait_ge(s("evacuated"), p - 1)

            def project(b, p, ws, ps, hi, lo, width=T, ready=None):
                pe.wait_ge(s("weights_split"), b + 1)
                room(p)
                n = min(width, HALF)
                for k in range(KT):
                    if ready:
                        pe.wait_ge(*operand_count("operand_lo", ready, k + 1))
                    w = slice(k * P, (k + 1) * P)
                    for h in range(width // n):
                        c = slice(h * n, (h + 1) * n)
                        for i, (a, x) in enumerate(((w_hi, hi), (w_hi, lo), (w_lo, hi))):
                            last = pe.matmul(G[:, ps, c], a[:, ws, w], x[:, k, c],
                                             start=(k == 0 and i == 0), stop=(k == KT - 1 and i == 2))
                last.then_inc(s("product_quarters"), 4)

            def gemm(name, n, ready, hi=act_hi, lo=act_lo, width=T, after_two=None):
                b, p = BLOCK0[name], PROD0[name]
                peel = 2 + n % 2
                for j in range(peel):
                    project(b + j, p + j, (b + j) % 2, (p + j) % 2, hi, lo, width, ready if j == 0 else None)
                    if j == 1 and after_two:
                        after_two()
                with pe.Fori(peel, n, 2) as i:
                    for j in range(2):
                        project(i + (b + j), i + (p + j), (b + peel + j) % 2, (p + peel + j) % 2, hi, lo, width)

            def value_gemm(name):
                b, p = BLOCK0[name], PROD0[name]
                with pe.Fori(0, 8, 2) as i:
                    for j in range(2):
                        ws, ps = (b + j) % 2, (p + j) % 2
                        pe.wait_ge(s("weights_split"), i + (b + j + 1))
                        room(i + (p + j))
                        for m in range(2):
                            for k in range(KT):
                                for n, (a, x) in enumerate(((m_hi, w_hi), (m_lo, w_hi), (m_hi, w_lo))):
                                    last = pe.matmul(G[:, ps, m * HALF:m * HALF + P], a[:, k, m * P:(m + 1) * P],
                                                     x[:, ws, k * P:(k + 1) * P],
                                                     start=(k == 0 and n == 0), stop=(k == KT - 1 and n == 2))
                        last.then_inc(s("product_quarters"), 4)

            def token_sums(name, wait, count, src=None):
                if name in NORMS:
                    pe.wait_ge(*norm("squares_summed", name, KT))
                else:
                    pe.wait_ge(s(wait), count)
                for h in range(2):
                    c = slice(h * HALF, (h + 1) * HALF)
                    last = pe.matmul(N[:, 0, c], ones, (src if src is not None else ssum)[:, c], start=True, stop=True)
                last.then_inc(s("token_sums" if name in NORMS else name + "_token_sums"), 1)

            def norm_sums(name):
                return lambda: token_sums(name, None, None)

            def standardize(name, jobs, ready):
                done = 0
                for n, (m, tiles) in enumerate(jobs):
                    pe.wait_ge(s(ready[0]), ready[1][n])
                    for h in range(2):
                        c = slice(h * HALF, (h + 1) * HALF)
                        for t, tile in enumerate(tiles):
                            last = pe.matmul(N[:, 0, c], m, tile[:, c], start=(t == 0), stop=(t == len(tiles) - 1))
                    last.then_inc(s("std_mean"), 1)
                    done += len(tiles)
                    pe.wait_ge(s("std_sq"), STD0[name][1] + done)
                    for h in range(2):
                        c = slice(h * HALF, (h + 1) * HALF)
                        for t in range(len(tiles)):
                            last = pe.matmul(N[:, 1, c], m, W[:, t, c], start=(t == 0), stop=(t == len(tiles) - 1))
                    last.then_inc(s("std_var"), 1)

            def gmlp():
                pe.wait_ge(s("ln_out"), 2)
                pe.wait_ge(s("evacuated"), PROD0["out1"])
                for c in range(NCH):
                    for t in range(2):
                        last = pe.transpose(Gf[:, (2 * c + t) * P:(2 * c + t + 1) * P], W[:, 10 + t, c * CH:(c + 1) * CH], ident)
                last.then_inc(s("gm_turned"), 1)
                pe.wait_ge(s("gm_tokens"), 2)
                pe.wait_ge(s("ws_masked"), 1)
                for c in range(NCH):
                    for h in range(NH):
                        r = slice(64 * (h % 2), 64 * (h % 2) + 64)
                        last = pe.matmul(Nf[r, (h // 2) * T + c * CH:(h // 2) * T + (c + 1) * CH],
                                         flat[:, 2 * T + 256 * c + 64 * h:2 * T + 256 * c + 64 * h + 64],
                                         wsT[:, h * P:(h + 1) * P], start=True, stop=True)
                last.then_inc(s("gm_mixed"), 1)

            def mlstm():
                pe.wait_ge(s("ml_rows"), 1)
                pe.wait_ge(s("mix_in"), 80)
                pe.wait_ge(s("phase_in"), 16)
                pe.wait_ge(s("ml_init"), 2)
                with pe.Fori(0, NCH) as c:
                    pe.wait_ge(s("ml_kept"), c + 1)
                    pe.wait_ge(s("ml_stage"), 3 * c + 3)
                    for n, (a, x) in enumerate(((wq, xvs), (wk, xvs))):
                        for h in range(NH):
                            last = pe.matmul(Gb[n][:, h, :], heads(a)[:, h, :], x[:, h, :], start=True, stop=True)
                    for n, (a, x) in enumerate(((xvs, wk), (xcs, wv))):
                        for h in range(NH):
                            last = pe.matmul(Gb[2 + n][:, h, :], a[:, h, :], heads(x)[:, h, :], start=True, stop=True)
                    last.then_inc(s("ml_proj"), 1)
                    for n, row in ((2, rowF), (3, rowE)):
                        rc = row[0:NH, :].rearrange("p (c t) -> p c t", t=CH)
                        for h in range(NH):
                            pe.matmul(Nb[n][:, h, :], sel[0:NH, h, :], rc[:, c, :], start=True, stop=True)
                    rc = rowM[0:NH, :].rearrange("p (c t) -> p c t", t=CH)
                    for h in range(NH):
                        pe.matmul(Nb[0][:, h, :], arow[0:NH, :], sel[0:NH, h, :], start=True, stop=False)
                        last = pe.matmul(Nb[0][:, h, :], sel[0:NH, h, :], rc[:, c, :], start=False, stop=True)
                    last.then_inc(s("ml_spread"), 1)
                    pe.wait_ge(s("ml_qkv"), 3 * c + 3)
                    for h in range(NH):
                        last = pe.matmul(Nb[1][:, h, :], kT[:, h, :], qT[:, h, :], start=True, stop=True)
                    last.then_inc(s("ml_scores"), 1)
                    pe.wait_ge(s("ml_weighted"), 3 * c + 3)
                    for h in range(NH):
                        pe.matmul(Gb[0][:, h, :], vt[:, h, 0:P], Pm[:, h, :], start=True, stop=False)
                        pe.matmul(Gb[0][:, h, :], Cst[:, h, 0:P], qw[:, h, :], start=False, stop=True)
                    for h in range(NH):
                        pe.matmul(Gb[1][:, h, :], ones, Pm[:, h, :], start=True, stop=False)
                        last = pe.matmul(Gb[1][:, h, :], Cst[:, h, P:2 * P], qw[:, h, :], start=False, stop=True)
                    last.then_inc(s("ml_num"), 1)
                    for h in range(NH):
                        last = pe.matmul(Gf[:, T + 256 * h:T + 256 * h + 256], kw[:, h, :], vt[:, h, :], start=True, stop=True)
                    last.then_inc(s("ml_update"), 1)

            def memory_sums(x):
                def run():
                    pe.wait_ge(s(x + "_mem_sq"), 1)
                    for k in range(KT):
                        last = pe.matmul(N[:, 1, 0:MEM], ones, flat[:, 12 * T + k * MEM:12 * T + (k + 1) * MEM],
                                         start=(k == 0), stop=(k == KT - 1))
                    last.then_inc(s(x + "_mem_sums"), 1)
                return run

            def cross(x):
                kTm = flat[:, 16 * T:18 * T].rearrange("p (k m) -> p k m", m=MEM)
                vm = W[:, 18:20, :]
                qs = TMP[:, 0, :].rearrange("p (k t) -> p k t", k=KT)
                p_, pT = TMP[:, 1, :], TMP[:, 2, :].rearrange("p (k t) -> p k t", k=KT)

                def scores(c):
                    pe.wait_ge(s("xa_q_staged"), c + 1 + XA0[x])
                    for h in range(NH):
                        for k in range(2):
                            last = pe.matmul(Nf[:, MEM * h:MEM * (h + 1)], qs[:, 2 * h + k, :], kTm[:, 2 * h + k, :],
                                             start=(k == 0), stop=(k == 1))
                    last.then_inc(s("xa_scores"), 1)

                def values(c):
                    pe.wait_ge(s("xa_probs"), c + 1 + XA0[x])
                    for n in range(8):
                        last = pe.transpose(N[:, 1, n * P:(n + 1) * P], p_[:, n * P:(n + 1) * P], ident)
                    last.then_inc(s("xa_turned"), 1)
                    pe.wait_ge(s("xa_pT"), c + 1 + XA0[x])
                    pe.wait_ge(s("xa_o_lo"), c + 1 + XA0[x])
                    for k in range(KT):
                        for m in range(2):
                            last = pe.matmul(G[:, 0, k * P:(k + 1) * P], vm[:, m, k * P:(k + 1) * P],
                                             pT[:, 2 * (k // 2) + m, :], start=(m == 0), stop=(m == 1))
                    last.then_inc(s("xa_out"), 1)

                pe.wait_ge(s("evacuated"), PROD0["xo" + x])
                scores(0)
                with pe.Fori(0, NCH - 1) as c:
                    pe.wait_ge(s("xa_exps"), c + 1 + XA0[x])
                    scores(c + 1)
                    values(c)
                values(NCH - 1)

            def ffn(name):
                b, p = BLOCK0[name], PROD0[name]

                def up(b, p, par, after_two=None, ready=None):
                    for j in range(4):
                        project(b + j, p + j, (par[0] + j) % 2, (par[1] + j) % 2, act_hi, act_lo, T, ready if j == 0 else None)
                        if j == 1 and after_two:
                            after_two()

                def down(b, p, par, c):
                    for j in range(2):
                        pe.wait_ge(s("weights_split"), b + (j + 1))
                        for o in range(4):
                            room(p + (4 * j + o))
                            if j == 0 and o == 0:
                                pe.wait_ge(s("ff_g_lo"), 2 * c + 2 + FF0[name])
                            ws, ps = (par[0] + j) % 2, (par[1] + o) % 2
                            for k in range(2):
                                w = slice((2 * o + k) * P, (2 * o + k + 1) * P)
                                for h in range(2):
                                    t = slice(h * HALF, (h + 1) * HALF)
                                    for i, (a, x) in enumerate(((w_hi, g_hi), (w_hi, g_lo), (w_lo, g_hi))):
                                        last = pe.matmul(G[:, ps, t], a[:, ws, w], x[:, k, t],
                                                         start=(k == 0 and i == 0), stop=(k == 1 and i == 2))
                            last.then_inc(s("product_quarters"), 1)

                up(b, p, (b, p), norm_sums(name), name)
                with pe.Fori(1, FC) as c:
                    up(c * 6 + (b - 2), c * 12 + (p - 8), (b, p))
                    down(c * 6 + (b + 2), c * 12 + (p - 4), (b, p), c - 1)
                down(b + 6 * FC - 2, p + 12 * FC - 8, (b, p), FC - 1)

            def windowed():
                qst = hi_free[:, 0, 0:512].rearrange("p (k t) -> p k t", k=4)
                kst = hi_free[:, 0, 512:768]
                vst = hi_free[:, 0, 768:1024]
                vtk = hi_free[:, 3, 0:256]
                pr = hi_free[:, 1:3, :].rearrange("p a t -> p (a t)")
                pTs = lo_free[:, 0:2, :].rearrange("p a t -> p (a t)")
                pe.wait_ge(s("evacuated"), PROD0["out2"])
                with pe.Fori(0, NCH) as c:
                    pe.wait_ge(s("sw_staged"), 4 * c + 4)
                    pe.wait_ge(s("sw_o_lo"), c + 1)
                    for g in range(2):
                        for i in range(4):
                            n = 4 * g + i
                            last = pe.matmul(Nf[:, n * 256:(n + 1) * 256], qst[64 * g:64 * g + 64, i, :],
                                             kst[64 * g:64 * g + 64, :], start=True, stop=True)
                    last.then_inc(s("sw_scores"), 1)
                    for n in range(2):
                        last = pe.transpose(G[:, 1, n * P:(n + 1) * P], vst[:, n * P:(n + 1) * P], ident)
                    last.then_inc(s("sw_v_turned"), 1)
                    pe.wait_ge(s("sw_v"), c + 1)
                    pe.wait_ge(s("sw_probs"), c + 1)
                    for n in range(16):
                        last = pe.transpose(Gf[:, n * P:(n + 1) * P], pr[:, n * P:(n + 1) * P], ident)
                    last.then_inc(s("sw_turned"), 1)
                    pe.wait_ge(s("sw_pT"), 2 * c + 2)
                    for g in range(2):
                        for i in range(4):
                            n = 4 * g + i
                            for m in range(2):
                                last = pe.matmul(Nf[64 * g:64 * g + 64, i * P:(i + 1) * P],
                                                 vtk[:, m * P + 64 * g:m * P + 64 * g + 64],
                                                 pTs[:, (2 * n + m) * P:(2 * n + m + 1) * P], start=(m == 0), stop=(m == 1))
                    last.then_inc(s("sw_pv"), 1)

            def hgrn():
                Q1, Q2, K1, K2, vs, AT, vtok, k2tok, S = hg("Q1 Q2 K1 K2 vs AT vtok k2tok S")
                pe.wait_ge(s("hg_init"), 1)
                with pe.Fori(0, NCH) as c:
                    pe.wait_ge(s("hg_qk"), 4 * c + 4)
                    pe.wait_ge(s("hg_v"), c + 1)
                    for h in range(NH):
                        last = pe.matmul(Nb[0][:, h, :], K1[:, h, :], Q1[:, h, :], start=True, stop=True)
                    last.then_inc(s("hg_scores"), 1)
                    for h in range(NH):
                        pe.transpose(Gb[0][:, h, :], vs[:, h, :], ident)
                    for h in range(NH):
                        last = pe.transpose(Gb[1][:, h, :], K2[:, h, :], ident)
                    last.then_inc(s("hg_turned"), 1)
                    pe.wait_ge(s("hg_masked"), c + 1)
                    pe.wait_ge(s("hg_tokens"), 2 * c + 2)
                    pe.wait_ge(s("hg_kept"), c + 1)
                    for h in range(NH):
                        pe.matmul(Nb[1][:, h, :], vtok[:, h, :], AT[:, h, :], start=(h == 0), stop=False, skip_group_check=True)
                    for sub in range(2):
                        r = slice(64 * sub, 64 * sub + 64)
                        for h in range(NH):
                            pe.matmul(Nb[1][:, h, r], S[:, h, :], Q2[:, h, r], start=False, stop=(sub == 1 and h == 3),
                                      skip_group_check=True)
                        for h in range(NH):
                            last = pe.matmul(Nb[2 + sub][:, h, :], k2tok[r, h, :], vtok[r, h, :], start=True, stop=True)
                        last.then_inc(s("hg_update"), 1)
                        if sub == 0:
                            pe.wait_ge(s("hg_S"), 2 * c + 2)
                    pe.wait_ge(s("hg_S"), 2 * c + 3)

            pe.wait_ge(s("consts"), 32)
            gemm("z1", 17, "z1", after_two=norm_sums("z1"))
            standardize("cf", [(blk, [W[:, 2, :]]), (blk, [W[:, 3, :]])], ("cb_done", [1, 2]))
            standardize("ln", [(ones, [W[:, 10, :], W[:, 11, :]])], ("gelus", [4]))
            gmlp()
            mlstm()
            standardize("hn", [(ones, [W[:, 4 + n, :]]) for n in range(4)], ("ml_h", [8] * 4))
            pe.wait_ge(s("y1_lo"), 8)
            gemm("out1", 8, None, after_two=memory_sums("1"))

            def attention(x):
                gemm("k" + x, 8, "m" + x, m_hi, m_lo, MEM)
                value_gemm("v" + x)
                gemm("q" + x, 8, "q" + x, after_two=norm_sums("q" + x))
                cross(x)
                pe.wait_ge(s("xa_o_lo"), NCH + 1 + XA0[x])
                gemm("xo" + x, 8, None)

            attention("1")
            ffn("ffn1")
            norm_sums("final")()
            gemm("z2", 22, "z2", after_two=norm_sums("z2"))
            windowed()
            hgrn()
            for n in range(4):
                token_sums("hr", "hr_sq", n + 1, W[:, 16, :])
            pe.wait_ge(s("y2_lo"), 4)
            pe.wait_ge(s("sw_o_lo"), NCH + 1)
            gemm("out2", 8, None)
            norm_sums("pm")()
            memory_sums("2")()
            attention("2")
            norm_sums("px")()
            ffn("ffn2")
            norm_sums("pf")()

        @block.scalar
        def _(act):
            chain = Chain(act, s("act_chain"))

            def apart():
                act.wait_ge(s("consts"), 32)

            def squares(name, src, ready, n=KT):
                for k in range(n):
                    act.wait_ge(*ready(k))
                    if k >= 2:
                        act.wait_ge(*norm("squares_summed", name, k - 1))
                    act.activation(sq[k % 2], src(k), ACT.Square).then_inc(s("squares"), 1)

            def roots(name, n=1, scale=1.0 / D, src=None, out=None):
                act.wait_ge(*(norm("token_sums", name, 1, 1) if name in NORMS else (s(name + "_token_sums"), n)))
                act.activation(root if out is None else out, N[:, 0, :] if src is None else src, ACT.Sqrt,
                               bias=epsc[:, 0:1], scale=scale)\
                   .then_inc(s("roots" if name in NORMS else name + "_root"), 1)

            def split_high(name, src, gain, ready=None):
                for k in range(KT):
                    if ready:
                        act.wait_ge(*ready(k))
                    act.activation(act_hi[:, k, :], src(k), ACT.Identity, scale=col(gain, k)).then_inc(s("operand_hi"), 1)

            def standardize(name, jobs, div, affine):
                done = 0
                for n, tiles in enumerate(jobs):
                    for t, tile in enumerate(tiles):
                        act.wait_ge(s("std_centred"), STD0[name][1] + done + t + 1)
                        act.activation(W[:, t, :], tile, ACT.Square).then_inc(s("std_sq"), 1)
                    act.wait_ge(s("std_var"), STD0[name][0] + n + 1)
                    act.activation(W[:, 0, :], N[:, 1, :], ACT.Sqrt, bias=epsc[:, 1:2], scale=1.0 / div)\
                       .then_inc(s("std_root"), 1)
                    for t, tile in enumerate(tiles):
                        act.wait_ge(s("std_scaled"), STD0[name][1] + done + t + 1)
                        affine(n, t, tile).then_inc(s(name + "_out"), 1)
                    done += len(tiles)

            def load(dst, src, name):
                act.dma_start(dst, src).then_inc(s(name), 16)

            load(cst[:, :], ap["consts"][:, 0:NKEPT], "consts")
            load(cols[:, :], ap["cols"], "consts")
            for k in range(KT):
                load(W[:, k, :], ap["xT"][:, k, :], f"x_in{k}")
            load(phase[:, :], ap["consts"][:, CST["sel"]:CST["sel"] + 512], "phase_in")
            load(wq, ap["w_q"], "mix_in")
            load(wk, ap["w_k"], "mix_in")
            load(wv, ap["w_v"], "mix_in")
            load(wsT, ap["w_sT"], "mix_in")
            load(bsb[:, :], ap["b_s"], "mix_in")
            act.wait_ge(s("consts"), 32)
            act.wait_ge(s("eps"), 2)
            for k in range(KT):
                act.wait_ge(s(f"x_in{k}"), 16)
                act.activation(act_hi[:, k, :], W[:, k, :], ACT.Identity, scale=col("mix1", k)).then_inc(s("operand_hi"), 1)
                if k >= 2:
                    act.wait_ge(*norm("squares_summed", "z1", k - 1))
                act.activation(sq[k % 2], W[:, k, :], ACT.Square).then_inc(s("squares"), 1)
            roots("z1")
            E0 = PROD0["z1"]
            act.wait_ge(s("row_forget"), 1)
            act.activation(rowE[0:NH, :], rowF[0:NH, :], ACT.Abs).then_inc(s("row_abs"), 1)
            act.wait_ge(s("row_abs"), 1)
            chain.link(act.activation(rowE[0:NH, :], rowE[0:NH, :], ACT.Exp, scale=-1.0))
            act.activation(rowE[0:NH, :], rowE[0:NH, :], ACT.Ln, bias=1.0).then_inc(s("row_log"), 1)
            for n in range(2):
                act.wait_ge(s("evacuated"), E0 + 4 + n)
                act.activation(W[:, 2 + n, :], W[:, 2 + n, :], ACT.Sigmoid).then_inc(s("cf_gate"), 1)
            for n in range(4):
                act.wait_ge(s("cc_done"), n + 1)
                act.activation(W[:, 16 + n, :], W[:, 16 + n, :], ACT.Silu).then_inc(s("xconv"), 1)
            for n in range(4):
                act.wait_ge(s("evacuated"), E0 + 10 + n)
                act.activation(W[:, 8 + n, :], W[:, 8 + n, :], ACT.Gelu).then_inc(s("gelus"), 1)
            for n in range(4):
                act.wait_ge(s("evacuated"), E0 + 14 + n)
                act.activation(W[:, 12 + n, :], W[:, 12 + n, :], ACT.Sigmoid).then_inc(s("ogate"), 1)

            def cf_affine(n, t, tile):
                return act.activation(tile, tile, ACT.Silu, scale=col("gnb_g", n), bias=col("gnb_b", n))

            standardize("cf", [[W[:, 2, :]], [W[:, 3, :]]], 64, cf_affine)
            act.wait_ge(s("evacuated"), PROD0["out1"])
            act.wait_ge(s("cf_out"), 2)
            for n in range(2):
                act.activation(act_hi[:, 2 + n, :], W[:, 2 + n, :], ACT.Copy).then_inc(s("y1_hi"), 1)

            def ln_affine(n, t, tile):
                return act.activation(tile, tile, ACT.Identity, scale=col("lna_g", t), bias=col("lna_b", t))

            standardize("ln", [[W[:, 10, :], W[:, 11, :]]], 256, ln_affine)
            act.wait_ge(s("y1_lo"), 2)
            act.wait_ge(s("gm_turned"), 1)
            for n in range(2):
                act.activation(W[:, 2 + n, :], G[:, n, :], ACT.Copy).then_inc(s("gm_tokens"), 1)
            for n in range(2):
                act.wait_ge(s("gm_y"), n + 1)
                act.activation(act_hi[:, n, :], W[:, n, :], ACT.Copy).then_inc(s("y1_hi"), 1)

            act.wait_ge(s("ml_free"), 1)
            act.wait_ge(s("xconv"), 4)
            rowAc = rowA[0:NH, :].rearrange("p (c t) -> p c t", t=CH)
            with act.Fori(0, NCH) as c:
                act.wait_ge(s("ml_kept"), c + 1)
                apart()
                act.activation(xvs, Wc[:, 16:20, c, :], ACT.Copy).then_inc(s("ml_stage"), 1)
                act.activation(xcs, Wc[:, 4:8, c, :], ACT.Copy).then_inc(s("ml_stage"), 1)
                act.activation(arow[0:NH, :], rowAc[:, c, :], ACT.Copy).then_inc(s("ml_stage"), 1)
                act.wait_ge(s("ml_proj"), c + 1)
                act.activation(qT, Gb[0], ACT.Copy, scale=float(P) ** -0.5).then_inc(s("ml_qkv"), 1)
                act.activation(kT, Gb[1], ACT.Copy).then_inc(s("ml_qkv"), 1)
                act.activation(vt[:, :, 0:P], Gb[3], ACT.Copy).then_inc(s("ml_qkv"), 1)
                act.wait_ge(s("ml_spread"), c + 1)
                act.activation(winter, Nb[2], ACT.Exp).then_inc(s("ml_exp"), 1)
                act.wait_ge(s("ml_bounded"), c + 1)
                act.activation(Wt, Et, ACT.Exp).then_inc(s("ml_exp"), 1)
                act.activation(emm, Nb[3], ACT.Exp).then_inc(s("ml_exp"), 1)
                act.wait_ge(s("ml_num"), c + 1)
                act.activation(dn, Gb[1], ACT.Abs).then_inc(s("ml_den"), 1)

            def hn_affine(n, t, tile):
                return act.activation(tile, tile, ACT.Identity, scale=col("hn_g", n))

            standardize("hn", [[W[:, 4 + n, :]] for n in range(4)], P, hn_affine)
            for n in range(4):
                act.wait_ge(s("ml_y"), n + 1)
                act.activation(act_hi[:, 4 + n, :], W[:, 4 + n, :], ACT.Copy).then_inc(s("y1_hi"), 1)
            act.wait_ge(s("y1_lo"), 8)

            def memory(x):
                mem = flat[:, 20 * T:22 * T]
                act.wait_ge(s(x + "_mem_in"), 16)
                if x == "2":
                    act.wait_ge(s("pm_h"), KT)
                act.activation(flat[:, 12 * T:14 * T], mem, ACT.Square).then_inc(s(x + "_mem_sq"), 1)
                act.wait_ge(s(x + "_mem_sums"), 1)
                act.activation(W[:, 14, 0:MEM], N[:, 1, 0:MEM], ACT.Sqrt, bias=epsc[:, 0:1], scale=1.0 / D)\
                   .then_inc(s(x + "_mem_root"), 1)
                act.wait_ge(s(x + "_mem_scaled"), 1)
                for k in range(KT):
                    act.activation(m_hi[:, k, :], mem[:, k * MEM:(k + 1) * MEM], ACT.Identity, scale=col("mem" + x, k))\
                       .then_inc(s(x + "_mem_hi"), 1)

            def cross(x):
                qs = TMP[:, 0, :].rearrange("p (k t) -> p k t", k=KT)
                pr, pT = TMP[:, 1, :], TMP[:, 2, :]

                def stage(c):
                    act.activation(qs, Wc[:, 8:16, c, :], ACT.Copy).then_inc(s("xa_q_staged"), 1)

                def exps(c):
                    act.wait_ge(s("xa_negmax"), c + 1 + XA0[x])
                    for h in range(NH):
                        last = act.activation(pr[:, h * MEM:(h + 1) * MEM], Nf[:, h * MEM:(h + 1) * MEM], ACT.Exp,
                                              bias=small[:, 4 + h:5 + h], accum_out=small[:, 8 + h:9 + h])
                    last.then_inc(s("xa_exps"), 1)

                def tail(c):
                    act.wait_ge(s("xa_turned"), c + 1 + XA0[x])
                    act.activation(pT, N[:, 1, :], ACT.Copy).then_inc(s("xa_pT"), 1)
                    act.wait_ge(s("xa_out"), c + 1 + XA0[x])
                    apart()
                    act.activation(hic[:, :, c, :], G[:, 0, :].rearrange("p (k t) -> p k t", k=KT), ACT.Copy)\
                       .then_inc(s("xa_o_hi"), 1)

                act.wait_ge(s("evacuated"), PROD0["xo" + x])
                stage(0)
                with act.Fori(0, NCH - 1) as c:
                    exps(c)
                    apart()
                    stage(c + 1)
                    tail(c)
                exps(NCH - 1)
                tail(NCH - 1)

            def ffn(name, two_tile_function):
                def hidden(c):
                    for j in range(2):
                        act.wait_ge(s("ff_gate_in"), 2 * c + j + 1 + FF0[name])
                        act.activation(W[:, 16 + j, :], W[:, 16 + j, :] if name == "ffn1" else TMP[:, j, :],
                                       two_tile_function).then_inc(s("ff_gate"), 1)
                    q = s("product_quarters")
                    if not isinstance(c, int):
                        act.wait_ge(q, c * 24 + 4 * (BLOCK0[name] + 4))
                    elif c:
                        act.wait_ge(q, 24 * c + 4 * (BLOCK0[name] + 4))
                    for j in range(2):
                        act.wait_ge(s("ff_hidden"), 2 * c + j + 1 + FF0[name])
                        act.activation(g_hi[:, j, :], W[:, 16 + j, :], ACT.Copy).then_inc(s("ff_g_hi"), 1)

                hidden(0)
                with act.Fori(1, FC) as c:
                    hidden(c)

            ev = lambda name: (lambda k: (s("evacuated"), PROD0[name] + k + 1))
            h_tile = lambda k: W[:, k, :]
            y_tile = lambda k: W[:, 8 + k, :]
            for k in range(KT):
                load(W[:, k, :], ap["xT"][:, k, :], f"x_in{k}")
            load(W[:, 20:22, :], ap["memT1"], "1_mem_in")
            memory("1")
            squares("q1", h_tile, ev("out1"))
            split_high("q1", h_tile, "x1", lambda k: (s("evacuated"), PROD0["k1"]))
            roots("q1")
            cross("1")
            squares("ffn1", h_tile, ev("xo1"))
            split_high("ffn1", h_tile, "ffn1", lambda k: (s("evacuated"), PROD0["ffn1"]))
            roots("ffn1")
            ffn("ffn1", ACT.Gelu)
            last_tile = lambda k: (s("evacuated"), PROD0["z2"] - KT + k + 1)
            squares("final", h_tile, last_tile)
            roots("final")
            load(phase[:, :], ap["consts"][:, CST["hg_reset"]:CST["hg_reset"] + 512], "phase2_in")
            for k in range(KT):
                act.wait_ge(s("h_final"), k + 1)
                act.activation(act_hi[:, k, :], W[:, k, :], ACT.Identity, scale=col("mix2", k)).then_inc(s("operand_hi"), 1)
                if k >= 2:
                    act.wait_ge(*norm("squares_summed", "z2", k - 1))
                act.activation(sq[k % 2], W[:, k, :], ACT.Square).then_inc(s("squares"), 1)
                act.wait_ge(*norm("squares", "z2", k + 1))
                load(ap["parked"][:, k, :], W[:, k, :], "parked")
            roots("z2")
            for n in range(22):
                if n < 4 or 12 <= n < 16 or 4 <= n < 8:
                    act.wait_ge(s("evacuated"), PROD0["z2"] + n + 1)
                    act.activation(W[:, n, :], W[:, n, :], ACT.Sigmoid if 4 <= n < 8 else ACT.Silu)\
                       .then_inc(s("z2_act"), 1)
                if n == 7:
                    act.wait_ge(s("lb_diff"), 1)
                    act.activation(small[:, 48:52], small[:, 48:52], ACT.Exp).then_inc(s("lb_exp"), 1)
            act.wait_ge(s("evacuated"), PROD0["out2"])
            qst = hi_free[:, 0, 0:512].rearrange("p (k t) -> p k t", k=4)
            kv = hi_free[:, 0, 512:1024].rearrange("p (a t) -> p a t", a=2)
            vtk = hi_free[:, 3, 0:256]
            pr = hi_free[:, 1:3, :].rearrange("p a t -> p (a t)")
            pTs = lo_free[:, 0:2, :].rearrange("p a t -> p (a t)")
            ssb = lo_free[:, 2:4, :].rearrange("p a t -> p (a t)")

            def windowed(c):
                if not isinstance(c, int):
                    act.wait_ge(s("sw_v_turned"), c)
                    act.wait_ge(s("sw_scores"), c)
                    apart()
                act.activation(qst, Wc[:, 16:20, c, :], ACT.Copy).then_inc(s("sw_staged"), 1)
                if isinstance(c, int):
                    act.activation(kv[:, :, 0:P], Wc[:, 20:22, c, :], ACT.Copy).then_inc(s("sw_staged"), 1)
                else:
                    act.activation(kv[:, :, 0:P], Wc[:, 20:22, c - 1, :], ACT.Copy).then_inc(s("sw_staged"), 1)
                act.activation(kv[:, 0, P:2 * P], Wc[:, 20, c, :], ACT.Copy).then_inc(s("sw_staged"), 1)
                act.activation(kv[:, 1, P:2 * P], Wc[:, 21, c, :], ACT.Copy).then_inc(s("sw_staged"), 1)
                act.wait_ge(s("sw_v_turned"), c + 1)
                act.activation(vtk, G[:, 1, 0:256], ACT.Copy).then_inc(s("sw_v"), 1)
                act.wait_ge(s("sw_negmax"), c + 1)
                for n in range(8):
                    last = act.activation(pr[:, n * 256:(n + 1) * 256], ssb[:, n * 256:(n + 1) * 256], ACT.Exp,
                                          bias=small[:, 8 + n:9 + n], accum_out=small[:, 16 + n:17 + n])
                act.activation(small[:, 24:32], small[:, 32:40], ACT.Exp).then_inc(s("sw_exps"), 1)
                act.wait_ge(s("sw_turned"), c + 1)
                for n in range(2):
                    act.activation(pTs[:, n * T:(n + 1) * T], G[:, n, :], ACT.Copy).then_inc(s("sw_pT"), 1)
                act.wait_ge(s("sw_pv"), c + 1)
                apart()
                act.activation(hic[:, 0:4, c, :], Nb[0], ACT.Copy).then_inc(s("sw_o_hi"), 1)

            windowed(0)
            with act.Fori(1, NCH) as c:
                windowed(c)
            lf, b_, D1, E1, E1n, Eb, D2, E2, vs, vtok, k2tok = hg("lf b D1 E1 E1n Eb D2 E2 vs vtok k2tok")
            act.wait_ge(s("sw_o_lo"), NCH + 1)
            act.wait_ge(s("hg_f"), 4)
            with act.Fori(0, NCH) as c:
                act.wait_ge(s("hg_kept"), c + 1)
                act.wait_ge(s("hg_S"), 2 * c + 1)
                apart()
                act.activation(lf, Wc[:, 4:8, c, :], ACT.Ln).then_inc(s("hg_log"), 1)
                act.activation(vs, Wc[:, 8:12, c, :], ACT.Copy).then_inc(s("hg_v"), 1)
                act.wait_ge(s("hg_d"), 2 * c + 1)
                act.activation(E1, D1, ACT.Exp).then_inc(s("hg_exp"), 1)
                act.activation(E1n, D1, ACT.Exp, scale=-1.0).then_inc(s("hg_exp"), 1)
                act.activation(Eb, b_, ACT.Exp).then_inc(s("hg_exp"), 1)
                act.wait_ge(s("hg_d"), 2 * c + 2)
                act.activation(E2, D2, ACT.Exp).then_inc(s("hg_exp"), 1)
                act.wait_ge(s("hg_turned"), c + 1)
                act.activation(vtok, Gb[0], ACT.Copy).then_inc(s("hg_tokens"), 1)
                act.activation(k2tok, Gb[1], ACT.Copy).then_inc(s("hg_tokens"), 1)
            for n in range(4):
                act.wait_ge(s("hg_kept"), NCH + 1)
                act.activation(W[:, 16, :], W[:, n, :], ACT.Square).then_inc(s("hr_sq"), 1)
                roots("hr", n + 1, 1.0 / P, None, W[:, 17, :])
                act.wait_ge(s("hr_y"), n + 1)
                act.activation(act_hi[:, 4 + n, :], W[:, n, :], ACT.Copy).then_inc(s("y2_hi"), 1)
            act.wait_ge(s("y2_lo"), 4)
            act.wait_ge(s("parked"), 16 * KT)
            for k in range(KT):
                load(W[:, k, :], ap["parked"][:, k, :], f"x_in{k}")
            load(W[:, 20:22, :], ap["memT2"], "2_mem_in")

            def post(name, nxt, gain, src_done):
                squares(name, y_tile, src_done)
                roots(name)
                for k in range(KT):
                    act.wait_ge(s(name + "_h"), k + 1)
                    act.activation(act_hi[:, k, :], W[:, k, :], ACT.Identity, scale=col(gain, k)).then_inc(s("operand_hi"), 1)
                    if k >= 2:
                        act.wait_ge(*norm("squares_summed", nxt, k - 1))
                    act.activation(sq[k % 2], W[:, k, :], ACT.Square).then_inc(s("squares"), 1)

            post("pm", "q2", "x2", ev("out2"))
            memory("2")
            roots("q2")
            cross("2")
            post("px", "ffn2", "ffn2", ev("xo2"))
            roots("ffn2")
            ffn("ffn2", ACT.Silu)
            squares("pf", y_tile, lambda k: (s("evacuated"), PROD0["ffn2"] + 12 * FC - KT + k + 1))
            roots("pf")
            for k in range(KT):
                act.wait_ge(s("pf_h"), k + 1)
                load(ap["out"][:, k, :], W[:, k, :], "stored")
            act.wait_ge(s("stored"), 16 * KT)

        @block.vector
        def _(dve):
            chain = Chain(dve, s("dve_chain"))
            link = chain.link

            def product(name, j, width=None):
                dve.wait_ge(s("product_quarters"), 4 * (j + (BLOCK0[name] + 1)) if not isinstance(j, int) else
                            4 * (BLOCK0[name] + 1 + j))

            def slot(name, j):
                return G[:, (PROD0[name] + j) % 2, :]

            def sums(name, k):
                dve.wait_ge(*norm("squares", name, k + 1))
                if k:
                    dve.wait_ge(*norm("squares_summed", name, k))
                    dve.tensor_tensor(ssum, ssum, sq[k % 2], ALU.add).then_inc(s("squares_summed"), 1)
                else:
                    dve.tensor_copy(ssum, sq[0]).then_inc(s("squares_summed"), 1)

            def reciprocal_root(name, n=1, tile=None, out=None):
                dve.wait_ge(*norm("roots", name, n, 1))
                link(dve.reciprocal(rstd[:, :] if out is None else out, root if tile is None else tile))

            def split_low(name, k, src, gain):
                dve.wait_ge(*operand_count("operand_hi", name, k + 1))
                dve.scalar_tensor_tensor(act_lo[:, k, :], src(k), col(gain, k), hi_as_f32[:, k, :], ALU.mult,
                                         ALU.subtract).then_inc(s("operand_lo"), 1)

            def low(name, k, tile, hi_count):
                dve.wait_ge(s(name + "_hi"), hi_count)
                dve.tensor_tensor(act_lo[:, k, :], tile, hi_as_f32[:, k, :], ALU.subtract).then_inc(s(name + "_lo"), 1)

            def standardize(name, jobs, div, before=None):
                done = 0
                for n, tiles in enumerate(jobs):
                    dve.wait_ge(s("std_mean"), STD0[name][0] + n + 1)
                    for t, tile in enumerate(tiles):
                        dve.scalar_tensor_tensor(tile, N[:, 0, :], -1.0 / div, tile, ALU.mult, ALU.add)\
                           .then_inc(s("std_centred"), 1)
                    dve.wait_ge(s("std_root"), STD0[name][0] + n + 1)
                    link(dve.reciprocal(W[:, 0, :], W[:, 0, :]))
                    for t, tile in enumerate(tiles):
                        dve.wait_ge(s("std_centred"), STD0[name][1] + done + t + 1)
                        dve.tensor_tensor(tile, tile, W[:, 0, :], ALU.mult).then_inc(s("std_scaled"), 1)
                    done += len(tiles)
                    dve.wait_ge(s("std_scaled"), STD0[name][1] + done)

            h_tile = lambda k: W[:, k, :]
            y_tile = lambda k: W[:, 8 + k, :]

            for free in ("ml_kept", "xa_o_lo", "sw_o_lo", "hg_kept", "hg_S"):
                dve.sem_inc(s(free), 1)
            dve.memset(epsc[:, 0:1], RMS_EPS).then_inc(s("eps"), 1)
            dve.memset(epsc[:, 1:2], LN_EPS).then_inc(s("eps"), 1)
            dve.wait_ge(s("consts"), 32)
            for k in range(KT):
                split_low("z1", k, h_tile, "mix1")
                sums("z1", k)
            reciprocal_root("z1")

            def evacuate(j, dst):
                product("z1", j)
                dve.tensor_tensor(dst, slot("z1", j), rstd[:, :], ALU.mult).then_inc(s("evacuated"), 1)

            def conv(acc, x, weight, bias, taps, lo, hi):
                for n in range(lo, hi):
                    w = weight(taps - 1 - n)
                    if n == 0:
                        ins = dve.tensor_scalar(acc, x, w, bias, ALU.mult, ALU.add)
                    else:
                        ins = dve.scalar_tensor_tensor(acc[:, n:T], x[:, 0:T - n], w, acc[:, n:T], ALU.mult, ALU.add)
                    link(ins)

            def conv_b(n, lo, hi):
                conv(W[:, 2 + n, :], W[:, n, :], lambda j: col("cb_w", 31 * n + j), col("cb_b", n), 31, lo, hi)

            def conv_c(n):
                conv(W[:, 16 + n, :], W[:, 4 + n, :], lambda j: col("cc_w", 4 * n + j), col("cc_b", n), 4, 0, 4)
                dve.sem_inc(s("cc_done"), 1)

            product("z1", 0)
            dve.tensor_tensor(rowA, slot("z1", 0), rstd[:, :], ALU.mult).then_inc(s("evacuated"), 1)
            dve.wait_ge(s("evacuated"), 1)
            H4 = slice(0, NH)
            link(dve.tensor_scalar(rowF[H4], rowA[32:36, :], cols[32:36, COL["gate_b"]:COL["gate_b"] + 1], None, ALU.add))
            link(dve.tensor_scalar(rowA[H4], rowA[H4], cols[H4, COL["gate_b"]:COL["gate_b"] + 1], None, ALU.add))
            dve.sem_inc(s("row_forget"), 1)
            link(dve.memset(rowM[H4], 1.0))
            chunked = lambda v: v[H4].rearrange("p (c t) -> p c t", t=CH)
            link(dve.memset(chunked(rowM)[:, :, 0:1], 0.0))
            dve.wait_ge(s("row_abs"), 1)
            link(dve.tensor_scalar(rowF[H4], rowF[H4], 0.0, None, ALU.min))
            dve.wait_ge(s("row_log"), 1)
            link(dve.tensor_tensor(rowF[H4], rowF[H4], rowE[H4], ALU.subtract))
            link(dve.tensor_tensor_scan(rowE[H4], rowM[H4], rowF[H4], 0.0, ALU.mult, ALU.add))
            link(dve.tensor_tensor(rowA[H4], rowA[H4], rowE[H4], ALU.subtract))
            link(dve.memset(rowF[H4], 0.0))
            link(dve.tensor_copy(chunked(rowF)[:, 1:NCH, 0:1], chunked(rowE)[:, 0:NCH - 1, CH - 1:CH]))
            link(dve.tensor_tensor_scan(rowM[H4], rowF[H4], rowA[H4], 0.0, ALU.add, ALU.max))
            mprev = small[H4, 40:48].rearrange("p (c t) -> p c t", t=1)
            link(dve.memset(mprev[:, 0:1, :], 0.0))
            link(dve.tensor_tensor(mprev[:, 1:NCH, :], chunked(rowM)[:, 0:NCH - 1, CH - 1:CH],
                                   chunked(rowE)[:, 0:NCH - 1, CH - 1:CH], ALU.add))
            link(dve.tensor_tensor(chunked(rowF), mprev.to_broadcast([NH, NCH, CH]), chunked(rowM), ALU.subtract))
            link(dve.scalar_tensor_tensor(rowE[H4], rowE[H4], -1.0, rowM[H4], ALU.mult, ALU.subtract))
            link(dve.tensor_scalar(rowM[H4], rowM[H4], -1.0, None, ALU.mult))
            dve.sem_inc(s("ml_rows"), 1)

            for j in range(4):
                evacuate(1 + j, W[:, j, :])
            for n in range(2):
                dve.wait_ge(s("cf_gate"), n + 1)
                link(dve.tensor_tensor(W[:, n, :], W[:, n, :], W[:, 2 + n, :], ALU.mult))
            conv_b(0, 0, 3)
            for j in range(4):
                evacuate(5 + j, W[:, 4 + j, :])
                conv_b(0, 3 + 6 * j, 9 + 6 * j)
            dve.wait_ge(s("evacuated"), 9)
            conv_c(0)
            conv_c(1)
            for j in range(2):
                evacuate(9 + j, W[:, 8 + j, :])
                conv_c(2 + j)
            evacuate(11, W[:, 10, :])
            conv_b(0, 27, 31)
            dve.sem_inc(s("cb_done"), 1)
            evacuate(12, W[:, 11, :])
            conv_b(1, 0, 7)
            for j in range(4):
                evacuate(13 + j, W[:, 12 + j, :])
                conv_b(1, 7 + 6 * j, 13 + 6 * j)
            dve.sem_inc(s("cb_done"), 1)

            standardize("cf", [[W[:, 2, :]], [W[:, 3, :]]], 64)
            for n in range(2):
                low("y1", 2 + n, W[:, 2 + n, :], n + 1)
            standardize("ln", [[W[:, 10, :], W[:, 11, :]]], 256)
            dve.wait_ge(s("mix_in"), 80)
            link(dve.tensor_scalar(W[:, 0, 0:P], const("ml_mask"), 0.0, None, ALU.is_gt))
            dve.tensor_tensor(wsT.rearrange("p (h t) -> p h t", h=NH), wsT.rearrange("p (h t) -> p h t", h=NH),
                              W[:, 0:1, 0:P].to_broadcast([P, NH, P]), ALU.mult).then_inc(s("ws_masked"), 1)
            dve.wait_ge(s("ws_masked"), 1)
            dve.wait_ge(s("gm_mixed"), 1)
            dve.wait_ge(s("ln_out"), 2)
            for k in range(2):
                link(dve.tensor_tensor(W[:, k, :].rearrange("p (c t) -> p c t", t=CH),
                                       N[:, k, :].rearrange("p (c t) -> p c t", t=CH),
                                       bsv[:, k:k + 1, :].to_broadcast([P, NCH, CH]), ALU.add))
                dve.tensor_tensor(W[:, k, :], W[:, k, :], W[:, 8 + k, :], ALU.mult).then_inc(s("gm_y"), 1)
            for k in range(2):
                low("y1", k, W[:, k, :], 3 + k)
            dve.wait_ge(s("y1_lo"), 4)
            dve.sem_inc(s("ml_free"), 1)
            dve.memset(Cst, 0.0).then_inc(s("ml_init"), 1)
            dve.memset(vt[:, :, P:2 * P], 1.0).then_inc(s("ml_init"), 1)
            dve.wait_ge(s("ml_init"), 2)
            mask = const("ml_mask").rearrange("p (a t) -> p a t", a=1).to_broadcast([P, NH, P])
            with dve.Fori(0, NCH) as c:
                chain.enter(c, 0, 2)
                dve.wait_ge(s("ml_spread"), c + 1)
                dve.tensor_tensor(Et, Nb[0], mask, ALU.min).then_inc(s("ml_bounded"), 1)
                dve.wait_ge(s("ml_exp"), 3 * c + 1)
                dve.wait_ge(s("ml_qkv"), 3 * c + 1)
                dve.tensor_tensor(qw, qT, winter, ALU.mult).then_inc(s("ml_weighted"), 1)
                dve.wait_ge(s("ml_exp"), 3 * c + 2)
                dve.wait_ge(s("ml_proj"), c + 1)
                dve.tensor_tensor(kw, Gb[2], Wt[:, :, P - 1:P].to_broadcast([P, NH, P]), ALU.mult)\
                   .then_inc(s("ml_weighted"), 1)
                dve.wait_ge(s("ml_scores"), c + 1)
                dve.tensor_tensor(Pm, Nb[1], Wt, ALU.mult).then_inc(s("ml_weighted"), 1)
                dve.wait_ge(s("ml_exp"), 3 * c + 3)
                dve.wait_ge(s("ml_den"), c + 1)
                link(dve.tensor_tensor(dn, dn, emm, ALU.max))
                link(dve.reciprocal(dn, dn))
                dve.tensor_tensor(Wc[:, 4:8, c, :], Gb[0], dn, ALU.mult).then_inc(s("ml_h"), 1)
                dve.wait_ge(s("ml_update"), c + 1)
                for h in range(NH):
                    last = dve.scalar_tensor_tensor(Cst[:, h, :], Cst[:, h, :], winter[:, h, P - 1:P],
                                                    Gf[:, T + 256 * h:T + 256 * h + 256], ALU.mult, ALU.add)
                last.then_inc(s("ml_kept"), 1)
            chain.leave(NCH)
            dve.wait_ge(s("ml_h"), NCH)
            dve.wait_ge(s("ml_kept"), NCH + 1)
            standardize("hn", [[W[:, 4 + n, :]] for n in range(4)], P)
            for n in range(4):
                dve.wait_ge(s("hn_out"), n + 1)
                dve.wait_ge(s("ogate"), 4)
                link(dve.scalar_tensor_tensor(W[:, 16 + n, :], W[:, 16 + n, :], col("skip", n), W[:, 4 + n, :],
                                              ALU.mult, ALU.add))
                dve.tensor_tensor(W[:, 4 + n, :], W[:, 16 + n, :], W[:, 12 + n, :], ALU.mult).then_inc(s("ml_y"), 1)
                dve.wait_ge(s("ml_y"), n + 1)
            for n in range(4):
                low("y1", 4 + n, W[:, 4 + n, :], 5 + n)

            def memory(x):
                mem = flat[:, 20 * T:22 * T]
                dve.wait_ge(s(x + "_mem_root"), 1)
                link(dve.reciprocal(W[:, 14, 0:MEM], W[:, 14, 0:MEM]))
                m3 = mem.rearrange("p (k m) -> p k m", m=MEM)
                dve.tensor_tensor(m3, m3, W[:, 14:15, 0:MEM].to_broadcast([P, KT, MEM]), ALU.mult)\
                   .then_inc(s(x + "_mem_scaled"), 1)
                dve.wait_ge(s(x + "_mem_scaled"), 1)
                for k in range(KT):
                    dve.wait_ge(s(x + "_mem_hi"), k + 1)
                    dve.scalar_tensor_tensor(m_lo[:, k, :], m3[:, k, :], col("mem" + x, k), m_hi[:, k, :].bitcast(F32),
                                             ALU.mult, ALU.subtract).then_inc(s("mem_lo"), 1)

            def keys_values(x):
                kTm = flat[:, 16 * T:18 * T].rearrange("p (k m) -> p k m", m=MEM)
                vm = W[:, 18:20, :].rearrange("p a (n f) -> p a n f", f=P)
                with dve.Fori(0, KT // 2) as n:
                    for j in range(2):
                        product("k" + x, n * 2 + j)
                        dve.tensor_scalar(kTm[:, n * 2 + j, :], slot("k" + x, j)[:, 0:MEM], 1.0, None, ALU.mult)\
                           .then_inc(s("evacuated"), 1)
                with dve.Fori(0, KT // 2) as n:
                    for j in range(2):
                        product("v" + x, n * 2 + j)
                        src = slot("v" + x, j).rearrange("p (a f) -> p a f", a=2)[:, :, 0:P]
                        dve.tensor_scalar(vm[:, :, n * 2 + j, :], src, 1.0, None, ALU.mult).then_inc(s("evacuated"), 1)

            def queries(x):
                with dve.Fori(0, KT // 2) as n:
                    for j in range(2):
                        product("q" + x, n * 2 + j)
                        dve.scalar_tensor_tensor(W[:, 8:16, :][:, n * 2 + j, :], slot("q" + x, j), float(D // NH) ** -0.5, rstd[:, :],
                                                 ALU.mult, ALU.mult).then_inc(s("evacuated"), 1)

            def cross(x):
                scores = Nf[:, 0:T].rearrange("p (h m) -> p h m", h=NH)
                pr = TMP[:, 1, :].rearrange("p (h m) -> p h m", h=NH)

                def head(c):
                    dve.wait_ge(s("xa_scores"), c + 1 + XA0[x])
                    link(dve.tensor_reduce(small[:, 0:4], scores, AX, ALU.max))
                    dve.tensor_scalar(small[:, 4:8], small[:, 0:4], -1.0, None, ALU.mult).then_inc(s("xa_negmax"), 1)
                    dve.wait_ge(s("xa_exps"), c + 1 + XA0[x])
                    link(dve.reciprocal(small[:, 12:16], small[:, 8:12]))
                    dve.tensor_tensor(pr, pr, small[:, 12:16].rearrange("p (h m) -> p h m", m=1).to_broadcast([P, NH, MEM]),
                                      ALU.mult).then_inc(s("xa_probs"), 1)

                def tail(c):
                    dve.wait_ge(s("xa_o_hi"), c + 1 + XA0[x])
                    dve.tensor_tensor(loc[:, :, c, :], G[:, 0, :].rearrange("p (k t) -> p k t", k=KT), hicf[:, :, c, :],
                                      ALU.subtract).then_inc(s("xa_o_lo"), 1)

                with dve.Fori(0, NCH) as c:
                    chain.enter(c, 0, 2)
                    head(c)
                    tail(c)
                chain.leave(NCH)

            def ffn(name, target, conv_tiles):
                cf = cols[:, COL["cf"]:COL["cf"] + 4 * FT].rearrange("p (c j) -> p c j", j=8)

                def hidden(c):
                    static = isinstance(c, int)
                    for j in range(4):
                        dve.wait_ge(s("product_quarters"), 24 * c + 4 * (BLOCK0[name] + 1 + j) if static
                                    else c * 24 + 4 * (BLOCK0[name] - 1 + j))
                        dve.tensor_tensor(TMP[:, j, :], slot(name, j), rstd[:, :], ALU.mult).then_inc(s("evacuated"), 1)
                        if j < 2:
                            dve.wait_ge(s("evacuated"), c * 12 + (PROD0[name] + j + 1) if static
                                        else c * 12 + (PROD0[name] + j - 7))
                        if conv_tiles and j < 2:
                            acc, x = W[:, 16 + j, :], TMP[:, j, :]
                            w = lambda n: cf[:, c, 4 * j + n:4 * j + n + 1]
                            link(dve.tensor_scalar(acc, x, w(2), w(3), ALU.mult, ALU.add))
                            link(dve.scalar_tensor_tensor(acc[:, 1:T], x[:, 0:T - 1], w(1), acc[:, 1:T], ALU.mult, ALU.add))
                            dve.scalar_tensor_tensor(acc[:, 2:T], x[:, 0:T - 2], w(0), acc[:, 2:T], ALU.mult, ALU.add)\
                               .then_inc(s("ff_gate_in"), 1)
                        elif j < 2:
                            dve.sem_inc(s("ff_gate_in"), 1)
                    for j in range(2):
                        dve.wait_ge(s("evacuated"), c * 12 + (PROD0[name] + j + 3) if static
                                    else c * 12 + (PROD0[name] + j - 5))
                        dve.wait_ge(s("ff_gate"), 2 * c + j + 1 + FF0[name])
                        dve.tensor_tensor(W[:, 16 + j, :], W[:, 16 + j, :], TMP[:, 2 + j, :], ALU.mult)\
                           .then_inc(s("ff_hidden"), 1)

                def low_parts(c):
                    for j in range(2):
                        dve.wait_ge(s("ff_g_hi"), 2 * c + j + 1 + FF0[name])
                        dve.tensor_tensor(g_lo[:, j, :], W[:, 16 + j, :], g_hi[:, j, :].bitcast(F32), ALU.subtract)\
                           .then_inc(s("ff_g_lo"), 1)

                def add_down(c):
                    for o in range(KT):
                        first = 4 * (BLOCK0[name] + 8) + o + 1
                        dve.wait_ge(s("product_quarters"), c * 24 + (first - 24))
                        dve.tensor_tensor(target(o), target(o), slot(name, 4 + o), ALU.add).then_inc(s("evacuated"), 1)

                hidden(0)
                low_parts(0)
                with dve.Fori(1, FC) as c:
                    if conv_tiles:
                        chain.enter(c, 1, 4)
                    hidden(c)
                    add_down(c)
                    low_parts(c)
                if conv_tiles:
                    chain.leave(FC - 1)

            def last_down(name, target, norm):
                for o in range(KT):
                    dve.wait_ge(s("product_quarters"), 4 * (BLOCK0[name] + 6 * FC - 2) + o + 1)
                    dve.tensor_tensor(target(o), target(o), slot(name, o), ALU.add).then_inc(s("evacuated"), 1)
                    if o:
                        sums(norm, o - 1)
                sums(norm, KT - 1)

            def to_tiles(name, norm, target, add, loaded=None):
                for j in range(KT):
                    product(name, j)
                    if loaded:
                        dve.wait_ge(*loaded(j))
                    if add:
                        ins = dve.tensor_tensor(target(j), target(j), slot(name, j), ALU.add)
                    else:
                        ins = dve.tensor_copy(target(j), slot(name, j))
                    ins.then_inc(s("evacuated"), 1)
                    if j:
                        sums(norm, j - 1)
                sums(norm, KT - 1)

            def operand(name, gain):
                for k in range(KT):
                    split_low(name, k, h_tile, gain)
                reciprocal_root(name)

            memory("1")
            to_tiles("out1", "q1", h_tile, True, lambda j: (s(f"x_in{j}"), 32))
            for k in range(KT):
                split_low("q1", k, h_tile, "x1")
            keys_values("1")
            reciprocal_root("q1")
            queries("1")
            cross("1")
            to_tiles("xo1", "ffn1", h_tile, True)
            operand("ffn1", "ffn1")
            ffn("ffn1", h_tile, True)
            last_down("ffn1", h_tile, "final")
            reciprocal_root("final")
            for k in range(KT):
                dve.scalar_tensor_tensor(W[:, k, :], W[:, k, :], col("final", k), rstd[:, :], ALU.mult, ALU.mult)\
                   .then_inc(s("h_final"), 1)
                if k:
                    split_low("z2", k - 1, h_tile, "mix2")
                    sums("z2", k - 1)
            split_low("z2", KT - 1, h_tile, "mix2")
            sums("z2", KT - 1)
            reciprocal_root("z2")
            dve.wait_ge(s("parked"), 16 * KT)
            for j in range(22):
                product("z2", j)
                dve.tensor_tensor(W[:, j, :], slot("z2", j), rstd[:, :], ALU.mult).then_inc(s("evacuated"), 1)
                if j == 8:
                    lb = cols[:, COL["lb"]:COL["lb"] + 8]
                    link(dve.tensor_tensor(small[:, 48:52], lb[:, 4:8], lb[:, 0:4], ALU.subtract))
                    dve.sem_inc(s("lb_diff"), 1)
                    dve.wait_ge(s("lb_exp"), 1)
                    link(dve.tensor_scalar(small[:, 48:52], small[:, 48:52], 1.0, None, ALU.add))
                    link(dve.reciprocal(small[:, 48:52], small[:, 48:52]))
                    link(dve.tensor_scalar(small[:, 52:56], small[:, 48:52], -1.0, 1.0, ALU.mult, ALU.add))
                if 8 < j <= 12:
                    n = j - 9
                    dve.wait_ge(s("z2_act"), 4 + n + 1)
                    dve.tensor_scalar(W[:, 4 + n, :], W[:, 4 + n, :], small[:, 52 + n:53 + n], small[:, 48 + n:49 + n],
                                      ALU.mult, ALU.add).then_inc(s("hg_f"), 1)

            pr = hi_free[:, 1:3, :].rearrange("p a t -> p (a t)").rearrange("p (h m) -> p h m", m=256)
            ssb = lo_free[:, 2:4, :].rearrange("p a t -> p (a t)").rearrange("p (h m) -> p h m", m=256)
            s3 = Nf.rearrange("p (h m) -> p h m", m=256)

            def windowed(c):
                mask = const("swa_first" if isinstance(c, int) else "swa_rest", 256).rearrange("p (a t) -> p a t", a=1)
                dve.wait_ge(s("sw_scores"), c + 1)
                link(dve.scalar_tensor_tensor(ssb, s3, 0.125, mask.to_broadcast([P, 8, 256]), ALU.mult, ALU.min))
                link(dve.tensor_reduce(small[:, 0:8], ssb, AX, ALU.max))
                link(dve.tensor_tensor(small[:, 0:8], small[:, 0:8], cols[:, COL["sinks"]:COL["sinks"] + 8], ALU.max))
                link(dve.tensor_tensor(small[:, 32:40], cols[:, COL["sinks"]:COL["sinks"] + 8], small[:, 0:8],
                                       ALU.subtract))
                dve.tensor_scalar(small[:, 8:16], small[:, 0:8], -1.0, None, ALU.mult).then_inc(s("sw_negmax"), 1)
                dve.wait_ge(s("sw_exps"), c + 1)
                link(dve.tensor_tensor(small[:, 16:24], small[:, 16:24], small[:, 24:32], ALU.add))
                link(dve.reciprocal(small[:, 16:24], small[:, 16:24]))
                dve.tensor_tensor(pr, pr, small[:, 16:24].rearrange("p (h m) -> p h m", m=1).to_broadcast([P, 8, 256]),
                                  ALU.mult).then_inc(s("sw_probs"), 1)
                dve.wait_ge(s("sw_o_hi"), c + 1)
                dve.tensor_tensor(loc[:, 0:4, c, :], Nb[0], hicf[:, 0:4, c, :], ALU.subtract).then_inc(s("sw_o_lo"), 1)

            windowed(0)
            with dve.Fori(1, NCH) as c:
                chain.enter(c, 1, 6)
                windowed(c)
            chain.leave(NCH - 1)
            Q1, Q2, K1, K2, AT, S, lf, b_, D1, D2, E1, E1n, Eb, E2 = hg("Q1 Q2 K1 K2 AT S lf b D1 D2 E1 E1n Eb E2")
            qscale = float(P) ** -0.5
            dve.wait_ge(s("sw_o_lo"), NCH + 1)
            link(dve.memset(AT, 0.0))
            link(dve.memset(S, 0.0))
            dve.sem_inc(s("hg_init"), 1)
            dve.wait_ge(s("phase2_in"), 16)
            hmask = const("hg_mask").bitcast(U32).rearrange("p (a t) -> p a t", a=1).to_broadcast([P, NH, P])
            halves = lambda v: v.rearrange("p h (a t) -> p (h a) t", t=64)
            with dve.Fori(0, NCH) as c:
                chain.enter(c, 0, 1)
                dve.wait_ge(s("hg_log"), c + 1)
                link(dve.tensor_tensor_scan(b_.rearrange("p h t -> p (h t)"), phase[:, :],
                                            lf.rearrange("p h t -> p (h t)"), 0.0, ALU.mult, ALU.add))
                dve.tensor_tensor(halves(D1), halves(b_), halves(b_)[:, :, 31:32].to_broadcast([P, 8, 64]), ALU.subtract)\
                   .then_inc(s("hg_d"), 1)
                dve.tensor_tensor(halves(D2), halves(b_)[:, :, 63:64].to_broadcast([P, 8, 64]), halves(b_), ALU.subtract)\
                   .then_inc(s("hg_d"), 1)
                q_, f_ = Wc[:, 0:4, c, :], Wc[:, 4:8, c, :]
                dve.wait_ge(s("hg_exp"), 4 * c + 1)
                dve.scalar_tensor_tensor(Q1, q_, qscale, E1, ALU.mult, ALU.mult).then_inc(s("hg_qk"), 1)
                dve.wait_ge(s("hg_exp"), 4 * c + 2)
                dve.scalar_tensor_tensor(K1, f_, 1.0, E1n, ALU.subtract, ALU.mult, reverse0=True).then_inc(s("hg_qk"), 1)
                dve.wait_ge(s("hg_exp"), 4 * c + 3)
                dve.scalar_tensor_tensor(Q2, q_, qscale, Eb, ALU.mult, ALU.mult).then_inc(s("hg_qk"), 1)
                dve.wait_ge(s("hg_exp"), 4 * c + 4)
                dve.scalar_tensor_tensor(K2, f_, 1.0, E2, ALU.subtract, ALU.mult, reverse0=True).then_inc(s("hg_qk"), 1)
                dve.wait_ge(s("hg_scores"), c + 1)
                dve.memset(small[:, 60:61], 0.0)
                dve.copy_predicated(AT, hmask, Nb[0]).then_inc(s("hg_masked"), 1)
                for sub in range(2):
                    dve.wait_ge(s("hg_update"), 2 * c + (sub + 1))
                    if sub:
                        dve.wait_ge(s("hg_S"), 2 * c + 2)
                    for h in range(NH):
                        last = dve.scalar_tensor_tensor(S[:, h, :], S[:, h, :], Eb[:, h, 64 * sub + 63:64 * sub + 64],
                                                        Nb[2 + sub][:, h, :], ALU.mult, ALU.add)
                    last.then_inc(s("hg_S"), 1)
                dve.tensor_scalar(Wc[:, 0:4, c, :], Nb[1], 1.0, None, ALU.mult).then_inc(s("hg_kept"), 1)
            chain.leave(NCH)
            dve.wait_ge(s("hg_kept"), NCH + 1)
            for n in range(4):
                dve.wait_ge(s("hr_root"), n + 1)
                link(dve.reciprocal(W[:, 17, :], W[:, 17, :]))
                link(dve.scalar_tensor_tensor(W[:, n, :], W[:, n, :], col("onorm", 0), W[:, 17, :], ALU.mult, ALU.mult))
                dve.tensor_tensor(W[:, n, :], W[:, n, :], W[:, 12 + n, :], ALU.mult).then_inc(s("hr_y"), 1)
                dve.wait_ge(s("hr_y"), n + 1)
                low("y2", 4 + n, W[:, n, :], n + 1)

            def post(name, nxt, post_gain, gain, loaded=None):
                reciprocal_root(name)
                for k in range(KT):
                    if loaded:
                        dve.wait_ge(*loaded(k))
                    link(dve.scalar_tensor_tensor(root, W[:, 8 + k, :], col(post_gain, k), rstd[:, :], ALU.mult, ALU.mult))
                    dve.tensor_tensor(W[:, k, :], W[:, k, :], root, ALU.add).then_inc(s(name + "_h"), 1)
                    dve.wait_ge(s(name + "_h"), k + 1)
                    if nxt and k:
                        split_low(nxt, k - 1, h_tile, gain)
                        sums(nxt, k - 1)
                if nxt:
                    split_low(nxt, KT - 1, h_tile, gain)
                    sums(nxt, KT - 1)

            to_tiles("out2", "pm", y_tile, False)
            post("pm", "q2", "post_mix", "x2", lambda k: (s(f"x_in{k}"), 48))
            memory("2")
            keys_values("2")
            reciprocal_root("q2")
            queries("2")
            cross("2")
            to_tiles("xo2", "px", y_tile, False)
            post("px", "ffn2", "post_x", "ffn2")
            reciprocal_root("ffn2")
            link(dve.memset(W[:, 8:16, :], 0.0))
            ffn("ffn2", y_tile, False)
            last_down("ffn2", y_tile, "pf")
            post("pf", None, "post_ffn", None)


def packed(w):
    return w.reshape(KT, P, -1, P).transpose(2, 1, 0, 3).reshape(-1, P, KT * P)


def packed_down(w, c):
    w = w[2 * P * c:2 * P * (c + 1)].reshape(2, P, 2, 4, P)
    return w.transpose(2, 1, 3, 0, 4).reshape(2, P, KT * P)


def packed_ffn(gate, up, down):
    gate, up = packed(gate), packed(up)
    out = []
    for c in range(FC + 1):
        if c < FC:
            out += [gate[2 * c:2 * c + 2], up[2 * c:2 * c + 2]]
        if c:
            out.append(packed_down(down, c - 1))
    return out


def columns(v):
    return v.reshape(-1, P).T


def constants():
    c = np.zeros((P, NCONST), np.float32)

    def put(name, value):
        c[:value.shape[0], CST[name]:CST[name] + value.shape[1]] = value

    r = np.arange(P)
    put("ident", np.eye(P))
    put("ones", np.ones((P, P)))
    put("blk", (r[:, None] // 64 == r[None] // 64) * 1.0)
    put("ml_mask", np.where(r[:, None] <= r[None], BIG, NEG))
    key, query = np.arange(256)[None] // 64, r[:, None] // 64
    seen = (key >= query) & (key <= query + 2)
    put("swa_rest", np.where(seen, BIG, NEG))
    put("swa_first", np.where(seen & (key >= 2), BIG, NEG))
    put("hg_mask", ((r[:, None] // 64 == r[None] // 64) & (r[:, None] <= r[None])) * 1.0)
    put("hg_reset", np.tile((np.arange(512) % 64 != 0) * 1.0, (P, 1)))
    put("sel", np.repeat(np.eye(NH), P, axis=1))
    return c


def kernel(**inputs):
    import concourse.bacc as bacc
    from concourse.bass_utils import run_bass_kernel_spmd

    i = {name: np.asarray(a) for name, a in inputs.items()}
    v = {name: a[0] for name, a in i.items() if name not in ("final_g",)}
    w_in = v["w_in"]
    gates = np.zeros((D, P), np.float32)
    gates[:, 0:NH] = w_in[:, 2048:2052]
    gates[:, 32:32 + NH] = w_in[:, 2052:2056]
    z1 = np.concatenate([gates, w_in[:, 512:1024], w_in[:, 1024:1536], w_in[:, 0:512], w_in[:, 1536:2048]], 1)
    w2 = v["w_in_2"]
    pair = [64 * h + d for n in range(4) for h in (n, 4 + n) for d in range(64)]
    z2 = np.concatenate([w2[:, 768:2816], w2[:, 0:512][:, pair], w2[:, 512:768]], 1)
    w_out2 = np.concatenate([v["w_out_2"][0:512][pair], v["w_out_2"][512:]], 0)
    stream = [packed(z1), packed(v["w_out"]), packed(v["w_xkv"]), packed(v["w_xq"]), packed(v["w_xo"]),
              *packed_ffn(v["w_up"][:, :FT * P], v["w_up"][:, FT * P:], v["w_down"]),
              packed(z2), packed(w_out2), packed(v["wk_x_2"]), packed(v["wv_x_2"]), packed(v["wq_x_2"]),
              packed(v["wo_x_2"]), *packed_ffn(v["w_gate_2"], v["w_up_2"], v["w_down_2"])]
    gate_b = np.zeros((P, 1), np.float32)
    gate_b[0:NH, 0], gate_b[32:32 + NH, 0] = v["b_igate"], v["b_fgate"]
    conv_f = np.concatenate([v["conv_f_w"], v["conv_f_b"][None]], 0)
    by = {"mix1": columns(v["norm_mix_g"]), "lna_g": columns(v["ln_a_g"]), "lna_b": columns(v["ln_a_b"]),
          "cb_w": columns(v["conv_b_w"].reshape(31, 2, P).transpose(1, 0, 2)),
          "cb_b": columns(v["conv_b_b"]), "gnb_g": columns(v["gn_b_g"]), "gnb_b": columns(v["gn_b_b"]),
          "cc_w": columns(v["conv_c_w"].reshape(4, 4, P).transpose(1, 0, 2)), "cc_b": columns(v["conv_c_b"]),
          "hn_g": columns(v["hn_c_g"]), "skip": columns(v["skip_c"]), "x1": columns(v["norm_x_g"]),
          "mem1": columns(v["norm_mem_g"]), "ffn1": columns(v["norm_ffn_g"]),
          "cf": columns(conv_f.reshape(4, FT, P).transpose(1, 0, 2)), "final": columns(i["final_g"]),
          "mix2": columns(v["g_mix_pre_2"]), "post_mix": columns(v["g_mix_post_2"]), "mem2": columns(v["g_mem_2"]),
          "x2": columns(v["g_x_pre_2"]), "post_x": columns(v["g_x_post_2"]), "ffn2": columns(v["g_ffn_pre_2"]),
          "post_ffn": columns(v["g_ffn_post_2"]), "lb": columns(i["hgrn_lb_2"]), "onorm": columns(v["hgrn_onorm_2"]),
          "sinks": np.broadcast_to(v["sinks_2"], (P, 8)), "gate_b": gate_b}
    tiles = lambda a: a.T.reshape(KT, P, -1).transpose(1, 0, 2)
    arrays = {
        "wstream": np.concatenate(stream, 0),
        "cols": np.concatenate([by[name] for name, _ in COLS], 1),
        "consts": constants(),
        "xT": tiles(v["x"]),
        "memT1": tiles(v["mem"]).reshape(P, 2, T),
        "memT2": tiles(v["mem_2"]).reshape(P, 2, T),
        "w_q": v["w_q_c"].transpose(1, 0, 2).reshape(P, -1),
        "w_k": v["w_k_c"].transpose(1, 0, 2).reshape(P, -1),
        "w_v": v["w_v_c"].transpose(1, 0, 2).reshape(P, -1),
        "w_sT": v["w_s"].transpose(2, 0, 1).reshape(P, -1),
        "b_s": np.repeat(v["b_s"].reshape(2, 2, 1, P), 64, axis=2).reshape(2, P, P).transpose(1, 0, 2).reshape(P, -1),
    }
    arrays = {name: np.ascontiguousarray(a, np.float32) for name, a in arrays.items()}
    nc = bacc.Bacc("TRN2", target_bir_lowering=False, num_devices=1)
    ap = {name: nc.dram_tensor(name, a.shape, F32, kind="ExternalInput").ap() for name, a in arrays.items()}
    ap["out"] = nc.dram_tensor("out", (P, KT, T), F32, kind="ExternalOutput").ap()
    ap["parked"] = nc.dram_tensor("parked", (P, KT, T), F32, kind="Internal").ap()
    program(nc, ap)
    result = run_bass_kernel_spmd(nc, [arrays], core_ids=[0]).results[0]["out"]
    return np.asarray(result).transpose(2, 1, 0).reshape(1, T, D)
```

```python
from contextlib import ExitStack

import numpy as np

import concourse.bass as bass
from concourse import mybir

F32 = mybir.dt.float32
F32R = mybir.dt.float32r
U32 = mybir.dt.uint32
ACT = mybir.ActivationFunctionType
ALU = mybir.AluOpType
AX = mybir.AxisListType.X

P = 128
T = 1024
D = 1024
KT = D // P
HALF = 512
CH = 128
NCH = T // CH
MEM = 256
FT = 22
FC = FT // 2
NH = 4
BIG = 3.0e38
NEG = -1.0e30
RMS_EPS = 1e-6
LN_EPS = 1e-5

STAGES = [("z1", 17, 17), ("out1", 8, 8), ("k1", 8, 8), ("v1", 8, 2), ("q1", 8, 8), ("xo1", 8, 8),
          ("ffn1", 6 * FC, 12 * FC),
          ("z2", 22, 22), ("out2", 8, 8), ("k2", 8, 8), ("v2", 8, 2), ("q2", 8, 8), ("xo2", 8, 8),
          ("ffn2", 6 * FC, 12 * FC)]
BLOCK0, PROD0 = {}, {}
_b = _p = 0
for _name, _nb, _np_ in STAGES:
    BLOCK0[_name], PROD0[_name] = _b, _p
    _b, _p = _b + _nb, _p + _np_
NBLOCKS = _b

COLS = [("mix1", 8), ("lna_g", 2), ("lna_b", 2), ("cb_w", 62), ("cb_b", 2), ("gnb_g", 2), ("gnb_b", 2),
        ("cc_w", 16), ("cc_b", 4), ("hn_g", 4), ("skip", 4), ("x1", 8), ("mem1", 8), ("ffn1", 8),
        ("cf", 4 * FT), ("final", 8), ("mix2", 8), ("post_mix", 8), ("mem2", 8), ("x2", 8),
        ("post_x", 8), ("ffn2", 8), ("post_ffn", 8), ("lb", 8), ("onorm", 1), ("sinks", 8), ("gate_b", 1)]
COL = {}
_c = 0
for _name, _n in COLS:
    COL[_name] = _c
    _c += _n
NCOLS = _c

CONSTS = [("ident", 128), ("ones", 128), ("blk", 128), ("ml_mask", 128), ("swa_rest", 256),
          ("swa_first", 256), ("hg_mask", 128), ("hg_reset", 512), ("sel", 512)]
CST = {}
_c = 0
for _name, _n in CONSTS:
    CST[_name] = _c
    _c += _n
NCONST = _c
NKEPT = CST["hg_reset"]


NORMS = ["z1", "q1", "ffn1", "final", "z2", "pm", "q2", "px", "ffn2", "pf"]
OPERANDS = ["z1", "q1", "ffn1", "z2", "q2", "ffn2"]
KV0 = {"1": 0, "2": 2 * KT}
XA0 = {"1": 0, "2": NCH}
STD0 = {"cf": (0, 0), "ln": (2, 2), "hn": (3, 4)}
FF0 = {"ffn1": 0, "ffn2": FT}


class Chain:

    def __init__(self, eng, sem):
        self.eng, self.sem, self.n, self.turn = eng, sem, 0, 0

    def link(self, ins):
        ins.then_inc(self.sem, 1)
        self.n += 1
        self.eng.wait_ge(self.sem, self.turn + self.n)

    def enter(self, i, first, per):
        self.turn, self.start, self.per = (i - first) * per, self.n, per

    def leave(self, trips):
        assert self.n - self.start == self.per, self.n - self.start
        self.n, self.turn = self.start + trips * self.per, 0


def program(nc, ap):
    ctx = ExitStack()
    with ctx:
        semaphores = {}

        def s(name):
            if name not in semaphores:
                semaphores[name] = ctx.enter_context(nc.semaphore(name))
            return semaphores[name]

        def norm(what, name, n, per=KT):
            return s(what), per * NORMS.index(name) + n

        def operand_count(what, name, n):
            if name in ("m1", "m2"):
                return s("mem_lo"), KT * (name == "m2") + n
            return s(what), KT * OPERANDS.index(name) + n

        arena_cols = 53200
        ctx.enter_context(nc.sbuf_tensor("arena", [P, arena_cols], F32))
        first_byte = nc.sbuf_base - 4 * arena_cols
        place_of = {}
        used = [0]

        def place(name, shape, dt=F32, over=None, offset=0):
            size = -(-int(np.prod(shape[1:])) // 8) * 8
            if over is None:
                start = used[0]
                used[0] += size
            else:
                start = place_of[over] + offset
            place_of[name] = start
            assert used[0] <= arena_cols, used
            return nc.alloc_sbuf_tensor_at(name, shape, dt, offset=first_byte + 4 * start)

        act_hi = place("act_hi", [P, KT, T], F32R)
        act_lo = place("act_lo", [P, KT, T], F32R)
        w_raw = place("w_raw", [P, 2, KT * P])
        w_hi = place("w_hi", [P, 2, KT * P], F32R)
        w_lo = place("w_lo", [P, 2, KT * P], F32R)
        W = place("work", [P, FT, T])
        TMP = place("tmp", [P, 4, T])
        rstd = place("rstd", [P, T])
        cst = place("cst", [P, NKEPT])
        phase = place("phase", [P, 512])
        cols = place("cols", [P, NCOLS])
        small = place("small", [P, 64])
        epsc = place("epsc", [P, 2])
        g_hi = place("g_hi", [P, 2, T], F32R, over="work", offset=18 * T)
        g_lo = place("g_lo", [P, 2, T], F32R, over="work", offset=20 * T)
        m_hi = place("m_hi", [P, KT, MEM], F32R, over="work", offset=16 * T)
        m_lo = place("m_lo", [P, KT, MEM], F32R, over="work", offset=18 * T)
        hi_as_f32 = act_hi[:, :, :].bitcast(F32)
        lo_free = place("lo_free", [P, 4, T], over="act_lo", offset=4 * T)
        hi_free = place("hi_free", [P, 4, T], over="act_hi", offset=4 * T)

        G = ctx.enter_context(nc.psum_tensor("products", [P, 2, T], F32))
        N = ctx.enter_context(nc.psum_tensor("others", [P, 2, T], F32))

        def const(name, n=None):
            c = CST[name]
            return cst[:, c:c + (n or 128)]

        keys = W[:, 20:22, :].rearrange("p a t -> p (a t)").rearrange("p (k m) -> p k m", m=MEM)
        values = W[:, 8:10, :]
        queries = W[:, 10:18, :]

        def col(name, k):
            return cols[:, COL[name] + k:COL[name] + k + 1]

        Wc = W[:, :, :].rearrange("p k (c t) -> p k c t", t=CH)
        hic = act_hi[:, :, :].rearrange("p k (c t) -> p k c t", t=CH)
        loc = act_lo[:, :, :].rearrange("p k (c t) -> p k c t", t=CH)
        hicf = hi_as_f32.rearrange("p k (c t) -> p k c t", t=CH)
        Tc = TMP[:, :, :].rearrange("p k (c t) -> p k c t", t=CH)
        flat = W[:, :, :].rearrange("p k t -> p (k t)")
        tflat = TMP[:, :, :].rearrange("p k t -> p (k t)")
        sq = [TMP[:, 0, :], TMP[:, 1, :]]
        ssum, root = TMP[:, 2, :], TMP[:, 3, :]
        ident, ones, blk = const("ident"), const("ones"), const("blk")

        rowA, rowF, rowE, rowM = (TMP[:, n, :] for n in range(4))
        wq, wk, wv, wsT = (flat[:, 20 * T + 512 * n:20 * T + 512 * n + 512] for n in range(4))
        ml = lambda n, k=1: (flat[:, 512 * n:512 * (n + k)] if n < 8 else
                             flat[:, 8 * T + 512 * (n - 8):8 * T + 512 * (n - 8 + k)])
        heads = lambda v: v.rearrange("p (h t) -> p h t", h=NH)
        xcs, xvs, qT, qw, kT, kw, Wt, Pm = (heads(ml(n)) for n in range(8))
        winter, emm, Et, dn = (heads(ml(8 + n)) for n in range(4))
        vt = ml(12, 2).rearrange("p (h t) -> p h t", h=NH)
        Cst = ml(14, 2).rearrange("p (h t) -> p h t", h=NH)
        sel = phase[:, :].rearrange("p (h t) -> p h t", h=NH)
        bsb = place("bsb", [P, 2 * P])
        arow = place("arow", [P, P])
        bsv = bsb[:, :].rearrange("p (k t) -> p k t", k=2)
        Gf = G[:, :, :].rearrange("p a t -> p (a t)")
        Nf = N[:, :, :].rearrange("p a t -> p (a t)")
        Gb = [heads(Gf[:, 512 * n:512 * n + 512]) for n in range(4)]
        Nb = [heads(Nf[:, 512 * n:512 * n + 512]) for n in range(4)]

        hg_names = "b D1 Q1 K1 Eb0 K2 Q20 S lf vs vtok k2tok AT Eb1 Q21".split()

        def hg(names):
            out = []
            for name in names.split():
                n = hg_names.index(name)
                v = (tflat[:, 512 * n:512 * n + 512] if n < 8 else
                     hi_free[:, n // 2 - 3, 512 * (n % 2):512 * (n % 2) + 512] if n < 12 else
                     rstd[:, 512 * (n - 12):512 * (n - 11)] if n < 14 else hi_free[:, 3, 512:1024])
                out.append(heads(v))
            return out

        sw_q = hi_free[:, 0, 0:512].rearrange("p (k t) -> p k t", k=4)
        sw_kv = hi_free[:, 0, 512:1024].rearrange("p (a t) -> p a t", a=2)
        sw_v = hi_free[:, 3, 0:256]
        sw_pT = lo_free[:, 0:2, :].rearrange("p a t -> p (a t)")
        sw_pr = lo_free[:, 2:4, :].rearrange("p a t -> p (a t)")

        block = ctx.enter_context(nc.Block())

        @block.sync
        def _(sp):
            def load(b, slot):
                sp.dma_start(w_raw[:, slot, :], ap["wstream"][b]).then_inc(s(f"weights_loaded{slot}"), 16)

            load(0, 0)
            load(1, 1)
            with sp.Fori(2, NBLOCKS - 1, 2) as b:
                for slot in range(2):
                    sp.wait_ge(s("weights_split"), b + slot - 1)
                    load(b + slot, slot)
            if NBLOCKS % 2:
                sp.wait_ge(s("weights_split"), NBLOCKS - 2)
                load(NBLOCKS - 1, 0)

        @block.gpsimd
        def _(pool):
            pool.memset(small[:, 63:64], 0.0).then_inc(s("pool_zero"), 1)
            pool.wait_ge(s("pool_zero"), 1)
            zeros = small[:, 63:64].to_broadcast([P, KT * P])

            def split(b, turn, slot, low_only=False):
                if low_only:
                    pool.wait_ge(s("kv_high"), low_only(b) + 1)
                else:
                    pool.wait_ge(s(f"weights_loaded{slot}"), 16 * (turn + 1))
                    if not isinstance(b, int) or b >= 2:
                        pool.wait_ge(s("product_quarters"), 4 * (b - 1))
                    pool.tensor_tensor(w_hi[:, slot, :], w_raw[:, slot, :], zeros, ALU.add)\
                        .then_inc(s("weights_high"), 1)
                    pool.wait_ge(s("weights_high"), b + (1 - made_elsewhere[0]))
                pool.tensor_tensor(w_lo[:, slot, :], w_raw[:, slot, :], w_hi[:, slot, :].bitcast(F32),
                                   ALU.subtract).then_inc(s("weights_split"), 1)

            made_elsewhere = [0]

            def split_blocks(first, end, low_only=False):
                with pool.Fori(0, (end - first) // 2) as i:
                    for j in range(2):
                        split(i * 2 + (first + j), i + (first + j) // 2, (first + j) % 2, low_only)
                if (end - first) % 2:
                    split(end - 1, (end - 1) // 2, (end - 1) % 2, low_only)
                if low_only:
                    made_elsewhere[0] += end - first

            split(0, 0, 0)
            split(1, 0, 1)
            split_blocks(2, BLOCK0["k1"])
            split_blocks(BLOCK0["k1"], BLOCK0["q1"], lambda b: b - (BLOCK0["k1"] - KV0["1"]))
            split_blocks(BLOCK0["q1"], BLOCK0["k2"])
            split_blocks(BLOCK0["k2"], BLOCK0["q2"], lambda b: b - (BLOCK0["k2"] - KV0["2"]))
            split_blocks(BLOCK0["q2"], NBLOCKS)

        @block.tensor
        def _(pe):
            def room(p):
                if not isinstance(p, int) or p >= 2:
                    pe.wait_ge(s("evacuated"), p - 1)

            def project(b, p, ws, ps, hi, lo, width=T, ready=None):
                pe.wait_ge(s("weights_split"), b + 1)
                room(p)
                n = min(width, HALF)
                for k in range(KT):
                    if ready:
                        pe.wait_ge(*operand_count("operand_lo", ready, k + 1))
                    w = slice(k * P, (k + 1) * P)
                    for h in range(width // n):
                        c = slice(h * n, (h + 1) * n)
                        for i, (a, x) in enumerate(((w_hi, hi), (w_hi, lo), (w_lo, hi))):
                            last = pe.matmul(G[:, ps, c], a[:, ws, w], x[:, k, c],
                                             start=(k == 0 and i == 0), stop=(k == KT - 1 and i == 2))
                last.then_inc(s("product_quarters"), 4)

            def gemm(name, n, ready, hi=act_hi, lo=act_lo, width=T, after_two=None):
                b, p = BLOCK0[name], PROD0[name]
                peel = 2 + n % 2
                for j in range(peel):
                    project(b + j, p + j, (b + j) % 2, (p + j) % 2, hi, lo, width, ready if j == 0 else None)
                    if j == 1 and after_two:
                        after_two()
                with pe.Fori(peel, n, 2) as i:
                    for j in range(2):
                        project(i + (b + j), i + (p + j), (b + peel + j) % 2, (p + peel + j) % 2, hi, lo, width)

            def value_gemm(name):
                b, p = BLOCK0[name], PROD0[name]
                for g in range(2):
                    ps = (p + g) % 2
                    room(p + g)
                    for q in range(4):
                        ws = (b + 4 * g + q) % 2
                        pe.wait_ge(s("weights_split"), b + 4 * g + q + 1)
                        for m in range(2):
                            for k in range(2):
                                for n, (a, x) in enumerate(((m_hi, w_hi), (m_lo, w_hi), (m_hi, w_lo))):
                                    last = pe.matmul(G[:, ps, m * HALF:(m + 1) * HALF],
                                                     a[:, 2 * q + k, m * P:(m + 1) * P],
                                                     x[:, ws, k * HALF:(k + 1) * HALF],
                                                     start=(q == 0 and k == 0 and n == 0),
                                                     stop=(q == 3 and k == 1 and n == 2))
                        last.then_inc(s("product_quarters"), 4)

            def token_sums(name, wait, count, src=None):
                if name in NORMS:
                    pe.wait_ge(*norm("squares_summed", name, KT))
                else:
                    pe.wait_ge(s(wait), count)
                for h in range(2):
                    c = slice(h * HALF, (h + 1) * HALF)
                    last = pe.matmul(N[:, 0, c], ones, (src if src is not None else ssum)[:, c], start=True, stop=True)
                last.then_inc(s("token_sums" if name in NORMS else name + "_token_sums"), 1)

            def norm_sums(name):
                return lambda: token_sums(name, None, None)

            def standardize(name, jobs, ready):
                done = 0
                for n, (m, tiles) in enumerate(jobs):
                    pe.wait_ge(s(ready[0]), ready[1][n])
                    for h in range(2):
                        c = slice(h * HALF, (h + 1) * HALF)
                        for t, tile in enumerate(tiles):
                            last = pe.matmul(N[:, 0, c], m, tile[:, c], start=(t == 0), stop=(t == len(tiles) - 1))
                    last.then_inc(s("std_mean"), 1)
                    done += len(tiles)
                    pe.wait_ge(s("std_sq"), STD0[name][1] + done)
                    for h in range(2):
                        c = slice(h * HALF, (h + 1) * HALF)
                        for t in range(len(tiles)):
                            last = pe.matmul(N[:, 1, c], m, W[:, t, c], start=(t == 0), stop=(t == len(tiles) - 1))
                    last.then_inc(s("std_var"), 1)

            def gmlp():
                pe.wait_ge(s("ln_out"), 2)
                pe.wait_ge(s("evacuated"), PROD0["out1"])
                for c in range(NCH):
                    for t in range(2):
                        last = pe.transpose(Gf[:, (2 * c + t) * P:(2 * c + t + 1) * P], W[:, 10 + t, c * CH:(c + 1) * CH], ident)
                last.then_inc(s("gm_turned"), 1)
                pe.wait_ge(s("gm_tokens"), 2)
                pe.wait_ge(s("ws_masked"), 1)
                for c in range(NCH):
                    for h in range(NH):
                        r = slice(64 * (h % 2), 64 * (h % 2) + 64)
                        last = pe.matmul(Nf[r, (h // 2) * T + c * CH:(h // 2) * T + (c + 1) * CH],
                                         flat[:, 2 * T + 256 * c + 64 * h:2 * T + 256 * c + 64 * h + 64],
                                         wsT[:, h * P:(h + 1) * P], start=True, stop=True)
                last.then_inc(s("gm_mixed"), 1)

            def mlstm():
                pe.wait_ge(s("ml_rows"), 1)
                pe.wait_ge(s("mix_in"), 80)
                pe.wait_ge(s("phase_in"), 16)
                pe.wait_ge(s("ml_init"), 2)

                def spread(c):
                    pe.wait_ge(s("ml_stage"), 3 * c + 3)
                    for n, row in ((2, rowF), (3, rowE)):
                        rc = row[0:NH, :].rearrange("p (c t) -> p c t", t=CH)
                        for h in range(NH):
                            pe.matmul(Nb[n][:, h, :], sel[0:NH, h, :], rc[:, c, :], start=True, stop=True)
                    rc = rowM[0:NH, :].rearrange("p (c t) -> p c t", t=CH)
                    for h in range(NH):
                        pe.matmul(Nb[0][:, h, :], arow[0:NH, :], sel[0:NH, h, :], start=True, stop=False)
                        last = pe.matmul(Nb[0][:, h, :], sel[0:NH, h, :], rc[:, c, :], start=False, stop=True)
                    last.then_inc(s("ml_spread"), 1)

                def chunk(c, ahead=True):
                    pe.wait_ge(s("ml_h"), c + 1)
                    for n, a in enumerate((wq, wk)):
                        for h in range(NH):
                            last = pe.matmul(Gb[n][:, h, :], heads(a)[:, h, :], xvs[:, h, :], start=True, stop=True)
                    last.then_inc(s("ml_proj"), 1)
                    pe.wait_ge(s("ml_kept"), c + 1)
                    for n, (a, x) in enumerate(((xvs, wk), (xcs, wv))):
                        for h in range(NH):
                            last = pe.matmul(Gb[2 + n][:, h, :], a[:, h, :], heads(x)[:, h, :], start=True, stop=True)
                    last.then_inc(s("ml_proj"), 1)
                    pe.wait_ge(s("ml_qkv"), 3 * c + 2)
                    for h in range(NH):
                        last = pe.matmul(Nb[1][:, h, :], kT[:, h, :], qT[:, h, :], start=True, stop=True)
                    last.then_inc(s("ml_scores"), 1)
                    pe.wait_ge(s("ml_qkv"), 3 * c + 3)
                    pe.wait_ge(s("ml_weighted"), 3 * c + 3)
                    for h in range(NH):
                        pe.matmul(Gb[0][:, h, :], vt[:, h, 0:P], Pm[:, h, :], start=True, stop=False)
                        pe.matmul(Gb[0][:, h, :], Cst[:, h, 0:P], qw[:, h, :], start=False, stop=True)
                    for h in range(NH):
                        pe.matmul(Gb[1][:, h, :], ones, Pm[:, h, :], start=True, stop=False)
                        last = pe.matmul(Gb[1][:, h, :], Cst[:, h, P:2 * P], qw[:, h, :], start=False, stop=True)
                    last.then_inc(s("ml_num"), 1)
                    for h in range(NH):
                        last = pe.matmul(Gf[:, T + 256 * h:T + 256 * h + 256], kw[:, h, :], vt[:, h, :], start=True, stop=True)
                    last.then_inc(s("ml_update"), 1)
                    if ahead:
                        spread(c + 1)

                spread(0)
                with pe.Fori(0, NCH - 1) as c:
                    chunk(c)
                chunk(NCH - 1, False)

            def memory_sums(x):
                def run():
                    pe.wait_ge(s(x + "_mem_sq"), 1)
                    for k in range(KT):
                        last = pe.matmul(N[:, 1, 0:MEM], ones, flat[:, 12 * T + k * MEM:12 * T + (k + 1) * MEM],
                                         start=(k == 0), stop=(k == KT - 1))
                    last.then_inc(s(x + "_mem_sums"), 1)
                return run

            def cross(x):
                qs = [TMP[:, n, :].rearrange("p (k t) -> p k t", k=KT) for n in (0, 3)]
                score_slots = [Nf[:, 0:T], G[:, 1, :]]
                p_, pT = TMP[:, 1, :], TMP[:, 2, :].rearrange("p (k t) -> p k t", k=KT)

                def scores(c, slot):
                    pe.wait_ge(s("xa_q_staged"), c + 1 + XA0[x])
                    for h in range(NH):
                        for k in range(2):
                            last = pe.matmul(score_slots[slot][:, MEM * h:MEM * (h + 1)], qs[slot][:, 2 * h + k, :],
                                             keys[:, 2 * h + k, :], start=(k == 0), stop=(k == 1))
                    last.then_inc(s("xa_scores"), 1)

                def chunk(c, slot, ahead=True):
                    pe.wait_ge(s("xa_probs"), c + 1 + XA0[x])
                    for n in range(8):
                        last = pe.transpose(N[:, 1, n * P:(n + 1) * P], p_[:, n * P:(n + 1) * P], ident)
                    last.then_inc(s("xa_turned"), 1)
                    if ahead:
                        scores(c + 2, slot)
                    pe.wait_ge(s("xa_pT"), c + 1 + XA0[x])
                    pe.wait_ge(s("xa_o_lo"), c + 1 + XA0[x])
                    for k in range(KT):
                        for m in range(2):
                            last = pe.matmul(G[:, 0, k * P:(k + 1) * P], values[:, m, k * P:(k + 1) * P],
                                             pT[:, 2 * (k // 2) + m, :], start=(m == 0), stop=(m == 1))
                    last.then_inc(s("xa_out"), 1)

                pe.wait_ge(s("evacuated"), PROD0["xo" + x])
                scores(0, 0)
                scores(1, 1)
                with pe.Fori(0, (NCH - 2) // 2) as i:
                    for n in range(2):
                        chunk(i * 2 + n, n)
                chunk(NCH - 2, 0, False)
                chunk(NCH - 1, 1, False)

            def ffn(name):
                b, p = BLOCK0[name], PROD0[name]

                def up(b, p, par, after_two=None, ready=None):
                    for j in range(4):
                        project(b + j, p + j, (par[0] + j) % 2, (par[1] + j) % 2, act_hi, act_lo, T, ready if j == 0 else None)
                        if j == 1 and after_two:
                            after_two()

                def down(b, p, par, c):
                    for j in range(2):
                        pe.wait_ge(s("weights_split"), b + (j + 1))
                        for o in range(4):
                            room(p + (4 * j + o))
                            if j == 0 and o == 0:
                                pe.wait_ge(s("ff_g_lo"), 2 * c + 2 + FF0[name])
                            ws, ps = (par[0] + j) % 2, (par[1] + o) % 2
                            for k in range(2):
                                w = slice((2 * o + k) * P, (2 * o + k + 1) * P)
                                for h in range(2):
                                    t = slice(h * HALF, (h + 1) * HALF)
                                    for i, (a, x) in enumerate(((w_hi, g_hi), (w_hi, g_lo), (w_lo, g_hi))):
                                        last = pe.matmul(G[:, ps, t], a[:, ws, w], x[:, k, t],
                                                         start=(k == 0 and i == 0), stop=(k == 1 and i == 2))
                            last.then_inc(s("product_quarters"), 1)

                up(b, p, (b, p), norm_sums(name), name)
                with pe.Fori(1, FC) as c:
                    up(c * 6 + (b - 2), c * 12 + (p - 8), (b, p))
                    down(c * 6 + (b + 2), c * 12 + (p - 4), (b, p), c - 1)
                down(b + 6 * FC - 2, p + 12 * FC - 8, (b, p), FC - 1)

            def mixer2():
                Q1, K1, K2, vs, AT, vtok, k2tok, S, *Q2 = hg("Q1 K1 K2 vs AT vtok k2tok S Q20 Q21")
                pe.wait_ge(s("evacuated"), PROD0["out2"])
                pe.wait_ge(s("hg_init"), 1)

                def scores(c):
                    pe.wait_ge(s("sw_staged"), 4 * c + 4)
                    pe.wait_ge(s("hg_kept"), c + 1)
                    for g in range(2):
                        for i in range(4):
                            n = 4 * g + i
                            last = pe.matmul(Nf[:, n * 256:(n + 1) * 256], sw_q[64 * g:64 * g + 64, i, :],
                                             sw_kv[64 * g:64 * g + 64, 0, :], start=True, stop=True)
                        last.then_inc(s("sw_scores"), 1)

                def turn_values():
                    for n in range(2):
                        last = pe.transpose(Gb[3][:, n, :], sw_kv[:, 1, n * P:(n + 1) * P], ident)
                    last.then_inc(s("sw_v_turned"), 1)

                def turn_hgrn(c):
                    pe.wait_ge(s("hg_v"), c + 1)
                    for h in range(NH):
                        pe.transpose(Gb[1][:, h, :], vs[:, h, :], ident)
                    pe.wait_ge(s("hg_qk"), 4 * c + 4)
                    for h in range(NH):
                        last = pe.transpose(Gb[2][:, h, :], K2[:, h, :], ident)
                    last.then_inc(s("hg_turned"), 1)

                def chunk(c, odd, ahead=True):
                    pe.wait_ge(s("sw_o_lo"), c + 1)
                    for h in range(NH):
                        last = pe.matmul(Gb[0][:, h, :], K1[:, h, :], Q1[:, h, :], start=True, stop=True)
                    last.then_inc(s("hg_scores"), 1)
                    pe.wait_ge(s("sw_negmax"), 2 * c + 2)
                    pe.wait_ge(s("hg_masked"), c + 1)
                    pe.wait_ge(s("hg_tokens"), 2 * c + 2)
                    for h in range(NH):
                        pe.matmul(Nb[1][:, h, :], vtok[:, h, :], AT[:, h, :], start=(h == 0), stop=False, skip_group_check=True)

                    def inter(sub):
                        r = slice(64 * sub, 64 * sub + 64)
                        for h in range(NH):
                            pe.matmul(Nb[1][:, h, r], S[:, h, :], Q2[odd][:, h, r], start=False, stop=(sub == 1 and h == 3),
                                      skip_group_check=True)
                        for h in range(NH):
                            last = pe.matmul(Nb[2 + sub][:, h, :], k2tok[r, h, :], vtok[r, h, :], start=True, stop=True)
                        last.then_inc(s("hg_update"), 1)

                    inter(0)
                    pe.wait_ge(s("sw_v"), c + 1)
                    for g in range(2):
                        pe.wait_ge(s("sw_probs"), 2 * c + (g + 1))
                        for n in range(8 * g, 8 * g + 8):
                            last = pe.transpose(Gf[:, n * P:(n + 1) * P], sw_pr[:, n * P:(n + 1) * P], ident)
                        last.then_inc(s("sw_turned"), 1)
                    pe.wait_ge(s("hg_S"), 2 * c + 2)
                    inter(1)
                    pe.wait_ge(s("hg_S"), 2 * c + 3)
                    pe.wait_ge(s("sw_pT"), 2 * c + 2)
                    for g in range(2):
                        for i in range(4):
                            n = 4 * g + i
                            for m in range(2):
                                last = pe.matmul(Gf[64 * g:64 * g + 64, i * P:(i + 1) * P],
                                                 sw_v[:, m * P + 64 * g:m * P + 64 * g + 64],
                                                 sw_pT[:, (2 * n + m) * P:(2 * n + m + 1) * P], start=(m == 0), stop=(m == 1))
                    last.then_inc(s("sw_pv"), 1)
                    if ahead:
                        scores(c + 1)
                        turn_values()
                        turn_hgrn(c + 1)

                scores(0)
                turn_values()
                turn_hgrn(0)
                chunk(0, 0)
                with pe.Fori(0, NCH // 2 - 1) as i:
                    for n in (1, 2):
                        chunk(i * 2 + n, n % 2)
                chunk(NCH - 1, 1, False)

            pe.wait_ge(s("consts"), 32)
            gemm("z1", 17, "z1", after_two=norm_sums("z1"))
            standardize("cf", [(blk, [W[:, 2, :]]), (blk, [W[:, 3, :]])], ("cb_done", [1, 2]))
            standardize("ln", [(ones, [W[:, 10, :], W[:, 11, :]])], ("gelus", [4]))
            gmlp()
            mlstm()
            standardize("hn", [(ones, [W[:, 4 + n, :]]) for n in range(4)], ("ml_h", [NCH + 1] * 4))
            pe.wait_ge(s("y1_lo"), 8)
            gemm("out1", 8, None, after_two=memory_sums("1"))

            def attention(x):
                gemm("k" + x, 8, "m" + x, m_hi, m_lo, MEM)
                value_gemm("v" + x)
                gemm("q" + x, 8, "q" + x, after_two=norm_sums("q" + x))
                cross(x)
                pe.wait_ge(s("xa_o_lo"), NCH + 1 + XA0[x])
                gemm("xo" + x, 8, None)

            attention("1")
            ffn("ffn1")
            norm_sums("final")()
            gemm("z2", 22, "z2", after_two=norm_sums("z2"))
            mixer2()
            pe.wait_ge(s("sw_o_lo"), NCH + 1)
            pe.wait_ge(s("hg_kept"), NCH + 1)
            for n in range(4):
                token_sums("hr", "hr_sq", n + 1, W[:, 16, :])
            pe.wait_ge(s("y2_lo"), 4)
            pe.wait_ge(s("sw_o_lo"), NCH + 1)
            gemm("out2", 8, None, after_two=memory_sums("2"))
            norm_sums("pm")()
            attention("2")
            norm_sums("px")()
            ffn("ffn2")
            norm_sums("pf")()

        @block.scalar
        def _(act):
            chain = Chain(act, s("act_chain"))

            def apart():
                act.wait_ge(s("consts"), 32)

            def squares(name, src, ready, n=KT):
                for k in range(n):
                    act.wait_ge(*ready(k))
                    if k >= 2:
                        act.wait_ge(*norm("squares_summed", name, k - 1))
                    act.activation(sq[k % 2], src(k), ACT.Square).then_inc(s("squares"), 1)

            def roots(name, n=1, scale=1.0 / D, out=None):
                act.wait_ge(*(norm("token_sums", name, 1, 1) if name in NORMS else (s(name + "_token_sums"), n)))
                log = root if out is None else out
                chain.link(act.activation(log, N[:, 0, :], ACT.Ln, bias=epsc[:, 0:1], scale=scale))
                act.activation(rstd[:, :] if out is None else out, log, ACT.Exp, scale=-0.5)\
                   .then_inc(s("roots" if name in NORMS else name + "_root"), 1)

            def weights_high(x, n):
                b = BLOCK0["k" + x] + n
                act.wait_ge(s(f"weights_loaded{b % 2}"), 16 * (b // 2 + 1))
                act.wait_ge(s("product_quarters"), 4 * (b - 1))
                act.activation(w_hi[:, b % 2, :], w_raw[:, b % 2, :], ACT.Copy).then_inc(s("kv_high"), 1)

            def split_high(name, src, gain, ready=None, beside=None):
                for k in range(KT):
                    if beside:
                        beside(k)
                    if ready:
                        act.wait_ge(*ready(k))
                    act.activation(act_hi[:, k, :], src(k), ACT.Identity, scale=col(gain, k)).then_inc(s("operand_hi"), 1)

            def standardize(name, jobs, div, affine):
                done = 0
                for n, tiles in enumerate(jobs):
                    for t, tile in enumerate(tiles):
                        act.wait_ge(s("std_centred"), STD0[name][1] + done + t + 1)
                        act.activation(W[:, t, :], tile, ACT.Square).then_inc(s("std_sq"), 1)
                    act.wait_ge(s("std_var"), STD0[name][0] + n + 1)
                    chain.link(act.activation(W[:, 0, :], N[:, 1, :], ACT.Ln, bias=epsc[:, 1:2], scale=1.0 / div))
                    act.activation(W[:, 0, :], W[:, 0, :], ACT.Exp, scale=-0.5).then_inc(s("std_root"), 1)
                    for t, tile in enumerate(tiles):
                        act.wait_ge(s("std_scaled"), STD0[name][1] + done + t + 1)
                        affine(n, t, tile).then_inc(s(name + "_out"), 1)
                    done += len(tiles)

            def load(dst, src, name):
                act.dma_start(dst, src).then_inc(s(name), 16)

            load(cst[:, :], ap["consts"][:, 0:NKEPT], "consts")
            load(cols[:, :], ap["cols"], "consts")
            for k in range(KT):
                load(W[:, k, :], ap["xT"][:, k, :], f"x_in{k}")
            load(phase[:, :], ap["consts"][:, CST["sel"]:CST["sel"] + 512], "phase_in")
            load(wq, ap["w_q"], "mix_in")
            load(wk, ap["w_k"], "mix_in")
            load(wv, ap["w_v"], "mix_in")
            load(wsT, ap["w_sT"], "mix_in")
            load(bsb[:, :], ap["b_s"], "mix_in")
            act.wait_ge(s("consts"), 32)
            act.wait_ge(s("eps"), 2)
            for k in range(KT):
                act.wait_ge(s(f"x_in{k}"), 16)
                act.activation(act_hi[:, k, :], W[:, k, :], ACT.Identity, scale=col("mix1", k)).then_inc(s("operand_hi"), 1)
                if k >= 2:
                    act.wait_ge(*norm("squares_summed", "z1", k - 1))
                act.activation(sq[k % 2], W[:, k, :], ACT.Square).then_inc(s("squares"), 1)
            roots("z1")
            E0 = PROD0["z1"]
            act.wait_ge(s("row_forget"), 1)
            act.activation(rowE[0:NH, :], rowF[0:NH, :], ACT.Abs).then_inc(s("row_abs"), 1)
            act.wait_ge(s("row_abs"), 1)
            chain.link(act.activation(rowE[0:NH, :], rowE[0:NH, :], ACT.Exp, scale=-1.0))
            act.activation(rowE[0:NH, :], rowE[0:NH, :], ACT.Ln, bias=1.0).then_inc(s("row_log"), 1)
            for n in range(2):
                act.wait_ge(s("evacuated"), E0 + 4 + n)
                act.activation(W[:, 2 + n, :], W[:, 2 + n, :], ACT.Sigmoid).then_inc(s("cf_gate"), 1)
            for n in range(4):
                act.wait_ge(s("cc_done"), n + 1)
                act.activation(W[:, 16 + n, :], W[:, 16 + n, :], ACT.Silu).then_inc(s("xconv"), 1)
            for n in range(4):
                act.wait_ge(s("evacuated"), E0 + 10 + n)
                act.activation(W[:, 8 + n, :], W[:, 8 + n, :], ACT.Gelu).then_inc(s("gelus"), 1)
            for n in range(4):
                act.wait_ge(s("evacuated"), E0 + 14 + n)
                act.activation(W[:, 12 + n, :], W[:, 12 + n, :], ACT.Sigmoid).then_inc(s("ogate"), 1)

            def cf_affine(n, t, tile):
                return act.activation(tile, tile, ACT.Silu, scale=col("gnb_g", n), bias=col("gnb_b", n))

            standardize("cf", [[W[:, 2, :]], [W[:, 3, :]]], 64, cf_affine)
            act.wait_ge(s("evacuated"), PROD0["out1"])
            act.wait_ge(s("cf_out"), 2)
            for n in range(2):
                act.activation(act_hi[:, 2 + n, :], W[:, 2 + n, :], ACT.Copy).then_inc(s("y1_hi"), 1)

            def ln_affine(n, t, tile):
                return act.activation(tile, tile, ACT.Identity, scale=col("lna_g", t), bias=col("lna_b", t))

            standardize("ln", [[W[:, 10, :], W[:, 11, :]]], 256, ln_affine)
            act.wait_ge(s("y1_lo"), 2)
            act.wait_ge(s("gm_turned"), 1)
            for n in range(2):
                act.activation(W[:, 2 + n, :], G[:, n, :], ACT.Copy).then_inc(s("gm_tokens"), 1)
            for n in range(2):
                act.wait_ge(s("gm_y"), n + 1)
                act.activation(act_hi[:, n, :], W[:, n, :], ACT.Copy).then_inc(s("y1_hi"), 1)

            act.wait_ge(s("ml_free"), 1)
            act.wait_ge(s("xconv"), 4)
            rowAc = rowA[0:NH, :].rearrange("p (c t) -> p c t", t=CH)

            def stage(c):
                act.activation(xvs, Wc[:, 16:20, c, :], ACT.Copy).then_inc(s("ml_stage"), 1)
                act.activation(xcs, Wc[:, 4:8, c, :], ACT.Copy).then_inc(s("ml_stage"), 1)
                act.activation(arow[0:NH, :], rowAc[:, c, :], ACT.Copy).then_inc(s("ml_stage"), 1)

            def mlstm(c, ahead=True):
                act.wait_ge(s("ml_kept"), c + 1)
                act.wait_ge(s("ml_spread"), c + 1)
                act.activation(winter, Nb[2], ACT.Exp).then_inc(s("ml_exp"), 1)
                act.activation(emm, Nb[3], ACT.Exp).then_inc(s("ml_exp"), 1)
                act.wait_ge(s("ml_proj"), 2 * c + 1)
                act.activation(qT, Gb[0], ACT.Copy, scale=float(P) ** -0.5).then_inc(s("ml_qkv"), 1)
                act.activation(kT, Gb[1], ACT.Copy).then_inc(s("ml_qkv"), 1)
                act.wait_ge(s("ml_bounded"), c + 1)
                act.activation(Wt, Et, ACT.Exp).then_inc(s("ml_exp"), 1)
                act.wait_ge(s("ml_proj"), 2 * c + 2)
                act.activation(vt[:, :, 0:P], Gb[3], ACT.Copy).then_inc(s("ml_qkv"), 1)
                if ahead:
                    stage(c + 1)
                act.wait_ge(s("ml_num"), c + 1)
                act.activation(dn, Gb[1], ACT.Abs).then_inc(s("ml_den"), 1)

            stage(0)
            with act.Fori(0, NCH - 1) as c:
                mlstm(c)
            mlstm(NCH - 1, False)

            def hn_affine(n, t, tile):
                return act.activation(tile, tile, ACT.Identity, scale=col("hn_g", n))

            standardize("hn", [[W[:, 4 + n, :]] for n in range(4)], P, hn_affine)
            for n in range(4):
                act.wait_ge(s("ml_y"), n + 1)
                act.activation(act_hi[:, 4 + n, :], W[:, 4 + n, :], ACT.Copy).then_inc(s("y1_hi"), 1)
            act.wait_ge(s("y1_lo"), 8)

            def memory(x):
                mem = flat[:, 20 * T:22 * T]
                act.wait_ge(s(x + "_mem_in"), 16)
                act.activation(flat[:, 12 * T:14 * T], mem, ACT.Square).then_inc(s(x + "_mem_sq"), 1)
                act.wait_ge(s(x + "_mem_sums"), 1)
                chain.link(act.activation(W[:, 14, 0:MEM], N[:, 1, 0:MEM], ACT.Ln, bias=epsc[:, 0:1], scale=1.0 / D))
                act.activation(W[:, 14, 0:MEM], W[:, 14, 0:MEM], ACT.Exp, scale=-0.5).then_inc(s(x + "_mem_root"), 1)
                act.wait_ge(s(x + "_mem_scaled"), 1)
                for k in range(KT):
                    act.activation(m_hi[:, k, :], mem[:, k * MEM:(k + 1) * MEM], ACT.Identity, scale=col("mem" + x, k))\
                       .then_inc(s(x + "_mem_hi"), 1)

            def cross(x):
                qs = [TMP[:, n, :].rearrange("p (k t) -> p k t", k=KT) for n in (0, 3)]
                score_slots = [Nf[:, 0:T], G[:, 1, :]]
                pr, pT = TMP[:, 1, :], TMP[:, 2, :]
                queries_c = queries.rearrange("p k (c t) -> p k c t", t=CH)

                def stage(c, slot):
                    act.activation(qs[slot], queries_c[:, :, c, :], ACT.Copy).then_inc(s("xa_q_staged"), 1)

                def exps(c, slot):
                    act.wait_ge(s("xa_negmax"), c + 1 + XA0[x])
                    for h in range(NH):
                        last = act.activation(pr[:, h * MEM:(h + 1) * MEM], score_slots[slot][:, h * MEM:(h + 1) * MEM],
                                              ACT.Exp, bias=small[:, 4 + 12 * slot + h:5 + 12 * slot + h],
                                              accum_out=small[:, 8 + h:9 + h])
                    last.then_inc(s("xa_exps"), 1)

                def chunk(c, slot, ahead=3):
                    act.wait_ge(s("xa_turned"), c + 1 + XA0[x])
                    act.activation(pT, N[:, 1, :], ACT.Copy).then_inc(s("xa_pT"), 1)
                    if ahead:
                        exps(c + 1, 1 - slot)
                    if ahead == 3:
                        stage(c + 3, 1 - slot)
                    act.wait_ge(s("xa_out"), c + 1 + XA0[x])
                    apart()
                    act.activation(hic[:, :, c, :], G[:, 0, :].rearrange("p (k t) -> p k t", k=KT), ACT.Copy)\
                       .then_inc(s("xa_o_hi"), 1)

                act.wait_ge(s("evacuated"), PROD0["xo" + x])
                stage(0, 0)
                stage(1, 1)
                exps(0, 0)
                stage(2, 0)
                with act.Fori(0, NCH // 2 - 2) as i:
                    for n in range(2):
                        chunk(i * 2 + n, n)
                for c in range(NCH - 4, NCH):
                    chunk(c, c % 2, min(3, NCH - 1 - c))

            def ffn(name, two_tile_function):
                def hidden(c):
                    for j in range(2):
                        act.wait_ge(s("ff_gate_in"), 2 * c + j + 1 + FF0[name])
                        act.activation(W[:, 16 + j, :], W[:, 16 + j, :] if name == "ffn1" else TMP[:, j, :],
                                       two_tile_function).then_inc(s("ff_gate"), 1)
                    q = s("product_quarters")
                    if not isinstance(c, int):
                        act.wait_ge(q, c * 24 + 4 * (BLOCK0[name] + 4))
                    elif c:
                        act.wait_ge(q, 24 * c + 4 * (BLOCK0[name] + 4))
                    for j in range(2):
                        act.wait_ge(s("ff_hidden"), 2 * c + j + 1 + FF0[name])
                        act.activation(g_hi[:, j, :], W[:, 16 + j, :], ACT.Copy).then_inc(s("ff_g_hi"), 1)

                hidden(0)
                with act.Fori(1, FC) as c:
                    hidden(c)

            ev = lambda name: (lambda k: (s("evacuated"), PROD0[name] + k + 1))
            h_tile = lambda k: W[:, k, :]
            y_tile = lambda k: W[:, 8 + k, :]
            for k in range(KT):
                load(W[:, k, :], ap["xT"][:, k, :], f"x_in{k}")
            load(W[:, 20:22, :], ap["memT1"], "1_mem_in")
            memory("1")
            squares("q1", h_tile, ev("out1"))
            split_high("q1", h_tile, "x1", lambda k: (s("evacuated"), PROD0["k1"]), lambda k: weights_high("1", k))
            for n in range(KT, 2 * KT):
                weights_high("1", n)
            roots("q1")
            cross("1")
            squares("ffn1", h_tile, ev("xo1"))
            split_high("ffn1", h_tile, "ffn1", lambda k: (s("evacuated"), PROD0["ffn1"]))
            roots("ffn1")
            ffn("ffn1", ACT.Gelu)
            last_tile = lambda k: (s("evacuated"), PROD0["z2"] - KT + k + 1)
            squares("final", h_tile, last_tile)
            roots("final")
            load(phase[:, :], ap["consts"][:, CST["hg_reset"]:CST["hg_reset"] + 512], "phase2_in")
            for k in range(KT):
                act.wait_ge(s("h_final"), k + 1)
                act.activation(act_hi[:, k, :], W[:, k, :], ACT.Identity, scale=col("mix2", k)).then_inc(s("operand_hi"), 1)
                if k >= 2:
                    act.wait_ge(*norm("squares_summed", "z2", k - 1))
                act.activation(sq[k % 2], W[:, k, :], ACT.Square).then_inc(s("squares"), 1)
                act.wait_ge(*norm("squares", "z2", k + 1))
                load(ap["parked"][:, k, :], W[:, k, :], "parked")
            roots("z2")
            for n in range(22):
                if n < 4 or 12 <= n < 16 or 4 <= n < 8:
                    act.wait_ge(s("evacuated"), PROD0["z2"] + n + 1)
                    act.activation(W[:, n, :], W[:, n, :], ACT.Sigmoid if 4 <= n < 8 else ACT.Silu)\
                       .then_inc(s("z2_act"), 1)
                if n == 7:
                    act.wait_ge(s("lb_diff"), 1)
                    act.activation(small[:, 48:52], small[:, 48:52], ACT.Exp).then_inc(s("lb_exp"), 1)
            act.wait_ge(s("evacuated"), PROD0["out2"])
            lf, b_, D1, E1, E1n, K2, vs, vtok, k2tok, *Eb = hg("lf b D1 Q1 K1 K2 vs vtok k2tok Eb0 Eb1")

            def stage_window(c):
                act.activation(sw_q, Wc[:, 16:20, c, :], ACT.Copy).then_inc(s("sw_staged"), 1)
                before = c if isinstance(c, int) and c == 0 else c - 1
                act.activation(sw_kv[:, :, 0:P], Wc[:, 20:22, before, :], ACT.Copy).then_inc(s("sw_staged"), 1)
                act.activation(sw_kv[:, 0, P:2 * P], Wc[:, 20, c, :], ACT.Copy).then_inc(s("sw_staged"), 1)
                act.activation(sw_kv[:, 1, P:2 * P], Wc[:, 21, c, :], ACT.Copy).then_inc(s("sw_staged"), 1)

            def prepare(c, odd):
                if not isinstance(c, int) or c:
                    act.wait_ge(s("hg_scores"), c)
                    apart()
                act.activation(lf, Wc[:, 4:8, c, :], ACT.Ln).then_inc(s("hg_log"), 1)
                act.activation(vs, Wc[:, 8:12, c, :], ACT.Copy).then_inc(s("hg_v"), 1)
                act.wait_ge(s("hg_d"), 2 * c + 1)
                act.activation(E1, D1, ACT.Exp).then_inc(s("hg_exp"), 1)
                act.activation(E1n, D1, ACT.Exp, scale=-1.0).then_inc(s("hg_exp"), 1)
                act.activation(Eb[odd], b_, ACT.Exp).then_inc(s("hg_exp"), 1)
                act.wait_ge(s("hg_d"), 2 * c + 2)
                act.activation(K2, K2, ACT.Exp).then_inc(s("hg_exp"), 1)

            def mixer2(c, odd, ahead=True):
                act.wait_ge(s("sw_v_turned"), c + 1)
                act.activation(sw_v, Gf[:, 3 * HALF:3 * HALF + 256], ACT.Copy).then_inc(s("sw_v"), 1)
                act.wait_ge(s("hg_turned"), c + 1)
                act.activation(vtok, Gb[1], ACT.Copy).then_inc(s("hg_tokens"), 1)
                act.activation(k2tok, Gb[2], ACT.Copy).then_inc(s("hg_tokens"), 1)
                for g in range(2):
                    act.wait_ge(s("sw_negmax"), 2 * c + (g + 1))
                    for n in range(4 * g, 4 * g + 4):
                        act.activation(sw_pr[:, n * 256:(n + 1) * 256], sw_pr[:, n * 256:(n + 1) * 256], ACT.Exp,
                                       bias=small[:, 8 + n:9 + n], accum_out=small[:, 16 + n:17 + n])
                    act.activation(small[:, 24 + 4 * g:28 + 4 * g], small[:, 32 + 4 * g:36 + 4 * g], ACT.Exp)\
                       .then_inc(s("sw_exps"), 1)
                if ahead:
                    stage_window(c + 1)
                    prepare(c + 1, 1 - odd)
                for n in range(2):
                    act.wait_ge(s("sw_turned"), 2 * c + (n + 1))
                    act.activation(sw_pT[:, n * T:(n + 1) * T], G[:, n, :], ACT.Copy).then_inc(s("sw_pT"), 1)
                act.wait_ge(s("sw_pv"), c + 1)
                apart()
                act.activation(hic[:, 0:4, c, :], Gb[0], ACT.Copy).then_inc(s("sw_o_hi"), 1)

            stage_window(0)
            prepare(0, 0)
            mixer2(0, 0)
            with act.Fori(0, NCH // 2 - 1) as i:
                for n in (1, 2):
                    mixer2(i * 2 + n, n % 2)
            mixer2(NCH - 1, 1, False)
            for n in range(4):
                act.wait_ge(s("hg_kept"), NCH + 1)
                act.activation(W[:, 16, :], W[:, n, :], ACT.Square).then_inc(s("hr_sq"), 1)
                roots("hr", n + 1, 1.0 / P, W[:, 17, :])
                act.wait_ge(s("hr_y"), n + 1)
                act.activation(act_hi[:, 4 + n, :], W[:, n, :], ACT.Copy).then_inc(s("y2_hi"), 1)
            act.wait_ge(s("y2_lo"), 4)
            act.wait_ge(s("parked"), 16 * KT)
            for k in range(KT):
                load(W[:, k, :], ap["parked"][:, k, :], f"x_in{k}")
            load(W[:, 20:22, :], ap["memT2"], "2_mem_in")

            def post(name, nxt, gain, src_done, beside=None):
                squares(name, y_tile, src_done)
                roots(name)
                for k in range(KT):
                    if beside:
                        beside(k)
                    act.wait_ge(s(name + "_h"), k + 1)
                    act.activation(act_hi[:, k, :], W[:, k, :], ACT.Identity, scale=col(gain, k)).then_inc(s("operand_hi"), 1)
                    if k >= 2:
                        act.wait_ge(*norm("squares_summed", nxt, k - 1))
                    act.activation(sq[k % 2], W[:, k, :], ACT.Square).then_inc(s("squares"), 1)

            memory("2")
            post("pm", "q2", "x2", ev("out2"), lambda k: weights_high("2", k))
            for n in range(KT, 2 * KT):
                weights_high("2", n)
            roots("q2")
            cross("2")
            post("px", "ffn2", "ffn2", ev("xo2"))
            roots("ffn2")
            ffn("ffn2", ACT.Silu)
            squares("pf", y_tile, lambda k: (s("evacuated"), PROD0["ffn2"] + 12 * FC - KT + k + 1))
            roots("pf")
            for k in range(KT):
                act.wait_ge(s("pf_h"), k + 1)
                load(ap["out"][:, k, :], W[:, k, :], "stored")
            act.wait_ge(s("stored"), 16 * KT)

        @block.vector
        def _(dve):
            chain = Chain(dve, s("dve_chain"))
            link = chain.link

            def product(name, j, width=None):
                dve.wait_ge(s("product_quarters"), 4 * (j + (BLOCK0[name] + 1)) if not isinstance(j, int) else
                            4 * (BLOCK0[name] + 1 + j))

            def slot(name, j):
                return G[:, (PROD0[name] + j) % 2, :]

            def sums(name, k):
                dve.wait_ge(*norm("squares", name, k + 1))
                if k:
                    dve.wait_ge(*norm("squares_summed", name, k))
                    dve.tensor_tensor(ssum, ssum, sq[k % 2], ALU.add).then_inc(s("squares_summed"), 1)
                else:
                    dve.tensor_copy(ssum, sq[0]).then_inc(s("squares_summed"), 1)

            def have_rstd(name):
                dve.wait_ge(*norm("roots", name, 1, 1))

            def split_low(name, k, src, gain):
                dve.wait_ge(*operand_count("operand_hi", name, k + 1))
                dve.scalar_tensor_tensor(act_lo[:, k, :], src(k), col(gain, k), hi_as_f32[:, k, :], ALU.mult,
                                         ALU.subtract).then_inc(s("operand_lo"), 1)

            def low(name, k, tile, hi_count):
                dve.wait_ge(s(name + "_hi"), hi_count)
                dve.tensor_tensor(act_lo[:, k, :], tile, hi_as_f32[:, k, :], ALU.subtract).then_inc(s(name + "_lo"), 1)

            def standardize(name, jobs, div, before=None):
                done = 0
                for n, tiles in enumerate(jobs):
                    dve.wait_ge(s("std_mean"), STD0[name][0] + n + 1)
                    for t, tile in enumerate(tiles):
                        dve.scalar_tensor_tensor(tile, N[:, 0, :], -1.0 / div, tile, ALU.mult, ALU.add)\
                           .then_inc(s("std_centred"), 1)
                    dve.wait_ge(s("std_root"), STD0[name][0] + n + 1)
                    for t, tile in enumerate(tiles):
                        dve.wait_ge(s("std_centred"), STD0[name][1] + done + t + 1)
                        dve.tensor_tensor(tile, tile, W[:, 0, :], ALU.mult).then_inc(s("std_scaled"), 1)
                    done += len(tiles)
                    dve.wait_ge(s("std_scaled"), STD0[name][1] + done)

            h_tile = lambda k: W[:, k, :]
            y_tile = lambda k: W[:, 8 + k, :]

            for free in ("ml_kept", "ml_h", "xa_o_lo", "sw_o_lo", "hg_kept", "hg_S"):
                dve.sem_inc(s(free), 1)
            dve.memset(epsc[:, 0:1], RMS_EPS).then_inc(s("eps"), 1)
            dve.memset(epsc[:, 1:2], LN_EPS).then_inc(s("eps"), 1)
            dve.wait_ge(s("consts"), 32)
            for k in range(KT):
                split_low("z1", k, h_tile, "mix1")
                sums("z1", k)
            have_rstd("z1")

            def evacuate(j, dst):
                product("z1", j)
                dve.tensor_tensor(dst, slot("z1", j), rstd[:, :], ALU.mult).then_inc(s("evacuated"), 1)

            def conv(acc, x, weight, bias, taps, lo, hi):
                for n in range(lo, hi):
                    w = weight(taps - 1 - n)
                    if n == 0:
                        ins = dve.tensor_scalar(acc, x, w, bias, ALU.mult, ALU.add)
                    else:
                        ins = dve.scalar_tensor_tensor(acc[:, n:T], x[:, 0:T - n], w, acc[:, n:T], ALU.mult, ALU.add)
                    link(ins)

            def conv_b(n, lo, hi):
                conv(W[:, 2 + n, :], W[:, n, :], lambda j: col("cb_w", 31 * n + j), col("cb_b", n), 31, lo, hi)

            def conv_c(n):
                conv(W[:, 16 + n, :], W[:, 4 + n, :], lambda j: col("cc_w", 4 * n + j), col("cc_b", n), 4, 0, 4)
                dve.sem_inc(s("cc_done"), 1)

            product("z1", 0)
            dve.tensor_tensor(rowA, slot("z1", 0), rstd[:, :], ALU.mult).then_inc(s("evacuated"), 1)
            dve.wait_ge(s("evacuated"), 1)
            H4 = slice(0, NH)
            link(dve.tensor_scalar(rowF[H4], rowA[32:36, :], cols[32:36, COL["gate_b"]:COL["gate_b"] + 1], None, ALU.add))
            link(dve.tensor_scalar(rowA[H4], rowA[H4], cols[H4, COL["gate_b"]:COL["gate_b"] + 1], None, ALU.add))
            dve.sem_inc(s("row_forget"), 1)
            link(dve.memset(rowM[H4], 1.0))
            chunked = lambda v: v[H4].rearrange("p (c t) -> p c t", t=CH)
            link(dve.memset(chunked(rowM)[:, :, 0:1], 0.0))
            dve.wait_ge(s("row_abs"), 1)
            link(dve.tensor_scalar(rowF[H4], rowF[H4], 0.0, None, ALU.min))
            dve.wait_ge(s("row_log"), 1)
            link(dve.tensor_tensor(rowF[H4], rowF[H4], rowE[H4], ALU.subtract))
            link(dve.tensor_tensor_scan(rowE[H4], rowM[H4], rowF[H4], 0.0, ALU.mult, ALU.add))
            link(dve.tensor_tensor(rowA[H4], rowA[H4], rowE[H4], ALU.subtract))
            link(dve.memset(rowF[H4], 0.0))
            link(dve.tensor_copy(chunked(rowF)[:, 1:NCH, 0:1], chunked(rowE)[:, 0:NCH - 1, CH - 1:CH]))
            link(dve.tensor_tensor_scan(rowM[H4], rowF[H4], rowA[H4], 0.0, ALU.add, ALU.max))
            mprev = small[H4, 40:48].rearrange("p (c t) -> p c t", t=1)
            link(dve.memset(mprev[:, 0:1, :], 0.0))
            link(dve.tensor_tensor(mprev[:, 1:NCH, :], chunked(rowM)[:, 0:NCH - 1, CH - 1:CH],
                                   chunked(rowE)[:, 0:NCH - 1, CH - 1:CH], ALU.add))
            link(dve.tensor_tensor(chunked(rowF), mprev.to_broadcast([NH, NCH, CH]), chunked(rowM), ALU.subtract))
            link(dve.scalar_tensor_tensor(rowE[H4], rowE[H4], -1.0, rowM[H4], ALU.mult, ALU.subtract))
            link(dve.tensor_scalar(rowM[H4], rowM[H4], -1.0, None, ALU.mult))
            dve.sem_inc(s("ml_rows"), 1)

            for j in range(4):
                evacuate(1 + j, W[:, j, :])
            for n in range(2):
                dve.wait_ge(s("cf_gate"), n + 1)
                link(dve.tensor_tensor(W[:, n, :], W[:, n, :], W[:, 2 + n, :], ALU.mult))
            conv_b(0, 0, 3)
            for j in range(4):
                evacuate(5 + j, W[:, 4 + j, :])
                conv_b(0, 3 + 6 * j, 9 + 6 * j)
            dve.wait_ge(s("evacuated"), 9)
            conv_c(0)
            conv_c(1)
            for j in range(2):
                evacuate(9 + j, W[:, 8 + j, :])
                conv_c(2 + j)
            evacuate(11, W[:, 10, :])
            conv_b(0, 27, 31)
            dve.sem_inc(s("cb_done"), 1)
            evacuate(12, W[:, 11, :])
            conv_b(1, 0, 7)
            for j in range(4):
                evacuate(13 + j, W[:, 12 + j, :])
                conv_b(1, 7 + 6 * j, 13 + 6 * j)
            dve.sem_inc(s("cb_done"), 1)

            standardize("cf", [[W[:, 2, :]], [W[:, 3, :]]], 64)
            for n in range(2):
                low("y1", 2 + n, W[:, 2 + n, :], n + 1)
            standardize("ln", [[W[:, 10, :], W[:, 11, :]]], 256)
            dve.wait_ge(s("mix_in"), 80)
            link(dve.tensor_scalar(W[:, 0, 0:P], const("ml_mask"), 0.0, None, ALU.is_gt))
            dve.tensor_tensor(wsT.rearrange("p (h t) -> p h t", h=NH), wsT.rearrange("p (h t) -> p h t", h=NH),
                              W[:, 0:1, 0:P].to_broadcast([P, NH, P]), ALU.mult).then_inc(s("ws_masked"), 1)
            dve.wait_ge(s("ws_masked"), 1)
            dve.wait_ge(s("gm_mixed"), 1)
            dve.wait_ge(s("ln_out"), 2)
            for k in range(2):
                link(dve.tensor_tensor(W[:, k, :].rearrange("p (c t) -> p c t", t=CH),
                                       N[:, k, :].rearrange("p (c t) -> p c t", t=CH),
                                       bsv[:, k:k + 1, :].to_broadcast([P, NCH, CH]), ALU.add))
                dve.tensor_tensor(W[:, k, :], W[:, k, :], W[:, 8 + k, :], ALU.mult).then_inc(s("gm_y"), 1)
            for k in range(2):
                low("y1", k, W[:, k, :], 3 + k)
            dve.wait_ge(s("y1_lo"), 4)
            dve.sem_inc(s("ml_free"), 1)
            dve.memset(Cst, 0.0).then_inc(s("ml_init"), 1)
            dve.memset(vt[:, :, P:2 * P], 1.0).then_inc(s("ml_init"), 1)
            dve.wait_ge(s("ml_init"), 2)
            mask = const("ml_mask").rearrange("p (a t) -> p a t", a=1).to_broadcast([P, NH, P])

            def bounded(c):
                dve.wait_ge(s("ml_spread"), c + 1)
                dve.tensor_tensor(Et, Nb[0], mask, ALU.min).then_inc(s("ml_bounded"), 1)

            def mlstm(c, ahead=True):
                dve.wait_ge(s("ml_exp"), 3 * c + 1)
                dve.wait_ge(s("ml_qkv"), 3 * c + 1)
                dve.tensor_tensor(qw, qT, winter, ALU.mult).then_inc(s("ml_weighted"), 1)
                dve.wait_ge(s("ml_exp"), 3 * c + 3)
                dve.wait_ge(s("ml_proj"), 2 * c + 2)
                dve.tensor_tensor(kw, Gb[2], Wt[:, :, P - 1:P].to_broadcast([P, NH, P]), ALU.mult)\
                   .then_inc(s("ml_weighted"), 1)
                dve.wait_ge(s("ml_scores"), c + 1)
                dve.tensor_tensor(Pm, Nb[1], Wt, ALU.mult).then_inc(s("ml_weighted"), 1)
                dve.wait_ge(s("ml_den"), c + 1)
                link(dve.tensor_tensor(dn, dn, emm, ALU.max))
                link(dve.reciprocal(dn, dn))
                dve.tensor_tensor(Wc[:, 4:8, c, :], Gb[0], dn, ALU.mult).then_inc(s("ml_h"), 1)
                dve.wait_ge(s("ml_update"), c + 1)
                for h in range(NH):
                    last = dve.scalar_tensor_tensor(Cst[:, h, :], Cst[:, h, :], winter[:, h, P - 1:P],
                                                    Gf[:, T + 256 * h:T + 256 * h + 256], ALU.mult, ALU.add)
                last.then_inc(s("ml_kept"), 1)
                if ahead:
                    bounded(c + 1)

            bounded(0)
            with dve.Fori(0, NCH - 1) as c:
                chain.enter(c, 0, 2)
                mlstm(c)
            chain.leave(NCH - 1)
            mlstm(NCH - 1, False)
            dve.wait_ge(s("ml_h"), NCH + 1)
            dve.wait_ge(s("ml_kept"), NCH + 1)
            standardize("hn", [[W[:, 4 + n, :]] for n in range(4)], P)
            for n in range(4):
                dve.wait_ge(s("hn_out"), n + 1)
                dve.wait_ge(s("ogate"), 4)
                link(dve.scalar_tensor_tensor(W[:, 16 + n, :], W[:, 16 + n, :], col("skip", n), W[:, 4 + n, :],
                                              ALU.mult, ALU.add))
                dve.tensor_tensor(W[:, 4 + n, :], W[:, 16 + n, :], W[:, 12 + n, :], ALU.mult).then_inc(s("ml_y"), 1)
                dve.wait_ge(s("ml_y"), n + 1)
            for n in range(4):
                low("y1", 4 + n, W[:, 4 + n, :], 5 + n)

            def memory(x):
                mem = flat[:, 20 * T:22 * T]
                dve.wait_ge(s(x + "_mem_root"), 1)
                m3 = mem.rearrange("p (k m) -> p k m", m=MEM)
                dve.tensor_tensor(m3, m3, W[:, 14:15, 0:MEM].to_broadcast([P, KT, MEM]), ALU.mult)\
                   .then_inc(s(x + "_mem_scaled"), 1)
                dve.wait_ge(s(x + "_mem_scaled"), 1)
                for k in range(KT):
                    dve.wait_ge(s(x + "_mem_hi"), k + 1)
                    dve.scalar_tensor_tensor(m_lo[:, k, :], m3[:, k, :], col("mem" + x, k), m_hi[:, k, :].bitcast(F32),
                                             ALU.mult, ALU.subtract).then_inc(s("mem_lo"), 1)

            def key(x, n):
                product("k" + x, n)
                dve.tensor_copy(keys[:, n, :], slot("k" + x, n)[:, 0:MEM]).then_inc(s("evacuated"), 1)

            def value(x, g):
                dve.wait_ge(s("product_quarters"), 4 * (BLOCK0["v" + x] + 4 * (g + 1)))
                dve.tensor_copy(values[:, :, g * HALF:(g + 1) * HALF], slot("v" + x, g).rearrange("p (m f) -> p m f", m=2))\
                   .then_inc(s("evacuated"), 1)

            def query_tiles(x):
                with dve.Fori(0, KT // 2) as n:
                    for j in range(2):
                        product("q" + x, n * 2 + j)
                        dve.scalar_tensor_tensor(queries[:, n * 2 + j, :], slot("q" + x, j), float(D // NH) ** -0.5,
                                                 rstd[:, :], ALU.mult, ALU.mult).then_inc(s("evacuated"), 1)

            def cross(x):
                score_slots = [Nf[:, 0:T], G[:, 1, :]]
                pr = TMP[:, 1, :].rearrange("p (h m) -> p h m", h=NH)

                def largest(c, slot):
                    dve.wait_ge(s("xa_scores"), c + 1 + XA0[x])
                    link(dve.tensor_reduce(small[:, 20 * slot:20 * slot + 4], score_slots[slot].rearrange("p (h m) -> p h m", h=NH), AX,
                                           ALU.max))
                    dve.tensor_scalar(small[:, 4 + 12 * slot:8 + 12 * slot], small[:, 20 * slot:20 * slot + 4], -1.0, None, ALU.mult)\
                       .then_inc(s("xa_negmax"), 1)

                def probs(c):
                    dve.wait_ge(s("xa_exps"), c + 1 + XA0[x])
                    link(dve.reciprocal(small[:, 12:16], small[:, 8:12]))
                    dve.tensor_tensor(pr, pr, small[:, 12:16].rearrange("p (h m) -> p h m", m=1).to_broadcast([P, NH, MEM]),
                                      ALU.mult).then_inc(s("xa_probs"), 1)

                def low_part(c):
                    dve.wait_ge(s("xa_o_hi"), c + 1 + XA0[x])
                    dve.tensor_tensor(loc[:, :, c, :], G[:, 0, :].rearrange("p (k t) -> p k t", k=KT), hicf[:, :, c, :],
                                      ALU.subtract).then_inc(s("xa_o_lo"), 1)

                largest(0, 0)
                largest(1, 1)
                probs(0)
                with dve.Fori(0, (NCH - 2) // 2) as i:
                    chain.enter(i, 0, 4)
                    for n in range(2):
                        probs(i * 2 + (n + 1))
                        largest(i * 2 + (n + 2), n)
                        low_part(i * 2 + n)
                chain.leave((NCH - 2) // 2)
                probs(NCH - 1)
                low_part(NCH - 2)
                low_part(NCH - 1)

            def ffn(name, target, conv_tiles):
                cf = cols[:, COL["cf"]:COL["cf"] + 4 * FT].rearrange("p (c j) -> p c j", j=8)

                def hidden(c):
                    static = isinstance(c, int)
                    for j in range(4):
                        dve.wait_ge(s("product_quarters"), 24 * c + 4 * (BLOCK0[name] + 1 + j) if static
                                    else c * 24 + 4 * (BLOCK0[name] - 1 + j))
                        dve.tensor_tensor(TMP[:, j, :], slot(name, j), rstd[:, :], ALU.mult).then_inc(s("evacuated"), 1)
                        if j < 2:
                            dve.wait_ge(s("evacuated"), c * 12 + (PROD0[name] + j + 1) if static
                                        else c * 12 + (PROD0[name] + j - 7))
                        if conv_tiles and j < 2:
                            acc, x = W[:, 16 + j, :], TMP[:, j, :]
                            w = lambda n: cf[:, c, 4 * j + n:4 * j + n + 1]
                            link(dve.tensor_scalar(acc, x, w(2), w(3), ALU.mult, ALU.add))
                            link(dve.scalar_tensor_tensor(acc[:, 1:T], x[:, 0:T - 1], w(1), acc[:, 1:T], ALU.mult, ALU.add))
                            dve.scalar_tensor_tensor(acc[:, 2:T], x[:, 0:T - 2], w(0), acc[:, 2:T], ALU.mult, ALU.add)\
                               .then_inc(s("ff_gate_in"), 1)
                        elif j < 2:
                            dve.sem_inc(s("ff_gate_in"), 1)
                    for j in range(2):
                        dve.wait_ge(s("evacuated"), c * 12 + (PROD0[name] + j + 3) if static
                                    else c * 12 + (PROD0[name] + j - 5))
                        dve.wait_ge(s("ff_gate"), 2 * c + j + 1 + FF0[name])
                        dve.tensor_tensor(W[:, 16 + j, :], W[:, 16 + j, :], TMP[:, 2 + j, :], ALU.mult)\
                           .then_inc(s("ff_hidden"), 1)

                def low_parts(c):
                    for j in range(2):
                        dve.wait_ge(s("ff_g_hi"), 2 * c + j + 1 + FF0[name])
                        dve.tensor_tensor(g_lo[:, j, :], W[:, 16 + j, :], g_hi[:, j, :].bitcast(F32), ALU.subtract)\
                           .then_inc(s("ff_g_lo"), 1)

                def add_down(c):
                    for o in range(KT):
                        first = 4 * (BLOCK0[name] + 8) + o + 1
                        dve.wait_ge(s("product_quarters"), c * 24 + (first - 24))
                        dve.tensor_tensor(target(o), target(o), slot(name, 4 + o), ALU.add).then_inc(s("evacuated"), 1)

                hidden(0)
                low_parts(0)
                with dve.Fori(1, FC) as c:
                    if conv_tiles:
                        chain.enter(c, 1, 4)
                    hidden(c)
                    add_down(c)
                    low_parts(c)
                if conv_tiles:
                    chain.leave(FC - 1)

            def last_down(name, target, norm):
                for o in range(KT):
                    dve.wait_ge(s("product_quarters"), 4 * (BLOCK0[name] + 6 * FC - 2) + o + 1)
                    dve.tensor_tensor(target(o), target(o), slot(name, o), ALU.add).then_inc(s("evacuated"), 1)
                    if o:
                        sums(norm, o - 1)
                sums(norm, KT - 1)

            def to_tiles(name, norm, target, add, loaded=None):
                for j in range(KT):
                    product(name, j)
                    if loaded:
                        dve.wait_ge(*loaded(j))
                    if add:
                        ins = dve.tensor_tensor(target(j), target(j), slot(name, j), ALU.add)
                    else:
                        ins = dve.tensor_copy(target(j), slot(name, j))
                    ins.then_inc(s("evacuated"), 1)
                    if j:
                        sums(norm, j - 1)
                sums(norm, KT - 1)

            def operand(name, gain):
                for k in range(KT):
                    split_low(name, k, h_tile, gain)
                have_rstd(name)

            memory("1")
            to_tiles("out1", "q1", h_tile, True, lambda j: (s(f"x_in{j}"), 32))
            for k in range(KT):
                split_low("q1", k, h_tile, "x1")
                key("1", k)
            for g in range(2):
                value("1", g)
            have_rstd("q1")
            query_tiles("1")
            cross("1")
            to_tiles("xo1", "ffn1", h_tile, True)
            operand("ffn1", "ffn1")
            ffn("ffn1", h_tile, True)
            last_down("ffn1", h_tile, "final")
            have_rstd("final")
            for k in range(KT):
                dve.scalar_tensor_tensor(W[:, k, :], W[:, k, :], col("final", k), rstd[:, :], ALU.mult, ALU.mult)\
                   .then_inc(s("h_final"), 1)
                if k:
                    split_low("z2", k - 1, h_tile, "mix2")
                    sums("z2", k - 1)
            split_low("z2", KT - 1, h_tile, "mix2")
            sums("z2", KT - 1)
            have_rstd("z2")
            dve.wait_ge(s("parked"), 16 * KT)
            for j in range(22):
                product("z2", j)
                dve.tensor_tensor(W[:, j, :], slot("z2", j), rstd[:, :], ALU.mult).then_inc(s("evacuated"), 1)
                if j == 8:
                    lb = cols[:, COL["lb"]:COL["lb"] + 8]
                    link(dve.tensor_tensor(small[:, 48:52], lb[:, 4:8], lb[:, 0:4], ALU.subtract))
                    dve.sem_inc(s("lb_diff"), 1)
                    dve.wait_ge(s("lb_exp"), 1)
                    link(dve.tensor_scalar(small[:, 48:52], small[:, 48:52], 1.0, None, ALU.add))
                    link(dve.reciprocal(small[:, 48:52], small[:, 48:52]))
                    link(dve.tensor_scalar(small[:, 52:56], small[:, 48:52], -1.0, 1.0, ALU.mult, ALU.add))
                if 8 < j <= 12:
                    n = j - 9
                    dve.wait_ge(s("z2_act"), 4 + n + 1)
                    dve.tensor_scalar(W[:, 4 + n, :], W[:, 4 + n, :], small[:, 52 + n:53 + n], small[:, 48 + n:49 + n],
                                      ALU.mult, ALU.add).then_inc(s("hg_f"), 1)

            sinks = cols[:, COL["sinks"]:COL["sinks"] + 8]
            pr = sw_pr.rearrange("p (h m) -> p h m", m=256)
            s3 = Nf.rearrange("p (h m) -> p h m", m=256)
            Q1, K1, K2, AT, S, lf, b_, D1 = hg("Q1 K1 K2 AT S lf b D1")
            Q2, Eb = hg("Q20 Q21"), hg("Eb0 Eb1")
            qscale = float(P) ** -0.5
            dve.wait_ge(s("evacuated"), PROD0["out2"])
            link(dve.memset(AT, 0.0))
            link(dve.memset(S, 0.0))
            dve.sem_inc(s("hg_init"), 1)
            dve.wait_ge(s("phase2_in"), 16)
            hmask = const("hg_mask").bitcast(U32).rearrange("p (a t) -> p a t", a=1).to_broadcast([P, NH, P])
            halves = lambda v: v.rearrange("p h (a t) -> p (h a) t", t=64)

            def attention_low(c):
                dve.wait_ge(s("sw_o_hi"), c + 1)
                dve.tensor_tensor(loc[:, 0:4, c, :], Gb[0], hicf[:, 0:4, c, :], ALU.subtract).then_inc(s("sw_o_lo"), 1)

            def decays(c):
                dve.wait_ge(s("hg_log"), c + 1)
                link(dve.tensor_tensor_scan(b_.rearrange("p h t -> p (h t)"), phase[:, :],
                                            lf.rearrange("p h t -> p (h t)"), 0.0, ALU.mult, ALU.add))
                dve.tensor_tensor(halves(D1), halves(b_), halves(b_)[:, :, 31:32].to_broadcast([P, 8, 64]), ALU.subtract)\
                   .then_inc(s("hg_d"), 1)
                dve.tensor_tensor(halves(K2), halves(b_)[:, :, 63:64].to_broadcast([P, 8, 64]), halves(b_), ALU.subtract)\
                   .then_inc(s("hg_d"), 1)

            def weighted(c, odd):
                q_, f_ = Wc[:, 0:4, c, :], Wc[:, 4:8, c, :]
                dve.wait_ge(s("hg_exp"), 4 * c + 4)
                dve.scalar_tensor_tensor(K2, f_, 1.0, K2, ALU.subtract, ALU.mult, reverse0=True).then_inc(s("hg_qk"), 1)
                dve.scalar_tensor_tensor(Q1, q_, qscale, Q1, ALU.mult, ALU.mult).then_inc(s("hg_qk"), 1)
                dve.scalar_tensor_tensor(K1, f_, 1.0, K1, ALU.subtract, ALU.mult, reverse0=True).then_inc(s("hg_qk"), 1)
                dve.scalar_tensor_tensor(Q2[odd], q_, qscale, Eb[odd], ALU.mult, ALU.mult).then_inc(s("hg_qk"), 1)

            def state(c, odd, sub):
                dve.wait_ge(s("hg_update"), 2 * c + (sub + 1))
                if sub:
                    dve.wait_ge(s("hg_S"), 2 * c + 2)
                for h in range(NH):
                    last = dve.scalar_tensor_tensor(S[:, h, :], S[:, h, :], Eb[odd][:, h, 64 * sub + 63:64 * sub + 64],
                                                    Nb[2 + sub][:, h, :], ALU.mult, ALU.add)
                last.then_inc(s("hg_S"), 1)

            def mixer2(c, odd, ahead=True):
                first = isinstance(c, int) and c == 0
                mask = const("swa_first" if first else "swa_rest", 256).rearrange("p (a t) -> p a t", a=1)
                if not first:
                    attention_low(c - 1)
                for g in range(2):
                    heads_g, of = slice(4 * g, 4 * g + 4), lambda n: small[:, n + 4 * g:n + 4 * g + 4]
                    dve.wait_ge(s("sw_scores"), 2 * c + (g + 1))
                    link(dve.scalar_tensor_tensor(pr[:, heads_g, :], s3[:, heads_g, :], 0.125,
                                                  mask.to_broadcast([P, 4, 256]), ALU.mult, ALU.min))
                    link(dve.tensor_reduce(of(0), pr[:, heads_g, :], AX, ALU.max))
                    link(dve.tensor_tensor(of(0), of(0), sinks[:, heads_g], ALU.max))
                    link(dve.tensor_tensor(of(32), sinks[:, heads_g], of(0), ALU.subtract))
                    dve.tensor_scalar(of(8), of(0), -1.0, None, ALU.mult).then_inc(s("sw_negmax"), 1)
                dve.wait_ge(s("hg_scores"), c + 1)
                dve.memset(small[:, 60:61], 0.0)
                dve.copy_predicated(AT, hmask, Gb[0]).then_inc(s("hg_masked"), 1)
                for g in range(2):
                    of = lambda n: small[:, n + 4 * g:n + 4 * g + 4]
                    dve.wait_ge(s("sw_exps"), 2 * c + (g + 1))
                    link(dve.tensor_tensor(of(16), of(16), of(24), ALU.add))
                    link(dve.reciprocal(of(16), of(16)))
                    pg = pr[:, 4 * g:4 * g + 4, :]
                    dve.tensor_tensor(pg, pg, of(16).rearrange("p (h m) -> p h m", m=1).to_broadcast([P, 4, 256]),
                                      ALU.mult).then_inc(s("sw_probs"), 1)
                state(c, odd, 0)
                if ahead:
                    decays(c + 1)
                state(c, odd, 1)
                dve.tensor_scalar(Wc[:, 0:4, c, :], Nb[1], 1.0, None, ALU.mult).then_inc(s("hg_kept"), 1)
                if ahead:
                    weighted(c + 1, 1 - odd)

            decays(0)
            weighted(0, 0)
            mixer2(0, 0)
            with dve.Fori(0, NCH // 2 - 1) as i:
                chain.enter(i, 0, 26)
                for n in (1, 2):
                    mixer2(i * 2 + n, n % 2)
            chain.leave(NCH // 2 - 1)
            mixer2(NCH - 1, 1, False)
            attention_low(NCH - 1)
            dve.wait_ge(s("sw_o_lo"), NCH + 1)
            dve.wait_ge(s("hg_kept"), NCH + 1)
            for n in range(4):
                dve.wait_ge(s("hr_root"), n + 1)
                link(dve.scalar_tensor_tensor(W[:, n, :], W[:, n, :], col("onorm", 0), W[:, 17, :], ALU.mult, ALU.mult))
                dve.tensor_tensor(W[:, n, :], W[:, n, :], W[:, 12 + n, :], ALU.mult).then_inc(s("hr_y"), 1)
                dve.wait_ge(s("hr_y"), n + 1)
                low("y2", 4 + n, W[:, n, :], n + 1)

            def post(name, nxt, post_gain, gain, loaded=None, beside=None):
                have_rstd(name)
                for k in range(KT):
                    if loaded:
                        dve.wait_ge(*loaded(k))
                    link(dve.scalar_tensor_tensor(root, W[:, 8 + k, :], col(post_gain, k), rstd[:, :], ALU.mult, ALU.mult))
                    dve.tensor_tensor(W[:, k, :], W[:, k, :], root, ALU.add).then_inc(s(name + "_h"), 1)
                    dve.wait_ge(s(name + "_h"), k + 1)
                    if beside:
                        beside(k)
                    if nxt and k:
                        split_low(nxt, k - 1, h_tile, gain)
                        sums(nxt, k - 1)
                if nxt:
                    split_low(nxt, KT - 1, h_tile, gain)
                    sums(nxt, KT - 1)

            memory("2")
            to_tiles("out2", "pm", y_tile, False)
            post("pm", "q2", "post_mix", "x2", lambda k: (s(f"x_in{k}"), 48), lambda k: key("2", k))
            for g in range(2):
                value("2", g)
            have_rstd("q2")
            query_tiles("2")
            cross("2")
            to_tiles("xo2", "px", y_tile, False)
            post("px", "ffn2", "post_x", "ffn2")
            have_rstd("ffn2")
            link(dve.memset(W[:, 8:16, :], 0.0))
            ffn("ffn2", y_tile, False)
            last_down("ffn2", y_tile, "pf")
            post("pf", None, "post_ffn", None)


def packed(w):
    return w.reshape(KT, P, -1, P).transpose(2, 1, 0, 3).reshape(-1, P, KT * P)


def packed_values(w):
    return w.reshape(4, 2, P, 2, HALF).transpose(3, 0, 2, 1, 4).reshape(KT, P, KT * P)


def packed_down(w, c):
    w = w[2 * P * c:2 * P * (c + 1)].reshape(2, P, 2, 4, P)
    return w.transpose(2, 1, 3, 0, 4).reshape(2, P, KT * P)


def packed_ffn(gate, up, down):
    gate, up = packed(gate), packed(up)
    out = []
    for c in range(FC + 1):
        if c < FC:
            out += [gate[2 * c:2 * c + 2], up[2 * c:2 * c + 2]]
        if c:
            out.append(packed_down(down, c - 1))
    return out


def columns(v):
    return v.reshape(-1, P).T


def constants():
    c = np.zeros((P, NCONST), np.float32)

    def put(name, value):
        c[:value.shape[0], CST[name]:CST[name] + value.shape[1]] = value

    r = np.arange(P)
    put("ident", np.eye(P))
    put("ones", np.ones((P, P)))
    put("blk", (r[:, None] // 64 == r[None] // 64) * 1.0)
    put("ml_mask", np.where(r[:, None] <= r[None], BIG, NEG))
    key, query = np.arange(256)[None] // 64, r[:, None] // 64
    seen = (key >= query) & (key <= query + 2)
    put("swa_rest", np.where(seen, BIG, NEG))
    put("swa_first", np.where(seen & (key >= 2), BIG, NEG))
    put("hg_mask", ((r[:, None] // 64 == r[None] // 64) & (r[:, None] <= r[None])) * 1.0)
    put("hg_reset", np.tile((np.arange(512) % 64 != 0) * 1.0, (P, 1)))
    put("sel", np.repeat(np.eye(NH), P, axis=1))
    return c


def kernel(**inputs):
    import concourse.bacc as bacc
    from concourse.bass_utils import run_bass_kernel_spmd

    i = {name: np.asarray(a) for name, a in inputs.items()}
    v = {name: a[0] for name, a in i.items() if name not in ("final_g",)}
    w_in = v["w_in"]
    gates = np.zeros((D, P), np.float32)
    gates[:, 0:NH] = w_in[:, 2048:2052]
    gates[:, 32:32 + NH] = w_in[:, 2052:2056]
    z1 = np.concatenate([gates, w_in[:, 512:1024], w_in[:, 1024:1536], w_in[:, 0:512], w_in[:, 1536:2048]], 1)
    w2 = v["w_in_2"]
    pair = [64 * h + d for n in range(4) for h in (n, 4 + n) for d in range(64)]
    z2 = np.concatenate([w2[:, 768:2816], w2[:, 0:512][:, pair], w2[:, 512:768]], 1)
    w_out2 = np.concatenate([v["w_out_2"][0:512][pair], v["w_out_2"][512:]], 0)
    stream = [packed(z1), packed(v["w_out"]), packed(v["w_xkv"][:, :D]), packed_values(v["w_xkv"][:, D:]), packed(v["w_xq"]), packed(v["w_xo"]),
              *packed_ffn(v["w_up"][:, :FT * P], v["w_up"][:, FT * P:], v["w_down"]),
              packed(z2), packed(w_out2), packed(v["wk_x_2"]), packed_values(v["wv_x_2"]), packed(v["wq_x_2"]),
              packed(v["wo_x_2"]), *packed_ffn(v["w_gate_2"], v["w_up_2"], v["w_down_2"])]
    gate_b = np.zeros((P, 1), np.float32)
    gate_b[0:NH, 0], gate_b[32:32 + NH, 0] = v["b_igate"], v["b_fgate"]
    conv_f = np.concatenate([v["conv_f_w"], v["conv_f_b"][None]], 0)
    by = {"mix1": columns(v["norm_mix_g"]), "lna_g": columns(v["ln_a_g"]), "lna_b": columns(v["ln_a_b"]),
          "cb_w": columns(v["conv_b_w"].reshape(31, 2, P).transpose(1, 0, 2)),
          "cb_b": columns(v["conv_b_b"]), "gnb_g": columns(v["gn_b_g"]), "gnb_b": columns(v["gn_b_b"]),
          "cc_w": columns(v["conv_c_w"].reshape(4, 4, P).transpose(1, 0, 2)), "cc_b": columns(v["conv_c_b"]),
          "hn_g": columns(v["hn_c_g"]), "skip": columns(v["skip_c"]), "x1": columns(v["norm_x_g"]),
          "mem1": columns(v["norm_mem_g"]), "ffn1": columns(v["norm_ffn_g"]),
          "cf": columns(conv_f.reshape(4, FT, P).transpose(1, 0, 2)), "final": columns(i["final_g"]),
          "mix2": columns(v["g_mix_pre_2"]), "post_mix": columns(v["g_mix_post_2"]), "mem2": columns(v["g_mem_2"]),
          "x2": columns(v["g_x_pre_2"]), "post_x": columns(v["g_x_post_2"]), "ffn2": columns(v["g_ffn_pre_2"]),
          "post_ffn": columns(v["g_ffn_post_2"]), "lb": columns(i["hgrn_lb_2"]), "onorm": columns(v["hgrn_onorm_2"]),
          "sinks": np.broadcast_to(v["sinks_2"], (P, 8)), "gate_b": gate_b}
    tiles = lambda a: a.T.reshape(KT, P, -1).transpose(1, 0, 2)
    arrays = {
        "wstream": np.concatenate(stream, 0),
        "cols": np.concatenate([by[name] for name, _ in COLS], 1),
        "consts": constants(),
        "xT": tiles(v["x"]),
        "memT1": tiles(v["mem"]).reshape(P, 2, T),
        "memT2": tiles(v["mem_2"]).reshape(P, 2, T),
        "w_q": v["w_q_c"].transpose(1, 0, 2).reshape(P, -1),
        "w_k": v["w_k_c"].transpose(1, 0, 2).reshape(P, -1),
        "w_v": v["w_v_c"].transpose(1, 0, 2).reshape(P, -1),
        "w_sT": v["w_s"].transpose(2, 0, 1).reshape(P, -1),
        "b_s": np.repeat(v["b_s"].reshape(2, 2, 1, P), 64, axis=2).reshape(2, P, P).transpose(1, 0, 2).reshape(P, -1),
    }
    arrays = {name: np.ascontiguousarray(a, np.float32) for name, a in arrays.items()}
    nc = bacc.Bacc("TRN2", target_bir_lowering=False, num_devices=1)
    ap = {name: nc.dram_tensor(name, a.shape, F32, kind="ExternalInput").ap() for name, a in arrays.items()}
    ap["out"] = nc.dram_tensor("out", (P, KT, T), F32, kind="ExternalOutput").ap()
    ap["parked"] = nc.dram_tensor("parked", (P, KT, T), F32, kind="Internal").ap()
    program(nc, ap)
    result = run_bass_kernel_spmd(nc, [arrays], core_ids=[0]).results[0]["out"]
    return np.asarray(result).transpose(2, 1, 0).reshape(1, T, D)
```

```python
from contextlib import ExitStack

import numpy as np

import concourse.bass as bass
from concourse import mybir

F32 = mybir.dt.float32
F32R = mybir.dt.float32r
U32 = mybir.dt.uint32
ACT = mybir.ActivationFunctionType
ALU = mybir.AluOpType
AX = mybir.AxisListType.X

P = 128
T = 1024
D = 1024
KT = D // P
HALF = 512
CH = 128
NCH = T // CH
MEM = 256
FT = 22
FC = FT // 2
NH = 4
BIG = 3.0e38
NEG = -1.0e30
RMS_EPS = 1e-6
LN_EPS = 1e-5

STAGES = [("z1", 17, 17), ("out1", 8, 8), ("k1", 8, 8), ("v1", 8, 2), ("q1", 8, 8), ("xo1", 8, 8),
          ("ffn1", 6 * FC, 12 * FC),
          ("z2", 22, 22), ("out2", 8, 8), ("k2", 8, 8), ("v2", 8, 2), ("q2", 8, 8), ("xo2", 8, 8),
          ("ffn2", 6 * FC, 12 * FC)]
BLOCK0, PROD0 = {}, {}
_b = _p = 0
for _name, _nb, _np_ in STAGES:
    BLOCK0[_name], PROD0[_name] = _b, _p
    _b, _p = _b + _nb, _p + _np_
NBLOCKS = _b

COLS = [("mix1", 8), ("lna_g", 2), ("lna_b", 2), ("cb_w", 62), ("cb_b", 2), ("gnb_g", 2), ("gnb_b", 2),
        ("cc_w", 16), ("cc_b", 4), ("hn_g", 4), ("skip", 4), ("x1", 8), ("mem1", 8), ("ffn1", 8),
        ("cf", 4 * FT), ("final", 8), ("mix2", 8), ("post_mix", 8), ("mem2", 8), ("x2", 8),
        ("post_x", 8), ("ffn2", 8), ("post_ffn", 8), ("lb", 8), ("onorm", 1), ("sinks", 8), ("gate_b", 1)]
COL = {}
_c = 0
for _name, _n in COLS:
    COL[_name] = _c
    _c += _n
NCOLS = _c

CONSTS = [("ident", 128), ("ones", 128), ("blk", 128), ("ml_mask", 128), ("swa_rest", 256),
          ("swa_first", 256), ("hg_mask", 128), ("hg_reset", 512), ("sel", 512)]
CST = {}
_c = 0
for _name, _n in CONSTS:
    CST[_name] = _c
    _c += _n
NCONST = _c
NKEPT = CST["hg_reset"]


NORMS = ["z1", "q1", "ffn1", "final", "z2", "pm", "q2", "px", "ffn2", "pf"]
OPERANDS = ["z1", "q1", "ffn1", "z2", "q2", "ffn2"]
KV0 = {"1": 0, "2": 2 * KT}
XA0 = {"1": 0, "2": NCH}
STD0 = {"mix": (0, 0), "hn": (3, 4)}
FF0 = {"ffn1": 0, "ffn2": FT}


class Chain:

    def __init__(self, eng, sem):
        self.eng, self.sem, self.n, self.turn = eng, sem, 0, 0

    def link(self, ins):
        ins.then_inc(self.sem, 1)
        self.n += 1
        self.eng.wait_ge(self.sem, self.turn + self.n)

    def enter(self, i, first, per):
        self.turn, self.start, self.per = (i - first) * per, self.n, per

    def leave(self, trips):
        assert self.n - self.start == self.per, self.n - self.start
        self.n, self.turn = self.start + trips * self.per, 0


def program(nc, ap):
    ctx = ExitStack()
    with ctx:
        semaphores = {}

        def s(name):
            if name not in semaphores:
                semaphores[name] = ctx.enter_context(nc.semaphore(name))
            return semaphores[name]

        def norm(what, name, n, per=KT):
            return s(what), per * NORMS.index(name) + n

        def operand_count(what, name, n):
            if name in ("m1", "m2"):
                return s("mem_lo"), KT * (name == "m2") + n
            return s(what), KT * OPERANDS.index(name) + n

        arena_cols = 53200
        ctx.enter_context(nc.sbuf_tensor("arena", [P, arena_cols], F32))
        first_byte = nc.sbuf_base - 4 * arena_cols
        place_of = {}
        used = [0]

        def place(name, shape, dt=F32, over=None, offset=0):
            size = -(-int(np.prod(shape[1:])) // 8) * 8
            if over is None:
                start = used[0]
                used[0] += size
            else:
                start = place_of[over] + offset
            place_of[name] = start
            assert used[0] <= arena_cols, used
            return nc.alloc_sbuf_tensor_at(name, shape, dt, offset=first_byte + 4 * start)

        act_hi = place("act_hi", [P, KT, T], F32R)
        act_lo = place("act_lo", [P, KT, T], F32R)
        w_raw = place("w_raw", [P, 2, KT * P])
        w_hi = place("w_hi", [P, 2, KT * P], F32R)
        w_lo = place("w_lo", [P, 2, KT * P], F32R)
        W = place("work", [P, FT, T])
        TMP = place("tmp", [P, 4, T])
        rstd = place("rstd", [P, T])
        cst = place("cst", [P, NKEPT])
        phase = place("phase", [P, 512])
        cols = place("cols", [P, NCOLS])
        small = place("small", [P, 64])
        epsc = place("epsc", [P, 2])
        g_hi = place("g_hi", [P, 2, T], F32R, over="work", offset=18 * T)
        g_lo = place("g_lo", [P, 2, T], F32R, over="work", offset=20 * T)
        m_hi = place("m_hi", [P, KT, MEM], F32R, over="work", offset=16 * T)
        m_lo = place("m_lo", [P, KT, MEM], F32R, over="work", offset=18 * T)
        hi_as_f32 = act_hi[:, :, :].bitcast(F32)
        lo_free = place("lo_free", [P, 4, T], over="act_lo", offset=4 * T)
        hi_free = place("hi_free", [P, 4, T], over="act_hi", offset=4 * T)

        G = ctx.enter_context(nc.psum_tensor("products", [P, 2, T], F32))
        N = ctx.enter_context(nc.psum_tensor("others", [P, 2, T], F32))

        def const(name, n=None):
            c = CST[name]
            return cst[:, c:c + (n or 128)]

        keys = W[:, 20:22, :].rearrange("p a t -> p (a t)").rearrange("p (k m) -> p k m", m=MEM)
        values = W[:, 8:10, :]
        queries = W[:, 10:18, :]

        def col(name, k):
            return cols[:, COL[name] + k:COL[name] + k + 1]

        Wc = W[:, :, :].rearrange("p k (c t) -> p k c t", t=CH)
        hic = act_hi[:, :, :].rearrange("p k (c t) -> p k c t", t=CH)
        loc = act_lo[:, :, :].rearrange("p k (c t) -> p k c t", t=CH)
        hicf = hi_as_f32.rearrange("p k (c t) -> p k c t", t=CH)
        flat = W[:, :, :].rearrange("p k t -> p (k t)")
        tflat = TMP[:, :, :].rearrange("p k t -> p (k t)")
        sq = [TMP[:, 0, :], TMP[:, 1, :]]
        ssum, root = TMP[:, 2, :], TMP[:, 3, :]
        ident, ones, blk = const("ident"), const("ones"), const("blk")

        rowA, rowF, rowE, rowM = (TMP[:, n, :] for n in range(4))
        wq, wk, wv, wsT = (flat[:, 20 * T + 512 * n:20 * T + 512 * n + 512] for n in range(4))
        ml = lambda n, k=1: (flat[:, 512 * n:512 * (n + k)] if n < 8 else
                             flat[:, 8 * T + 512 * (n - 8):8 * T + 512 * (n - 8 + k)])
        heads = lambda v: v.rearrange("p (h t) -> p h t", h=NH)
        xcs, xvs, qT, qw, kT, kw, Wt, Pm = (heads(ml(n)) for n in range(8))
        winter, emm, Et, dn = (heads(ml(8 + n)) for n in range(4))
        vt = ml(12, 2).rearrange("p (h t) -> p h t", h=NH)
        Cst = ml(14, 2).rearrange("p (h t) -> p h t", h=NH)
        sel = phase[:, :].rearrange("p (h t) -> p h t", h=NH)
        bsb = place("bsb", [P, 2 * P])
        arow = place("arow", [P, P])
        bsv = bsb[:, :].rearrange("p (k t) -> p k t", k=2)
        Gf = G[:, :, :].rearrange("p a t -> p (a t)")
        Nf = N[:, :, :].rearrange("p a t -> p (a t)")
        Gb = [heads(Gf[:, 512 * n:512 * n + 512]) for n in range(4)]
        Nb = [heads(Nf[:, 512 * n:512 * n + 512]) for n in range(4)]

        hg_names = "b D1 Q1 K1 Eb0 K2 Q20 S lf vs vtok k2tok AT Eb1 Q21".split()

        def hg(names):
            out = []
            for name in names.split():
                n = hg_names.index(name)
                v = (tflat[:, 512 * n:512 * n + 512] if n < 8 else
                     hi_free[:, n // 2 - 3, 512 * (n % 2):512 * (n % 2) + 512] if n < 12 else
                     rstd[:, 512 * (n - 12):512 * (n - 11)] if n < 14 else hi_free[:, 3, 512:1024])
                out.append(heads(v))
            return out

        sw_q = hi_free[:, 0, 0:512].rearrange("p (k t) -> p k t", k=4)
        sw_kv = hi_free[:, 0, 512:1024].rearrange("p (a t) -> p a t", a=2)
        sw_v = hi_free[:, 3, 0:256]
        sw_pT = lo_free[:, 0:2, :].rearrange("p a t -> p (a t)")
        sw_pr = lo_free[:, 2:4, :].rearrange("p a t -> p (a t)")

        std_slots = [N[:, 0, :], N[:, 1, :], G[:, 0, :], G[:, 1, :]]
        mix_jobs = [(ones, 256, [W[:, 10, :], W[:, 11, :]]), (blk, 64, [W[:, 2, :]]), (blk, 64, [W[:, 3, :]])]
        hn_jobs = [(ones, P, [W[:, 4 + n, :]]) for n in range(4)]
        gm_tokens = hi_free[:, 2:4, :].rearrange("p a t -> p (a t)")

        block = ctx.enter_context(nc.Block())

        @block.sync
        def _(sp):
            def load(b, slot):
                sp.dma_start(w_raw[:, slot, :], ap["wstream"][b]).then_inc(s(f"weights_loaded{slot}"), 16)

            load(0, 0)
            load(1, 1)
            with sp.Fori(2, NBLOCKS - 1, 2) as b:
                for slot in range(2):
                    sp.wait_ge(s("weights_split"), b + slot - 1)
                    load(b + slot, slot)
            if NBLOCKS % 2:
                sp.wait_ge(s("weights_split"), NBLOCKS - 2)
                load(NBLOCKS - 1, 0)

        @block.gpsimd
        def _(pool):
            pool.memset(small[:, 63:64], 0.0).then_inc(s("pool_zero"), 1)
            pool.wait_ge(s("pool_zero"), 1)
            zeros = small[:, 63:64].to_broadcast([P, KT * P])

            made_elsewhere = [0]

            def split(b, turn, slot, high_from=None):
                if high_from is not None:
                    pool.wait_ge(s("kv_high"), b - high_from + 1)
                else:
                    pool.wait_ge(s(f"weights_loaded{slot}"), 16 * (turn + 1))
                    if not isinstance(b, int) or b >= 2:
                        pool.wait_ge(s("product_quarters"), 4 * (b - 1))
                    pool.tensor_tensor(w_hi[:, slot, :], w_raw[:, slot, :], zeros, ALU.add)\
                        .then_inc(s("weights_high"), 1)
                    pool.wait_ge(s("weights_high"), b + (1 - made_elsewhere[0]))
                pool.tensor_tensor(w_lo[:, slot, :], w_raw[:, slot, :], w_hi[:, slot, :].bitcast(F32),
                                   ALU.subtract).then_inc(s("weights_split"), 1)

            def relay(first, end, count0):
                pool.wait_ge(s("weights_split"), first)
                with pool.Fori(count0, count0 + end - first) as n:
                    pool.wait_ge(s("kv_low"), n + 1)
                    pool.sem_inc(s("weights_split"), 1)
                made_elsewhere[0] += end - first

            def split_blocks(first, end, high_from=None):
                with pool.Fori(0, (end - first) // 2) as i:
                    for j in range(2):
                        split(i * 2 + (first + j), i + (first + j) // 2, (first + j) % 2, high_from)
                if (end - first) % 2:
                    split(end - 1, (end - 1) // 2, (end - 1) % 2, high_from)
                if high_from is not None:
                    made_elsewhere[0] += end - first

            split(0, 0, 0)
            split(1, 0, 1)
            split_blocks(2, BLOCK0["k1"])
            relay(BLOCK0["k1"], BLOCK0["q1"], 0)
            split_blocks(BLOCK0["q1"], BLOCK0["k2"])
            split_blocks(BLOCK0["k2"], BLOCK0["v2"], BLOCK0["k2"] - KV0["2"])
            relay(BLOCK0["v2"], BLOCK0["q2"], 2 * KT)
            split_blocks(BLOCK0["q2"], BLOCK0["ffn2"] + 2)
            for k in range(KT):
                pool.wait_ge(s("px_y"), k + 1)
                pool.tensor_tensor(W[:, k, :], W[:, k, :], W[:, 8 + k, :], ALU.add).then_inc(s("px_h"), 1)
            split_blocks(BLOCK0["ffn2"] + 2, NBLOCKS)
            for k in range(1, KT, 2):
                pool.wait_ge(s("pf_y"), k + 1)
                pool.tensor_tensor(W[:, k, :], W[:, k, :], W[:, 8 + k, :], ALU.add).then_inc(s("pf_h_odd"), 1)

        @block.tensor
        def _(pe):
            def room(p):
                if not isinstance(p, int) or p >= 2:
                    pe.wait_ge(s("evacuated"), p - 1)

            def project(b, p, ws, ps, hi, lo, width=T, ready=None, beside=None):
                pe.wait_ge(s("weights_split"), b + 1)
                room(p)
                n = min(width, HALF)
                for k in range(KT):
                    if ready:
                        pe.wait_ge(*(ready(k) if callable(ready) else operand_count("operand_lo", ready, k + 1)))
                    w = slice(k * P, (k + 1) * P)
                    for h in range(width // n):
                        c = slice(h * n, (h + 1) * n)
                        for i, (a, x) in enumerate(((w_hi, hi), (w_hi, lo), (w_lo, hi))):
                            last = pe.matmul(G[:, ps, c], a[:, ws, w], x[:, k, c],
                                             start=(k == 0 and i == 0), stop=(k == KT - 1 and i == 2))
                    if beside:
                        beside(k)
                last.then_inc(s("product_quarters"), 4)

            def square_sum(name, k):
                pe.wait_ge(*norm("squares", name, k + 1))
                for h in range(2):
                    c = slice(h * HALF, (h + 1) * HALF)
                    last = pe.matmul(N[:, 0, c], ones, sq[k % 2][:, c], start=(k == 0), stop=(k == KT - 1))
                last.then_inc(s("squares_summed"), 1)
                if k == KT - 1:
                    pe.wait_ge(*norm("squares_summed", name, KT))
                    pe.sem_inc(s("token_sums"), 1)

            def gemm(name, n, ready, hi=act_hi, lo=act_lo, width=T, after_two=None, beside=None):
                b, p = BLOCK0[name], PROD0[name]
                peel = 2 + n % 2
                for j in range(peel):
                    project(b + j, p + j, (b + j) % 2, (p + j) % 2, hi, lo, width, ready if j == 0 else None,
                            beside if j == 0 else None)
                    if j == 1 and after_two:
                        after_two()
                with pe.Fori(peel, n, 2) as i:
                    for j in range(2):
                        project(i + (b + j), i + (p + j), (b + peel + j) % 2, (p + peel + j) % 2, hi, lo, width)

            def value_gemm(name):
                b, p = BLOCK0[name], PROD0[name]
                for g in range(2):
                    ps = (p + g) % 2
                    room(p + g)
                    for q in range(4):
                        ws = (b + 4 * g + q) % 2
                        pe.wait_ge(s("weights_split"), b + 4 * g + q + 1)
                        for m in range(2):
                            for k in range(2):
                                for n, (a, x) in enumerate(((m_hi, w_hi), (m_lo, w_hi), (m_hi, w_lo))):
                                    last = pe.matmul(G[:, ps, m * HALF:(m + 1) * HALF],
                                                     a[:, 2 * q + k, m * P:(m + 1) * P],
                                                     x[:, ws, k * HALF:(k + 1) * HALF],
                                                     start=(q == 0 and k == 0 and n == 0),
                                                     stop=(q == 3 and k == 1 and n == 2))
                        last.then_inc(s("product_quarters"), 4)

            def token_sums(name):
                pe.wait_ge(*norm("squares_summed", name, KT))
                for h in range(2):
                    c = slice(h * HALF, (h + 1) * HALF)
                    last = pe.matmul(N[:, 0, c], ones, ssum[:, c], start=True, stop=True)
                last.then_inc(s("token_sums"), 1)

            def norm_sums(name):
                return lambda: token_sums(name)

            def standardize(name, jobs, ready):
                _, done = STD0[name]
                for n, (m, _, tiles) in enumerate(jobs):
                    for wait in ready[n]:
                        pe.wait_ge(*wait)
                    for h in range(2):
                        c = slice(h * HALF, (h + 1) * HALF)
                        for t, tile in enumerate(tiles):
                            last = pe.matmul(std_slots[n][:, c], m, tile[:, c], start=(t == 0), stop=(t == len(tiles) - 1))
                    last.then_inc(s("std_mean"), 1)
                first = 0
                for n, (m, _, tiles) in enumerate(jobs):
                    pe.wait_ge(s("std_sq"), done + first + len(tiles))
                    for h in range(2):
                        c = slice(h * HALF, (h + 1) * HALF)
                        for t in range(len(tiles)):
                            last = pe.matmul(std_slots[n][:, c], m, hi_free[:, first + t, c], start=(t == 0),
                                             stop=(t == len(tiles) - 1))
                    last.then_inc(s("std_var"), 1)
                    first += len(tiles)

            def gmlp():
                pe.wait_ge(s("ln_out"), 2)
                for c in range(NCH):
                    for t in range(2):
                        last = pe.transpose(Gf[:, (2 * c + t) * P:(2 * c + t + 1) * P], W[:, 10 + t, c * CH:(c + 1) * CH], ident)
                last.then_inc(s("gm_turned"), 1)
                pe.wait_ge(s("gm_tokens"), 2)
                pe.wait_ge(s("ws_masked"), 1)
                for c in range(NCH):
                    for h in range(NH):
                        r = slice(64 * (h % 2), 64 * (h % 2) + 64)
                        last = pe.matmul(Nf[r, (h // 2) * T + c * CH:(h // 2) * T + (c + 1) * CH],
                                         gm_tokens[:, 256 * c + 64 * h:256 * c + 64 * h + 64],
                                         wsT[:, h * P:(h + 1) * P], start=True, stop=True)
                last.then_inc(s("gm_mixed"), 1)

            def mlstm():
                pe.wait_ge(s("ml_rows"), 1)
                pe.wait_ge(s("mix_in"), 80)
                pe.wait_ge(s("phase_in"), 16)
                pe.wait_ge(s("ml_init"), 2)

                def spread(c):
                    pe.wait_ge(s("ml_stage"), 3 * c + 3)
                    for n, row in ((2, rowF), (3, rowE)):
                        rc = row[0:NH, :].rearrange("p (c t) -> p c t", t=CH)
                        for h in range(NH):
                            pe.matmul(Nb[n][:, h, :], sel[0:NH, h, :], rc[:, c, :], start=True, stop=True)
                    rc = rowM[0:NH, :].rearrange("p (c t) -> p c t", t=CH)
                    for h in range(NH):
                        pe.matmul(Nb[0][:, h, :], arow[0:NH, :], sel[0:NH, h, :], start=True, stop=False)
                        last = pe.matmul(Nb[0][:, h, :], sel[0:NH, h, :], rc[:, c, :], start=False, stop=True)
                    last.then_inc(s("ml_spread"), 1)

                def chunk(c, ahead=True):
                    pe.wait_ge(s("ml_h"), c + 1)
                    for n, a in enumerate((wq, wk)):
                        for h in range(NH):
                            last = pe.matmul(Gb[n][:, h, :], heads(a)[:, h, :], xvs[:, h, :], start=True, stop=True)
                    last.then_inc(s("ml_proj"), 1)
                    pe.wait_ge(s("ml_kept"), c + 1)
                    for n, (a, x) in enumerate(((xvs, wk), (xcs, wv))):
                        for h in range(NH):
                            last = pe.matmul(Gb[2 + n][:, h, :], a[:, h, :], heads(x)[:, h, :], start=True, stop=True)
                    last.then_inc(s("ml_proj"), 1)
                    pe.wait_ge(s("ml_qkv"), 3 * c + 2)
                    for h in range(NH):
                        last = pe.matmul(Nb[1][:, h, :], kT[:, h, :], qT[:, h, :], start=True, stop=True)
                    last.then_inc(s("ml_scores"), 1)
                    pe.wait_ge(s("ml_qkv"), 3 * c + 3)
                    pe.wait_ge(s("ml_weighted"), 3 * c + 3)
                    for h in range(NH):
                        pe.matmul(Gb[0][:, h, :], vt[:, h, 0:P], Pm[:, h, :], start=True, stop=False)
                        pe.matmul(Gb[0][:, h, :], Cst[:, h, 0:P], qw[:, h, :], start=False, stop=True)
                    for h in range(NH):
                        pe.matmul(Gb[1][:, h, :], ones, Pm[:, h, :], start=True, stop=False)
                        last = pe.matmul(Gb[1][:, h, :], Cst[:, h, P:2 * P], qw[:, h, :], start=False, stop=True)
                    last.then_inc(s("ml_num"), 1)
                    for h in range(NH):
                        last = pe.matmul(Gf[:, T + 256 * h:T + 256 * h + 256], kw[:, h, :], vt[:, h, :], start=True, stop=True)
                    last.then_inc(s("ml_update"), 1)
                    if ahead:
                        spread(c + 1)

                spread(0)
                with pe.Fori(0, NCH - 1) as c:
                    chunk(c)
                chunk(NCH - 1, False)

            def memory_sums(x):
                def run():
                    pe.wait_ge(s(x + "_mem_sq"), 1)
                    for k in range(KT):
                        last = pe.matmul(N[:, 1, 0:MEM], ones, flat[:, 12 * T + k * MEM:12 * T + (k + 1) * MEM],
                                         start=(k == 0), stop=(k == KT - 1))
                    last.then_inc(s(x + "_mem_sums"), 1)
                return run

            def cross(x):
                qs = [TMP[:, n, :].rearrange("p (k t) -> p k t", k=KT) for n in (0, 3)]
                score_slots = [Nf[:, 0:T], G[:, 1, :]]
                p_, pT = TMP[:, 1, :], TMP[:, 2, :].rearrange("p (k t) -> p k t", k=KT)

                def scores(c, slot):
                    pe.wait_ge(s("xa_q_staged"), c + 1 + XA0[x])
                    for h in range(NH):
                        for k in range(2):
                            last = pe.matmul(score_slots[slot][:, MEM * h:MEM * (h + 1)], qs[slot][:, 2 * h + k, :],
                                             keys[:, 2 * h + k, :], start=(k == 0), stop=(k == 1))
                    last.then_inc(s("xa_scores"), 1)

                def chunk(c, slot, ahead=True):
                    pe.wait_ge(s("xa_probs"), c + 1 + XA0[x])
                    for n in range(8):
                        last = pe.transpose(N[:, 1, n * P:(n + 1) * P], p_[:, n * P:(n + 1) * P], ident)
                    last.then_inc(s("xa_turned"), 1)
                    if ahead:
                        scores(c + 2, slot)
                    pe.wait_ge(s("xa_pT"), c + 1 + XA0[x])
                    pe.wait_ge(s("xa_o_lo"), c + 1 + XA0[x])
                    for k in range(KT):
                        for m in range(2):
                            last = pe.matmul(G[:, 0, k * P:(k + 1) * P], values[:, m, k * P:(k + 1) * P],
                                             pT[:, 2 * (k // 2) + m, :], start=(m == 0), stop=(m == 1))
                    last.then_inc(s("xa_out"), 1)

                pe.wait_ge(s("evacuated"), PROD0["xo" + x])
                scores(0, 0)
                scores(1, 1)
                with pe.Fori(0, (NCH - 2) // 2) as i:
                    for n in range(2):
                        chunk(i * 2 + n, n)
                chunk(NCH - 2, 0, False)
                chunk(NCH - 1, 1, False)

            def ffn(name):
                b, p = BLOCK0[name], PROD0[name]

                def up(b, p, par, after_two=None, ready=None, beside=None):
                    for j in range(4):
                        project(b + j, p + j, (par[0] + j) % 2, (par[1] + j) % 2, act_hi, act_lo, T, ready if j == 0 else None,
                                beside if j == 0 else None)
                        if j == 1 and after_two:
                            after_two()

                def down(b, p, par, c):
                    for j in range(2):
                        pe.wait_ge(s("weights_split"), b + (j + 1))
                        for o in range(4):
                            room(p + (4 * j + o))
                            if j == 0 and o == 0:
                                pe.wait_ge(s("ff_g_lo"), 2 * c + 2 + FF0[name])
                            ws, ps = (par[0] + j) % 2, (par[1] + o) % 2
                            for k in range(2):
                                w = slice((2 * o + k) * P, (2 * o + k + 1) * P)
                                for h in range(2):
                                    t = slice(h * HALF, (h + 1) * HALF)
                                    for i, (a, x) in enumerate(((w_hi, g_hi), (w_hi, g_lo), (w_lo, g_hi))):
                                        last = pe.matmul(G[:, ps, t], a[:, ws, w], x[:, k, t],
                                                         start=(k == 0 and i == 0), stop=(k == 1 and i == 2))
                            last.then_inc(s("product_quarters"), 1)

                if name == "ffn2":
                    up(b, p, (b, p), None, name, lambda k: square_sum(name, k))
                else:
                    up(b, p, (b, p), norm_sums(name), name)
                with pe.Fori(1, FC) as c:
                    up(c * 6 + (b - 2), c * 12 + (p - 8), (b, p))
                    down(c * 6 + (b + 2), c * 12 + (p - 4), (b, p), c - 1)
                down(b + 6 * FC - 2, p + 12 * FC - 8, (b, p), FC - 1)

            def mixer2():
                Q1, K1, K2, vs, AT, vtok, k2tok, S, *Q2 = hg("Q1 K1 K2 vs AT vtok k2tok S Q20 Q21")
                pe.wait_ge(s("evacuated"), PROD0["out2"])
                pe.wait_ge(s("hg_init"), 1)

                def scores(c):
                    pe.wait_ge(s("sw_staged"), 4 * c + 4)
                    pe.wait_ge(s("hg_kept"), c + 1)
                    for g in range(2):
                        for i in range(4):
                            n = 4 * g + i
                            last = pe.matmul(Nf[:, n * 256:(n + 1) * 256], sw_q[64 * g:64 * g + 64, i, :],
                                             sw_kv[64 * g:64 * g + 64, 0, :], start=True, stop=True)
                        last.then_inc(s("sw_scores"), 1)

                def turn_values():
                    for n in range(2):
                        last = pe.transpose(Gb[3][:, n, :], sw_kv[:, 1, n * P:(n + 1) * P], ident)
                    last.then_inc(s("sw_v_turned"), 1)

                def turn_hgrn(c):
                    pe.wait_ge(s("hg_v"), c + 1)
                    for h in range(NH):
                        pe.transpose(Gb[1][:, h, :], vs[:, h, :], ident)
                    pe.wait_ge(s("hg_qk"), 4 * c + 4)
                    for h in range(NH):
                        last = pe.transpose(Gb[2][:, h, :], K2[:, h, :], ident)
                    last.then_inc(s("hg_turned"), 1)

                def chunk(c, odd, ahead=True):
                    pe.wait_ge(s("sw_o_lo"), c + 1)
                    for h in range(NH):
                        last = pe.matmul(Gb[0][:, h, :], K1[:, h, :], Q1[:, h, :], start=True, stop=True)
                    last.then_inc(s("hg_scores"), 1)
                    pe.wait_ge(s("sw_negmax"), 2 * c + 1)
                    pe.wait_ge(s("hg_masked"), c + 1)
                    pe.wait_ge(s("hg_tokens"), 2 * c + 2)
                    for h in range(NH):
                        pe.matmul(Nb[1][:, h, :], vtok[:, h, :], AT[:, h, :], start=(h == 0), stop=False, skip_group_check=True)

                    def inter(sub):
                        r = slice(64 * sub, 64 * sub + 64)
                        for h in range(NH):
                            pe.matmul(Nb[1][:, h, r], S[:, h, :], Q2[odd][:, h, r], start=False, stop=(sub == 1 and h == 3),
                                      skip_group_check=True)
                        pe.wait_ge(s("sw_negmax"), 2 * c + 2)
                        for h in range(NH):
                            last = pe.matmul(Nb[2 + sub][:, h, :], k2tok[r, h, :], vtok[r, h, :], start=True, stop=True)
                        last.then_inc(s("hg_update"), 1)

                    inter(0)
                    pe.wait_ge(s("sw_v"), c + 1)
                    for g in range(2):
                        pe.wait_ge(s("sw_probs"), 2 * c + (g + 1))
                        for n in range(8 * g, 8 * g + 8):
                            last = pe.transpose(Gf[:, n * P:(n + 1) * P], sw_pr[:, n * P:(n + 1) * P], ident)
                        last.then_inc(s("sw_turned"), 1)
                    pe.wait_ge(s("hg_S"), 2 * c + 2)
                    inter(1)
                    pe.wait_ge(s("hg_S"), 2 * c + 3)
                    pe.wait_ge(s("sw_pT"), 2 * c + 2)
                    for g in range(2):
                        for i in range(4):
                            n = 4 * g + i
                            for m in range(2):
                                last = pe.matmul(Gf[64 * g:64 * g + 64, i * P:(i + 1) * P],
                                                 sw_v[:, m * P + 64 * g:m * P + 64 * g + 64],
                                                 sw_pT[:, (2 * n + m) * P:(2 * n + m + 1) * P], start=(m == 0), stop=(m == 1))
                    last.then_inc(s("sw_pv"), 1)
                    if ahead:
                        scores(c + 1)
                        turn_values()
                        turn_hgrn(c + 1)

                scores(0)
                turn_values()
                turn_hgrn(0)
                chunk(0, 0)
                with pe.Fori(0, NCH // 2 - 1) as i:
                    for n in (1, 2):
                        chunk(i * 2 + n, n % 2)
                chunk(NCH - 1, 1, False)

            pe.wait_ge(s("consts"), 32)
            gemm("z1", 17, "z1", beside=lambda k: square_sum("z1", k))
            standardize("mix", mix_jobs, [[(s("gelus"), 4)], [(s("cb_done"), 1)],
                                          [(s("cb_done"), 2), (s("evacuated"), PROD0["out1"])]])
            gmlp()
            mlstm()
            pe.wait_ge(s("ml_kept"), NCH + 1)
            standardize("hn", hn_jobs, [[(s("ml_h"), NCH + 1)]] * 4)
            pe.wait_ge(s("std_root"), STD0["hn"][0] + 1)
            gemm("out1", 8, lambda k: (s("y1_lo"), max(4, k + 1)), after_two=memory_sums("1"))

            def attention(x):
                gemm("k" + x, 8, "m" + x, m_hi, m_lo, MEM)
                value_gemm("v" + x)
                gemm("q" + x, 8, "q" + x, after_two=norm_sums("q" + x))
                cross(x)
                pe.wait_ge(s("xa_o_lo"), NCH + 1 + XA0[x])
                gemm("xo" + x, 8, None)

            attention("1")
            ffn("ffn1")
            norm_sums("final")()
            gemm("z2", 22, "z2", beside=lambda k: square_sum("z2", k))
            mixer2()
            pe.wait_ge(s("sw_o_lo"), NCH + 1)
            pe.wait_ge(s("hg_kept"), NCH + 1)
            pe.wait_ge(s("hg_squares"), NCH)
            for n in range(4):
                for h in range(2):
                    c = slice(h * HALF, (h + 1) * HALF)
                    last = pe.matmul(std_slots[n][:, c], ones, W[:, 16 + n, c], start=True, stop=True)
                last.then_inc(s("hr_sums"), 1)
            pe.wait_ge(s("hr_root"), 1)
            gemm("out2", 8, lambda k: (s("y2_lo"), max(1, k - 3)), after_two=memory_sums("2"))
            norm_sums("pm")()
            attention("2")
            norm_sums("px")()
            ffn("ffn2")
            norm_sums("pf")()

        @block.scalar
        def _(act):
            chain = Chain(act, s("act_chain"))

            def apart():
                act.wait_ge(s("consts"), 32)

            def squares(name, src, ready, before_last=None):
                for k in range(KT):
                    if k == KT - 1 and before_last:
                        before_last()
                    act.wait_ge(*ready(k))
                    if k >= 2:
                        act.wait_ge(*norm("squares_summed", name, k - 1))
                    act.activation(sq[k % 2], src(k), ACT.Square).then_inc(s("squares"), 1)

            def roots(name):
                act.wait_ge(*norm("token_sums", name, 1, 1))
                chain.link(act.activation(root, N[:, 0, :], ACT.Ln, bias=epsc[:, 0:1], scale=1.0 / D))
                act.activation(rstd[:, :], root, ACT.Exp, scale=-0.5).then_inc(s("roots"), 1)

            def weights_high(x, n):
                b = BLOCK0["k" + x] + n
                act.wait_ge(s(f"weights_loaded{b % 2}"), 16 * (b // 2 + 1))
                act.wait_ge(s("product_quarters"), 4 * (b - 1))
                act.activation(w_hi[:, b % 2, :], w_raw[:, b % 2, :], ACT.Copy).then_inc(s("kv_high"), 1)

            def split_high(name, src, gain, ready=None, beside=None):
                for k in range(KT):
                    if beside:
                        beside(k)
                    if ready:
                        act.wait_ge(*ready(k))
                    act.activation(act_hi[:, k, :], src(k), ACT.Identity, scale=col(gain, k)).then_inc(s("operand_hi"), 1)

            def standardize(name, jobs):
                job0, done = STD0[name]
                for t in range(sum(len(tiles) for _, _, tiles in jobs)):
                    act.wait_ge(s("std_centred"), done + t + 1)
                    tile = [tile for _, _, tiles in jobs for tile in tiles][t]
                    act.activation(hi_free[:, t, :], tile, ACT.Square).then_inc(s("std_sq"), 1)
                for n, (_, size, _) in enumerate(jobs):
                    act.wait_ge(s("std_var"), job0 + n + 1)
                    chain.link(act.activation(lo_free[:, n, :], std_slots[n], ACT.Ln, bias=epsc[:, 1:2], scale=1.0 / size))
                for n in range(len(jobs)):
                    act.activation(lo_free[:, n, :], lo_free[:, n, :], ACT.Exp, scale=-0.5).then_inc(s("std_root"), 1)

            def load(dst, src, name):
                act.dma_start(dst, src).then_inc(s(name), 16)

            load(cst[:, :], ap["consts"][:, 0:NKEPT], "consts")
            load(cols[:, :], ap["cols"], "consts")
            for k in range(KT):
                load(W[:, k, :], ap["xT"][:, k, :], f"x_in{k}")
            load(phase[:, :], ap["consts"][:, CST["sel"]:CST["sel"] + 512], "phase_in")
            load(wq, ap["w_q"], "mix_in")
            load(wk, ap["w_k"], "mix_in")
            load(wv, ap["w_v"], "mix_in")
            load(wsT, ap["w_sT"], "mix_in")
            load(bsb[:, :], ap["b_s"], "mix_in")
            act.wait_ge(s("consts"), 32)
            act.wait_ge(s("eps"), 2)
            for k in range(KT):
                act.wait_ge(s(f"x_in{k}"), 16)
                act.activation(act_hi[:, k, :], W[:, k, :], ACT.Identity, scale=col("mix1", k)).then_inc(s("operand_hi"), 1)
                if k >= 2:
                    act.wait_ge(*norm("squares_summed", "z1", k - 1))
                act.activation(sq[k % 2], W[:, k, :], ACT.Square).then_inc(s("squares"), 1)
            roots("z1")
            E0 = PROD0["z1"]
            act.wait_ge(s("row_forget"), 1)
            act.activation(rowE[0:NH, :], rowF[0:NH, :], ACT.Abs).then_inc(s("row_abs"), 1)
            act.wait_ge(s("row_abs"), 1)
            chain.link(act.activation(rowE[0:NH, :], rowE[0:NH, :], ACT.Exp, scale=-1.0))
            act.activation(rowE[0:NH, :], rowE[0:NH, :], ACT.Ln, bias=1.0).then_inc(s("row_log"), 1)
            for n in range(2):
                act.wait_ge(s("evacuated"), E0 + 4 + n)
                act.activation(W[:, 2 + n, :], W[:, 2 + n, :], ACT.Sigmoid).then_inc(s("cf_gate"), 1)
            for n in range(4):
                act.wait_ge(s("cc_done"), n + 1)
                act.activation(W[:, 16 + n, :], W[:, 16 + n, :], ACT.Silu).then_inc(s("xconv"), 1)
            for n in range(4):
                act.wait_ge(s("evacuated"), E0 + 10 + n)
                act.activation(W[:, 8 + n, :], W[:, 8 + n, :], ACT.Gelu).then_inc(s("gelus"), 1)
            for n in range(4):
                act.wait_ge(s("evacuated"), E0 + 14 + n)
                act.activation(W[:, 12 + n, :], W[:, 12 + n, :], ACT.Sigmoid).then_inc(s("ogate"), 1)

            act.wait_ge(s("evacuated"), PROD0["out1"])
            standardize("mix", mix_jobs)
            for n in range(2):
                act.wait_ge(s("std_scaled"), n + 1)
                act.activation(W[:, 10 + n, :], W[:, 10 + n, :], ACT.Identity, scale=col("lna_g", n), bias=col("lna_b", n))\
                   .then_inc(s("ln_out"), 1)
            for n in range(2):
                act.wait_ge(s("std_scaled"), n + 3)
                act.activation(W[:, 2 + n, :], W[:, 2 + n, :], ACT.Silu, scale=col("gnb_g", n), bias=col("gnb_b", n))\
                   .then_inc(s("cf_out"), 1)
            act.wait_ge(s("gm_turned"), 1)
            for n in range(2):
                act.activation(hi_free[:, 2 + n, :], G[:, n, :], ACT.Copy).then_inc(s("gm_tokens"), 1)
            act.wait_ge(s("cf_out"), 2)
            for n in range(2):
                act.activation(act_hi[:, 2 + n, :], W[:, 2 + n, :], ACT.Copy).then_inc(s("y1_hi"), 1)
            for n in range(2):
                act.wait_ge(s("gm_y"), n + 1)
                act.activation(act_hi[:, n, :], W[:, n, :], ACT.Copy).then_inc(s("y1_hi"), 1)

            act.wait_ge(s("ml_free"), 1)
            act.wait_ge(s("xconv"), 4)
            rowAc = rowA[0:NH, :].rearrange("p (c t) -> p c t", t=CH)

            def stage(c):
                act.activation(xvs, Wc[:, 16:20, c, :], ACT.Copy).then_inc(s("ml_stage"), 1)
                act.activation(xcs, Wc[:, 4:8, c, :], ACT.Copy).then_inc(s("ml_stage"), 1)
                act.activation(arow[0:NH, :], rowAc[:, c, :], ACT.Copy).then_inc(s("ml_stage"), 1)

            def mlstm(c, ahead=True):
                act.wait_ge(s("ml_kept"), c + 1)
                act.wait_ge(s("ml_spread"), c + 1)
                act.activation(winter, Nb[2], ACT.Exp).then_inc(s("ml_exp"), 1)
                act.activation(emm, Nb[3], ACT.Exp).then_inc(s("ml_exp"), 1)
                act.wait_ge(s("ml_proj"), 2 * c + 1)
                act.activation(qT, Gb[0], ACT.Copy, scale=float(P) ** -0.5).then_inc(s("ml_qkv"), 1)
                act.activation(kT, Gb[1], ACT.Copy).then_inc(s("ml_qkv"), 1)
                act.wait_ge(s("ml_bounded"), c + 1)
                act.activation(Wt, Et, ACT.Exp).then_inc(s("ml_exp"), 1)
                act.wait_ge(s("ml_proj"), 2 * c + 2)
                act.activation(vt[:, :, 0:P], Gb[3], ACT.Copy).then_inc(s("ml_qkv"), 1)
                if ahead:
                    stage(c + 1)
                act.wait_ge(s("ml_num"), c + 1)
                act.activation(dn, Gb[1], ACT.Abs).then_inc(s("ml_den"), 1)

            stage(0)
            with act.Fori(0, NCH - 1) as c:
                mlstm(c)
            mlstm(NCH - 1, False)

            standardize("hn", hn_jobs)
            for n in range(4):
                act.wait_ge(s("ml_y"), n + 1)
                act.activation(act_hi[:, 4 + n, :], W[:, 4 + n, :], ACT.Copy).then_inc(s("y1_hi"), 1)
            act.wait_ge(s("y1_lo"), 8)

            def memory(x):
                mem = flat[:, 20 * T:22 * T]
                act.wait_ge(s(x + "_mem_in"), 16)
                act.activation(flat[:, 12 * T:14 * T], mem, ACT.Square).then_inc(s(x + "_mem_sq"), 1)
                act.wait_ge(s(x + "_mem_sums"), 1)
                chain.link(act.activation(W[:, 14, 0:MEM], N[:, 1, 0:MEM], ACT.Ln, bias=epsc[:, 0:1], scale=1.0 / D))
                act.activation(W[:, 14, 0:MEM], W[:, 14, 0:MEM], ACT.Exp, scale=-0.5).then_inc(s(x + "_mem_root"), 1)
                act.wait_ge(s(x + "_mem_scaled"), 1)
                for k in range(KT):
                    act.activation(m_hi[:, k, :], mem[:, k * MEM:(k + 1) * MEM], ACT.Identity, scale=col("mem" + x, k))\
                       .then_inc(s(x + "_mem_hi"), 1)

            def cross(x):
                qs = [TMP[:, n, :].rearrange("p (k t) -> p k t", k=KT) for n in (0, 3)]
                score_slots = [Nf[:, 0:T], G[:, 1, :]]
                pr, pT = TMP[:, 1, :], TMP[:, 2, :]
                queries_c = queries.rearrange("p k (c t) -> p k c t", t=CH)

                def stage(c, slot):
                    act.activation(qs[slot], queries_c[:, :, c, :], ACT.Copy).then_inc(s("xa_q_staged"), 1)

                def exps(c, slot):
                    act.wait_ge(s("xa_negmax"), c + 1 + XA0[x])
                    for h in range(NH):
                        last = act.activation(pr[:, h * MEM:(h + 1) * MEM], score_slots[slot][:, h * MEM:(h + 1) * MEM],
                                              ACT.Exp, bias=small[:, 4 + 12 * slot + h:5 + 12 * slot + h],
                                              accum_out=small[:, 8 + h:9 + h])
                    last.then_inc(s("xa_exps"), 1)

                def chunk(c, slot, ahead=3):
                    act.wait_ge(s("xa_turned"), c + 1 + XA0[x])
                    act.activation(pT, N[:, 1, :], ACT.Copy).then_inc(s("xa_pT"), 1)
                    if ahead:
                        exps(c + 1, 1 - slot)
                    if ahead == 3:
                        stage(c + 3, 1 - slot)
                    act.wait_ge(s("xa_out"), c + 1 + XA0[x])
                    apart()
                    act.activation(hic[:, :, c, :], G[:, 0, :].rearrange("p (k t) -> p k t", k=KT), ACT.Copy)\
                       .then_inc(s("xa_o_hi"), 1)

                act.wait_ge(s("evacuated"), PROD0["xo" + x])
                stage(0, 0)
                stage(1, 1)
                exps(0, 0)
                stage(2, 0)
                with act.Fori(0, NCH // 2 - 2) as i:
                    for n in range(2):
                        chunk(i * 2 + n, n)
                for c in range(NCH - 4, NCH):
                    chunk(c, c % 2, min(3, NCH - 1 - c))

            def ffn(name, two_tile_function):
                def hidden(c):
                    for j in range(2):
                        act.wait_ge(s("ff_gate_in"), 2 * c + j + 1 + FF0[name])
                        act.activation(W[:, 16 + j, :], W[:, 16 + j, :] if name == "ffn1" else TMP[:, j, :],
                                       two_tile_function).then_inc(s("ff_gate"), 1)
                    q = s("product_quarters")
                    if not isinstance(c, int):
                        act.wait_ge(q, c * 24 + 4 * (BLOCK0[name] + 4))
                    elif c:
                        act.wait_ge(q, 24 * c + 4 * (BLOCK0[name] + 4))
                    for j in range(2):
                        act.wait_ge(s("ff_hidden"), 2 * c + j + 1 + FF0[name])
                        act.activation(g_hi[:, j, :], W[:, 16 + j, :], ACT.Copy).then_inc(s("ff_g_hi"), 1)

                hidden(0)
                with act.Fori(1, FC) as c:
                    hidden(c)

            ev = lambda name: (lambda k: (s("evacuated"), PROD0[name] + k + 1))
            h_tile = lambda k: W[:, k, :]
            y_tile = lambda k: W[:, 8 + k, :]
            for k in range(KT):
                load(W[:, k, :], ap["xT"][:, k, :], f"x_in{k}")
            load(W[:, 20:22, :], ap["memT1"], "1_mem_in")
            memory("1")
            squares("q1", h_tile, ev("out1"), lambda: weights_high("1", 0))
            split_high("q1", h_tile, "x1", lambda k: (s("evacuated"), PROD0["k1"]), lambda k: weights_high("1", k) if k else None)
            for n in range(KT, 2 * KT):
                weights_high("1", n)
            roots("q1")
            cross("1")
            squares("ffn1", h_tile, ev("xo1"))
            split_high("ffn1", h_tile, "ffn1", lambda k: (s("evacuated"), PROD0["ffn1"]))
            roots("ffn1")
            ffn("ffn1", ACT.Gelu)
            last_tile = lambda k: (s("evacuated"), PROD0["z2"] - KT + k + 1)
            squares("final", h_tile, last_tile)
            roots("final")
            load(phase[:, :], ap["consts"][:, CST["hg_reset"]:CST["hg_reset"] + 512], "phase2_in")
            for k in range(KT):
                act.wait_ge(s("h_final"), k + 1)
                act.activation(act_hi[:, k, :], W[:, k, :], ACT.Identity, scale=col("mix2", k)).then_inc(s("operand_hi"), 1)
                if k >= 2:
                    act.wait_ge(*norm("squares_summed", "z2", k - 1))
                act.activation(sq[k % 2], W[:, k, :], ACT.Square).then_inc(s("squares"), 1)
                act.wait_ge(*norm("squares", "z2", k + 1))
                load(ap["parked"][:, k, :], W[:, k, :], "parked")
            roots("z2")
            for n in range(22):
                if n < 8 or 12 <= n < 16:
                    act.wait_ge(s("evacuated"), PROD0["z2"] + n + 1)
                    act.activation(W[:, n, :], W[:, n, :], ACT.Sigmoid if 4 <= n < 8 else ACT.Silu)\
                       .then_inc(s("z2_act"), 1)
                if n == 7:
                    act.wait_ge(s("lb_diff"), 1)
                    act.activation(small[:, 48:52], small[:, 48:52], ACT.Exp).then_inc(s("lb_exp"), 1)
            act.wait_ge(s("evacuated"), PROD0["out2"])
            lf, b_, D1, E1, E1n, K2, vs, vtok, k2tok, *Eb = hg("lf b D1 Q1 K1 K2 vs vtok k2tok Eb0 Eb1")

            def stage_window(c):
                act.activation(sw_q, Wc[:, 16:20, c, :], ACT.Copy).then_inc(s("sw_staged"), 1)
                before = c if isinstance(c, int) and c == 0 else c - 1
                act.activation(sw_kv[:, :, 0:P], Wc[:, 20:22, before, :], ACT.Copy).then_inc(s("sw_staged"), 1)
                act.activation(sw_kv[:, 0, P:2 * P], Wc[:, 20, c, :], ACT.Copy).then_inc(s("sw_staged"), 1)
                act.activation(sw_kv[:, 1, P:2 * P], Wc[:, 21, c, :], ACT.Copy).then_inc(s("sw_staged"), 1)

            def logs(c):
                if not isinstance(c, int) or c:
                    act.wait_ge(s("hg_scores"), c)
                    apart()
                act.activation(lf, Wc[:, 4:8, c, :], ACT.Ln).then_inc(s("hg_log"), 1)
                act.activation(vs, Wc[:, 8:12, c, :], ACT.Copy).then_inc(s("hg_v"), 1)

            def exponentials(c, odd):
                act.wait_ge(s("hg_d"), 2 * c + 1)
                act.activation(E1, D1, ACT.Exp).then_inc(s("hg_exp"), 1)
                act.activation(E1n, D1, ACT.Exp, scale=-1.0).then_inc(s("hg_exp"), 1)
                act.activation(Eb[odd], b_, ACT.Exp).then_inc(s("hg_exp"), 1)
                act.wait_ge(s("hg_d"), 2 * c + 2)
                act.activation(K2, K2, ACT.Exp).then_inc(s("hg_exp"), 1)

            def mixer2(c, odd, ahead=True):
                act.wait_ge(s("sw_v_turned"), c + 1)
                act.activation(sw_v, Gf[:, 3 * HALF:3 * HALF + 256], ACT.Copy).then_inc(s("sw_v"), 1)
                act.wait_ge(s("hg_turned"), c + 1)
                act.activation(vtok, Gb[1], ACT.Copy).then_inc(s("hg_tokens"), 1)
                act.activation(k2tok, Gb[2], ACT.Copy).then_inc(s("hg_tokens"), 1)
                for g in range(2):
                    act.wait_ge(s("sw_negmax"), 2 * c + (g + 1))
                    for n in range(4 * g, 4 * g + 4):
                        act.activation(sw_pr[:, n * 256:(n + 1) * 256], sw_pr[:, n * 256:(n + 1) * 256], ACT.Exp,
                                       bias=small[:, 8 + n:9 + n], accum_out=small[:, 16 + n:17 + n])
                    act.activation(small[:, 24 + 4 * g:28 + 4 * g], small[:, 32 + 4 * g:36 + 4 * g], ACT.Exp)\
                       .then_inc(s("sw_exps"), 1)
                if ahead:
                    stage_window(c + 1)
                    logs(c + 1)
                for n in range(2):
                    act.wait_ge(s("sw_turned"), 2 * c + (n + 1))
                    act.activation(sw_pT[:, n * T:(n + 1) * T], G[:, n, :], ACT.Copy).then_inc(s("sw_pT"), 1)
                if ahead:
                    exponentials(c + 1, 1 - odd)
                act.wait_ge(s("sw_pv"), c + 1)
                apart()
                act.activation(hic[:, 0:4, c, :], Gb[0], ACT.Copy).then_inc(s("sw_o_hi"), 1)
                act.wait_ge(s("hg_kept"), c + 2)
                apart()
                act.activation(Wc[:, 16:20, c, :], Wc[:, 0:4, c, :], ACT.Square).then_inc(s("hg_squares"), 1)

            stage_window(0)
            logs(0)
            exponentials(0, 0)
            mixer2(0, 0)
            with act.Fori(0, NCH // 2 - 1) as i:
                for n in (1, 2):
                    mixer2(i * 2 + n, n % 2)
            mixer2(NCH - 1, 1, False)
            load(W[:, 20:22, :], ap["memT2"], "2_mem_in")
            for n in range(4):
                act.wait_ge(s("hr_sums"), n + 1)
                chain.link(act.activation(W[:, 16 + n, :], std_slots[n], ACT.Ln, bias=epsc[:, 0:1], scale=1.0 / P))

            def hgrn_root(n):
                act.activation(W[:, 16 + n, :], W[:, 16 + n, :], ACT.Exp, scale=-0.5).then_inc(s("hr_root"), 1)

            hgrn_root(0)
            for n in range(4):
                if n < 3:
                    hgrn_root(n + 1)
                act.wait_ge(s("hr_y"), n + 1)
                act.activation(act_hi[:, 4 + n, :], W[:, n, :], ACT.Copy).then_inc(s("y2_hi"), 1)
            act.wait_ge(s("y2_lo"), 4)
            act.wait_ge(s("parked"), 16 * KT)
            for k in range(KT):
                load(W[:, k, :], ap["parked"][:, k, :], f"x_in{k}")

            def post(name, nxt, gain, src_done, before_last=None, beside=None):
                squares(name, y_tile, src_done, before_last)
                roots(name)
                for k in range(KT):
                    if beside:
                        beside(k)
                    act.wait_ge(s(name + "_h"), k + 1)
                    act.activation(act_hi[:, k, :], W[:, k, :], ACT.Identity, scale=col(gain, k)).then_inc(s("operand_hi"), 1)
                    if k >= 2:
                        act.wait_ge(*norm("squares_summed", nxt, k - 1))
                    act.activation(sq[k % 2], W[:, k, :], ACT.Square).then_inc(s("squares"), 1)

            memory("2")
            post("pm", "q2", "x2", ev("out2"), lambda: weights_high("2", 0),
                 lambda k: weights_high("2", k) if k else None)
            for n in range(KT, 2 * KT):
                weights_high("2", n)
            roots("q2")
            cross("2")
            post("px", "ffn2", "ffn2", ev("xo2"))
            roots("ffn2")
            ffn("ffn2", ACT.Silu)
            squares("pf", y_tile, lambda k: (s("evacuated"), PROD0["ffn2"] + 12 * FC - KT + k + 1))
            roots("pf")
            for k in range(KT):
                act.wait_ge(s("pf_h_odd" if k % 2 else "pf_h"), k // 2 + 1)
                load(ap["out"][:, k, :], W[:, k, :], "stored")
            act.wait_ge(s("stored"), 16 * KT)

        @block.vector
        def _(dve):
            chain = Chain(dve, s("dve_chain"))
            link = chain.link

            def product(name, j, width=None):
                dve.wait_ge(s("product_quarters"), 4 * (j + (BLOCK0[name] + 1)) if not isinstance(j, int) else
                            4 * (BLOCK0[name] + 1 + j))

            def slot(name, j):
                return G[:, (PROD0[name] + j) % 2, :]

            def sums(name, k):
                dve.wait_ge(*norm("squares", name, k + 1))
                if k:
                    dve.wait_ge(*norm("squares_summed", name, k))
                    dve.tensor_tensor(ssum, ssum, sq[k % 2], ALU.add).then_inc(s("squares_summed"), 1)
                else:
                    dve.tensor_copy(ssum, sq[0]).then_inc(s("squares_summed"), 1)

            def have_rstd(name):
                dve.wait_ge(*norm("roots", name, 1, 1))

            def split_low(name, k, src, gain):
                dve.wait_ge(*operand_count("operand_hi", name, k + 1))
                dve.scalar_tensor_tensor(act_lo[:, k, :], src(k), col(gain, k), hi_as_f32[:, k, :], ALU.mult,
                                         ALU.subtract).then_inc(s("operand_lo"), 1)

            def low(name, k, tile, hi_count):
                dve.wait_ge(s(name + "_hi"), hi_count)
                dve.tensor_tensor(act_lo[:, k, :], tile, hi_as_f32[:, k, :], ALU.subtract).then_inc(s(name + "_lo"), 1)

            def centre(name, jobs):
                job0, _ = STD0[name]
                for n, (_, size, tiles) in enumerate(jobs):
                    dve.wait_ge(s("std_mean"), job0 + n + 1)
                    for tile in tiles:
                        dve.scalar_tensor_tensor(tile, std_slots[n], -1.0 / size, tile, ALU.mult, ALU.add)\
                           .then_inc(s("std_centred"), 1)

            def scaled(name, n, t, tile, gain=None):
                job0, done = STD0[name]
                dve.wait_ge(s("std_root"), job0 + n + 1)
                dve.wait_ge(s("std_centred"), done + t + 1)
                if gain is None:
                    ins = dve.tensor_tensor(tile, tile, lo_free[:, n, :], ALU.mult)
                else:
                    ins = dve.scalar_tensor_tensor(tile, tile, gain, lo_free[:, n, :], ALU.mult, ALU.mult)
                ins.then_inc(s("std_scaled"), 1)

            h_tile = lambda k: W[:, k, :]
            y_tile = lambda k: W[:, 8 + k, :]

            for free in ("ml_kept", "ml_h", "xa_o_lo", "sw_o_lo", "hg_kept", "hg_S"):
                dve.sem_inc(s(free), 1)
            dve.memset(epsc[:, 0:1], RMS_EPS).then_inc(s("eps"), 1)
            dve.memset(epsc[:, 1:2], LN_EPS).then_inc(s("eps"), 1)
            dve.wait_ge(s("consts"), 32)
            for k in range(KT):
                split_low("z1", k, h_tile, "mix1")
            have_rstd("z1")

            def evacuate(j, dst):
                product("z1", j)
                dve.tensor_tensor(dst, slot("z1", j), rstd[:, :], ALU.mult).then_inc(s("evacuated"), 1)

            def conv(acc, x, weight, bias, taps, lo, hi):
                for n in range(lo, hi):
                    w = weight(taps - 1 - n)
                    if n == 0:
                        ins = dve.tensor_scalar(acc, x, w, bias, ALU.mult, ALU.add)
                    else:
                        ins = dve.scalar_tensor_tensor(acc[:, n:T], x[:, 0:T - n], w, acc[:, n:T], ALU.mult, ALU.add)
                    link(ins)

            def conv_b(n, lo, hi):
                conv(W[:, 2 + n, :], W[:, n, :], lambda j: col("cb_w", 31 * n + j), col("cb_b", n), 31, lo, hi)

            def conv_c(n):
                conv(W[:, 16 + n, :], W[:, 4 + n, :], lambda j: col("cc_w", 4 * n + j), col("cc_b", n), 4, 0, 4)
                dve.sem_inc(s("cc_done"), 1)

            product("z1", 0)
            dve.tensor_tensor(rowA, slot("z1", 0), rstd[:, :], ALU.mult).then_inc(s("evacuated"), 1)
            dve.wait_ge(s("evacuated"), 1)
            H4 = slice(0, NH)
            link(dve.tensor_scalar(rowF[H4], rowA[32:36, :], cols[32:36, COL["gate_b"]:COL["gate_b"] + 1], None, ALU.add))
            link(dve.tensor_scalar(rowA[H4], rowA[H4], cols[H4, COL["gate_b"]:COL["gate_b"] + 1], None, ALU.add))
            dve.sem_inc(s("row_forget"), 1)
            link(dve.memset(rowM[H4], 1.0))
            chunked = lambda v: v[H4].rearrange("p (c t) -> p c t", t=CH)
            link(dve.memset(chunked(rowM)[:, :, 0:1], 0.0))
            dve.wait_ge(s("row_abs"), 1)
            link(dve.tensor_scalar(rowF[H4], rowF[H4], 0.0, None, ALU.min))
            dve.wait_ge(s("row_log"), 1)
            link(dve.tensor_tensor(rowF[H4], rowF[H4], rowE[H4], ALU.subtract))
            link(dve.tensor_tensor_scan(rowE[H4], rowM[H4], rowF[H4], 0.0, ALU.mult, ALU.add))
            link(dve.tensor_tensor(rowA[H4], rowA[H4], rowE[H4], ALU.subtract))
            link(dve.memset(rowF[H4], 0.0))
            link(dve.tensor_copy(chunked(rowF)[:, 1:NCH, 0:1], chunked(rowE)[:, 0:NCH - 1, CH - 1:CH]))
            link(dve.tensor_tensor_scan(rowM[H4], rowF[H4], rowA[H4], 0.0, ALU.add, ALU.max))
            mprev = small[H4, 40:48].rearrange("p (c t) -> p c t", t=1)
            link(dve.memset(mprev[:, 0:1, :], 0.0))
            link(dve.tensor_tensor(mprev[:, 1:NCH, :], chunked(rowM)[:, 0:NCH - 1, CH - 1:CH],
                                   chunked(rowE)[:, 0:NCH - 1, CH - 1:CH], ALU.add))
            link(dve.tensor_tensor(chunked(rowF), mprev.to_broadcast([NH, NCH, CH]), chunked(rowM), ALU.subtract))
            link(dve.scalar_tensor_tensor(rowE[H4], rowE[H4], -1.0, rowM[H4], ALU.mult, ALU.subtract))
            link(dve.tensor_scalar(rowM[H4], rowM[H4], -1.0, None, ALU.mult))
            dve.sem_inc(s("ml_rows"), 1)

            for j in range(4):
                evacuate(1 + j, W[:, j, :])
            for n in range(2):
                dve.wait_ge(s("cf_gate"), n + 1)
                link(dve.tensor_tensor(W[:, n, :], W[:, n, :], W[:, 2 + n, :], ALU.mult))
            conv_b(0, 0, 3)
            for j in range(4):
                evacuate(5 + j, W[:, 4 + j, :])
                conv_b(0, 3 + 6 * j, 9 + 6 * j)
            dve.wait_ge(s("evacuated"), 9)
            conv_c(0)
            conv_c(1)
            for j in range(2):
                evacuate(9 + j, W[:, 8 + j, :])
                conv_c(2 + j)
            evacuate(11, W[:, 10, :])
            conv_b(0, 27, 31)
            dve.sem_inc(s("cb_done"), 1)
            evacuate(12, W[:, 11, :])
            conv_b(1, 0, 7)
            for j in range(4):
                evacuate(13 + j, W[:, 12 + j, :])
                conv_b(1, 7 + 6 * j, 13 + 6 * j)
            dve.sem_inc(s("cb_done"), 1)

            centre("mix", mix_jobs)
            dve.wait_ge(s("mix_in"), 80)
            link(dve.tensor_scalar(W[:, 0, 0:P], const("ml_mask"), 0.0, None, ALU.is_gt))
            dve.tensor_tensor(wsT.rearrange("p (h t) -> p h t", h=NH), wsT.rearrange("p (h t) -> p h t", h=NH),
                              W[:, 0:1, 0:P].to_broadcast([P, NH, P]), ALU.mult).then_inc(s("ws_masked"), 1)
            scaled("mix", 0, 0, W[:, 10, :])
            scaled("mix", 0, 1, W[:, 11, :])
            scaled("mix", 1, 2, W[:, 2, :])
            scaled("mix", 2, 3, W[:, 3, :])
            for n in range(2):
                low("y1", 2 + n, W[:, 2 + n, :], n + 1)
            dve.wait_ge(s("ws_masked"), 1)
            dve.wait_ge(s("gm_mixed"), 1)
            dve.wait_ge(s("ln_out"), 2)
            for k in range(2):
                link(dve.tensor_tensor(W[:, k, :].rearrange("p (c t) -> p c t", t=CH),
                                       N[:, k, :].rearrange("p (c t) -> p c t", t=CH),
                                       bsv[:, k:k + 1, :].to_broadcast([P, NCH, CH]), ALU.add))
                dve.tensor_tensor(W[:, k, :], W[:, k, :], W[:, 8 + k, :], ALU.mult).then_inc(s("gm_y"), 1)
            for k in range(2):
                low("y1", k, W[:, k, :], 3 + k)
            dve.wait_ge(s("y1_lo"), 4)
            dve.sem_inc(s("ml_free"), 1)
            dve.memset(Cst, 0.0).then_inc(s("ml_init"), 1)
            dve.memset(vt[:, :, P:2 * P], 1.0).then_inc(s("ml_init"), 1)
            dve.wait_ge(s("ml_init"), 2)
            mask = const("ml_mask").rearrange("p (a t) -> p a t", a=1).to_broadcast([P, NH, P])

            def bounded(c):
                dve.wait_ge(s("ml_spread"), c + 1)
                dve.tensor_tensor(Et, Nb[0], mask, ALU.min).then_inc(s("ml_bounded"), 1)

            def mlstm(c, ahead=True):
                dve.wait_ge(s("ml_exp"), 3 * c + 1)
                dve.wait_ge(s("ml_qkv"), 3 * c + 1)
                dve.tensor_tensor(qw, qT, winter, ALU.mult).then_inc(s("ml_weighted"), 1)
                dve.wait_ge(s("ml_exp"), 3 * c + 3)
                dve.wait_ge(s("ml_proj"), 2 * c + 2)
                dve.tensor_tensor(kw, Gb[2], Wt[:, :, P - 1:P].to_broadcast([P, NH, P]), ALU.mult)\
                   .then_inc(s("ml_weighted"), 1)
                dve.wait_ge(s("ml_scores"), c + 1)
                dve.tensor_tensor(Pm, Nb[1], Wt, ALU.mult).then_inc(s("ml_weighted"), 1)
                dve.wait_ge(s("ml_den"), c + 1)
                link(dve.tensor_tensor(dn, dn, emm, ALU.max))
                link(dve.reciprocal(dn, dn))
                dve.tensor_tensor(Wc[:, 4:8, c, :], Gb[0], dn, ALU.mult).then_inc(s("ml_h"), 1)
                dve.wait_ge(s("ml_update"), c + 1)
                for h in range(NH):
                    last = dve.scalar_tensor_tensor(Cst[:, h, :], Cst[:, h, :], winter[:, h, P - 1:P],
                                                    Gf[:, T + 256 * h:T + 256 * h + 256], ALU.mult, ALU.add)
                last.then_inc(s("ml_kept"), 1)
                if ahead:
                    bounded(c + 1)

            bounded(0)
            with dve.Fori(0, NCH - 1) as c:
                chain.enter(c, 0, 2)
                mlstm(c)
            chain.leave(NCH - 1)
            mlstm(NCH - 1, False)
            dve.wait_ge(s("ml_h"), NCH + 1)
            dve.wait_ge(s("ml_kept"), NCH + 1)
            centre("hn", hn_jobs)
            dve.wait_ge(s("ogate"), 4)
            for n in range(4):
                scaled("hn", n, n, W[:, 4 + n, :], col("hn_g", n))
                dve.wait_ge(s("std_scaled"), STD0["hn"][1] + n + 1)
                link(dve.scalar_tensor_tensor(W[:, 16 + n, :], W[:, 16 + n, :], col("skip", n), W[:, 4 + n, :],
                                              ALU.mult, ALU.add))
                dve.tensor_tensor(W[:, 4 + n, :], W[:, 16 + n, :], W[:, 12 + n, :], ALU.mult).then_inc(s("ml_y"), 1)
                dve.wait_ge(s("ml_y"), n + 1)
                if n:
                    low("y1", 3 + n, W[:, 3 + n, :], 4 + n)
            low("y1", 7, W[:, 7, :], 8)

            def memory(x):
                mem = flat[:, 20 * T:22 * T]
                dve.wait_ge(s(x + "_mem_root"), 1)
                m3 = mem.rearrange("p (k m) -> p k m", m=MEM)
                dve.tensor_tensor(m3, m3, W[:, 14:15, 0:MEM].to_broadcast([P, KT, MEM]), ALU.mult)\
                   .then_inc(s(x + "_mem_scaled"), 1)
                dve.wait_ge(s(x + "_mem_scaled"), 1)
                for k in range(KT):
                    dve.wait_ge(s(x + "_mem_hi"), k + 1)
                    dve.scalar_tensor_tensor(m_lo[:, k, :], m3[:, k, :], col("mem" + x, k), m_hi[:, k, :].bitcast(F32),
                                             ALU.mult, ALU.subtract).then_inc(s("mem_lo"), 1)

            def weights_low(x, n):
                ws = (BLOCK0["k" + x] + n) % 2
                dve.wait_ge(s("kv_high"), KV0[x] + n + 1)
                dve.tensor_tensor(w_lo[:, ws, :], w_raw[:, ws, :], w_hi[:, ws, :].bitcast(F32), ALU.subtract)\
                   .then_inc(s("kv_low"), 1)

            def key(x, n):
                product("k" + x, n)
                dve.tensor_copy(keys[:, n, :], slot("k" + x, n)[:, 0:MEM]).then_inc(s("evacuated"), 1)

            def value(x, g):
                dve.wait_ge(s("product_quarters"), 4 * (BLOCK0["v" + x] + 4 * (g + 1)))
                dve.tensor_copy(values[:, :, g * HALF:(g + 1) * HALF], slot("v" + x, g).rearrange("p (m f) -> p m f", m=2))\
                   .then_inc(s("evacuated"), 1)

            def last_keys_and_values(x):
                key(x, KT - 2)
                weights_low(x, KT)
                key(x, KT - 1)
                for n in range(KT + 1, 2 * KT):
                    weights_low(x, n)
                for g in range(2):
                    value(x, g)

            def query_tiles(x):
                with dve.Fori(0, KT // 2) as n:
                    for j in range(2):
                        product("q" + x, n * 2 + j)
                        dve.scalar_tensor_tensor(queries[:, n * 2 + j, :], slot("q" + x, j), float(D // NH) ** -0.5,
                                                 rstd[:, :], ALU.mult, ALU.mult).then_inc(s("evacuated"), 1)

            def cross(x):
                score_slots = [Nf[:, 0:T], G[:, 1, :]]
                pr = TMP[:, 1, :].rearrange("p (h m) -> p h m", h=NH)

                def largest(c, slot):
                    dve.wait_ge(s("xa_scores"), c + 1 + XA0[x])
                    link(dve.tensor_reduce(small[:, 20 * slot:20 * slot + 4], score_slots[slot].rearrange("p (h m) -> p h m", h=NH), AX,
                                           ALU.max))
                    dve.tensor_scalar(small[:, 4 + 12 * slot:8 + 12 * slot], small[:, 20 * slot:20 * slot + 4], -1.0, None, ALU.mult)\
                       .then_inc(s("xa_negmax"), 1)

                def probs(c):
                    dve.wait_ge(s("xa_exps"), c + 1 + XA0[x])
                    link(dve.reciprocal(small[:, 12:16], small[:, 8:12]))
                    dve.tensor_tensor(pr, pr, small[:, 12:16].rearrange("p (h m) -> p h m", m=1).to_broadcast([P, NH, MEM]),
                                      ALU.mult).then_inc(s("xa_probs"), 1)

                def low_part(c):
                    dve.wait_ge(s("xa_o_hi"), c + 1 + XA0[x])
                    dve.tensor_tensor(loc[:, :, c, :], G[:, 0, :].rearrange("p (k t) -> p k t", k=KT), hicf[:, :, c, :],
                                      ALU.subtract).then_inc(s("xa_o_lo"), 1)

                largest(0, 0)
                largest(1, 1)
                probs(0)
                with dve.Fori(0, (NCH - 2) // 2) as i:
                    chain.enter(i, 0, 4)
                    for n in range(2):
                        probs(i * 2 + (n + 1))
                        largest(i * 2 + (n + 2), n)
                        low_part(i * 2 + n)
                chain.leave((NCH - 2) // 2)
                probs(NCH - 1)
                low_part(NCH - 2)
                low_part(NCH - 1)

            def ffn(name, target, conv_tiles):
                cf = cols[:, COL["cf"]:COL["cf"] + 4 * FT].rearrange("p (c j) -> p c j", j=8)

                def hidden(c):
                    static = isinstance(c, int)
                    for j in range(4):
                        dve.wait_ge(s("product_quarters"), 24 * c + 4 * (BLOCK0[name] + 1 + j) if static
                                    else c * 24 + 4 * (BLOCK0[name] - 1 + j))
                        dve.tensor_tensor(TMP[:, j, :], slot(name, j), rstd[:, :], ALU.mult).then_inc(s("evacuated"), 1)
                        if j < 2:
                            dve.wait_ge(s("evacuated"), c * 12 + (PROD0[name] + j + 1) if static
                                        else c * 12 + (PROD0[name] + j - 7))
                        if conv_tiles and j < 2:
                            acc, x = W[:, 16 + j, :], TMP[:, j, :]
                            w = lambda n: cf[:, c, 4 * j + n:4 * j + n + 1]
                            link(dve.tensor_scalar(acc, x, w(2), w(3), ALU.mult, ALU.add))
                            link(dve.scalar_tensor_tensor(acc[:, 1:T], x[:, 0:T - 1], w(1), acc[:, 1:T], ALU.mult, ALU.add))
                            dve.scalar_tensor_tensor(acc[:, 2:T], x[:, 0:T - 2], w(0), acc[:, 2:T], ALU.mult, ALU.add)\
                               .then_inc(s("ff_gate_in"), 1)
                        elif j < 2:
                            dve.sem_inc(s("ff_gate_in"), 1)
                    for j in range(2):
                        dve.wait_ge(s("evacuated"), c * 12 + (PROD0[name] + j + 3) if static
                                    else c * 12 + (PROD0[name] + j - 5))
                        dve.wait_ge(s("ff_gate"), 2 * c + j + 1 + FF0[name])
                        dve.tensor_tensor(W[:, 16 + j, :], W[:, 16 + j, :], TMP[:, 2 + j, :], ALU.mult)\
                           .then_inc(s("ff_hidden"), 1)

                def low_parts(c):
                    for j in range(2):
                        dve.wait_ge(s("ff_g_hi"), 2 * c + j + 1 + FF0[name])
                        dve.tensor_tensor(g_lo[:, j, :], W[:, 16 + j, :], g_hi[:, j, :].bitcast(F32), ALU.subtract)\
                           .then_inc(s("ff_g_lo"), 1)

                def add_down(c):
                    for o in range(KT):
                        first = 4 * (BLOCK0[name] + 8) + o + 1
                        dve.wait_ge(s("product_quarters"), c * 24 + (first - 24))
                        dve.tensor_tensor(target(o), target(o), slot(name, 4 + o), ALU.add).then_inc(s("evacuated"), 1)

                hidden(0)
                low_parts(0)
                with dve.Fori(1, FC) as c:
                    if conv_tiles:
                        chain.enter(c, 1, 4)
                    hidden(c)
                    add_down(c)
                    low_parts(c)
                if conv_tiles:
                    chain.leave(FC - 1)

            def last_down(name, target, norm):
                for o in range(KT):
                    dve.wait_ge(s("product_quarters"), 4 * (BLOCK0[name] + 6 * FC - 2) + o + 1)
                    dve.tensor_tensor(target(o), target(o), slot(name, o), ALU.add).then_inc(s("evacuated"), 1)
                    if o:
                        sums(norm, o - 1)
                sums(norm, KT - 1)

            def to_tiles(name, norm, target, add, loaded=None, beside=None):
                for j in range(KT):
                    product(name, j)
                    if loaded:
                        dve.wait_ge(*loaded(j))
                    if add:
                        ins = dve.tensor_tensor(target(j), target(j), slot(name, j), ALU.add)
                    else:
                        ins = dve.tensor_copy(target(j), slot(name, j))
                    ins.then_inc(s("evacuated"), 1)
                    if j == 1 and beside:
                        beside()
                    if j:
                        sums(norm, j - 1)
                sums(norm, KT - 1)

            def operand(name, gain):
                for k in range(KT):
                    split_low(name, k, h_tile, gain)
                have_rstd(name)

            to_tiles("out1", "q1", h_tile, True, lambda j: (s(f"x_in{j}"), 32), lambda: memory("1"))
            for k in range(KT):
                weights_low("1", k)
                split_low("q1", k, h_tile, "x1")
                if k > 1:
                    key("1", k - 2)
            last_keys_and_values("1")
            have_rstd("q1")
            query_tiles("1")
            cross("1")
            to_tiles("xo1", "ffn1", h_tile, True)
            operand("ffn1", "ffn1")
            ffn("ffn1", h_tile, True)
            last_down("ffn1", h_tile, "final")
            have_rstd("final")
            for k in range(KT):
                dve.scalar_tensor_tensor(W[:, k, :], W[:, k, :], col("final", k), rstd[:, :], ALU.mult, ALU.mult)\
                   .then_inc(s("h_final"), 1)
                if k:
                    split_low("z2", k - 1, h_tile, "mix2")
            split_low("z2", KT - 1, h_tile, "mix2")
            have_rstd("z2")
            dve.wait_ge(s("parked"), 16 * KT)
            for j in range(22):
                product("z2", j)
                dve.tensor_tensor(W[:, j, :], slot("z2", j), rstd[:, :], ALU.mult).then_inc(s("evacuated"), 1)
                if j == 8:
                    lb = cols[:, COL["lb"]:COL["lb"] + 8]
                    link(dve.tensor_tensor(small[:, 48:52], lb[:, 4:8], lb[:, 0:4], ALU.subtract))
                    dve.sem_inc(s("lb_diff"), 1)
                    dve.wait_ge(s("lb_exp"), 1)
                    link(dve.tensor_scalar(small[:, 48:52], small[:, 48:52], 1.0, None, ALU.add))
                    link(dve.reciprocal(small[:, 48:52], small[:, 48:52]))
                    link(dve.tensor_scalar(small[:, 52:56], small[:, 48:52], -1.0, 1.0, ALU.mult, ALU.add))
                if j > 15 and j < 20:
                    dve.wait_ge(s("z2_act"), j - 7)
                    link(dve.tensor_scalar(W[:, j - 4, :], W[:, j - 4, :], col("onorm", 0), None, ALU.mult))
                if 8 < j <= 12:
                    n = j - 9
                    dve.wait_ge(s("z2_act"), 4 + n + 1)
                    dve.tensor_scalar(W[:, 4 + n, :], W[:, 4 + n, :], small[:, 52 + n:53 + n], small[:, 48 + n:49 + n],
                                      ALU.mult, ALU.add).then_inc(s("hg_f"), 1)

            sinks = cols[:, COL["sinks"]:COL["sinks"] + 8]
            pr = sw_pr.rearrange("p (h m) -> p h m", m=256)
            s3 = Nf.rearrange("p (h m) -> p h m", m=256)
            Q1, K1, K2, AT, S, lf, b_, D1 = hg("Q1 K1 K2 AT S lf b D1")
            Q2, Eb = hg("Q20 Q21"), hg("Eb0 Eb1")
            qscale = float(P) ** -0.5
            dve.wait_ge(s("evacuated"), PROD0["out2"])
            link(dve.memset(AT, 0.0))
            link(dve.memset(S, 0.0))
            dve.sem_inc(s("hg_init"), 1)
            dve.wait_ge(s("phase2_in"), 16)
            hmask = const("hg_mask").bitcast(U32).rearrange("p (a t) -> p a t", a=1).to_broadcast([P, NH, P])
            halves = lambda v: v.rearrange("p h (a t) -> p (h a) t", t=64)

            def attention_low(c):
                dve.wait_ge(s("sw_o_hi"), c + 1)
                dve.tensor_tensor(loc[:, 0:4, c, :], Gb[0], hicf[:, 0:4, c, :], ALU.subtract).then_inc(s("sw_o_lo"), 1)

            def decays(c):
                dve.wait_ge(s("hg_log"), c + 1)
                link(dve.tensor_tensor_scan(b_.rearrange("p h t -> p (h t)"), phase[:, :],
                                            lf.rearrange("p h t -> p (h t)"), 0.0, ALU.mult, ALU.add))
                dve.tensor_tensor(halves(D1), halves(b_), halves(b_)[:, :, 31:32].to_broadcast([P, 8, 64]), ALU.subtract)\
                   .then_inc(s("hg_d"), 1)
                dve.tensor_tensor(halves(K2), halves(b_)[:, :, 63:64].to_broadcast([P, 8, 64]), halves(b_), ALU.subtract)\
                   .then_inc(s("hg_d"), 1)

            def weighted(c, odd):
                q_, f_ = Wc[:, 0:4, c, :], Wc[:, 4:8, c, :]
                dve.wait_ge(s("hg_exp"), 4 * c + 4)
                dve.scalar_tensor_tensor(K2, f_, 1.0, K2, ALU.subtract, ALU.mult, reverse0=True).then_inc(s("hg_qk"), 1)
                dve.scalar_tensor_tensor(Q1, q_, qscale, Q1, ALU.mult, ALU.mult).then_inc(s("hg_qk"), 1)
                dve.scalar_tensor_tensor(K1, f_, 1.0, K1, ALU.subtract, ALU.mult, reverse0=True).then_inc(s("hg_qk"), 1)
                dve.scalar_tensor_tensor(Q2[odd], q_, qscale, Eb[odd], ALU.mult, ALU.mult).then_inc(s("hg_qk"), 1)

            def state(c, odd, sub):
                dve.wait_ge(s("hg_update"), 2 * c + (sub + 1))
                if sub:
                    dve.wait_ge(s("hg_S"), 2 * c + 2)
                for h in range(NH):
                    last = dve.scalar_tensor_tensor(S[:, h, :], S[:, h, :], Eb[odd][:, h, 64 * sub + 63:64 * sub + 64],
                                                    Nb[2 + sub][:, h, :], ALU.mult, ALU.add)
                last.then_inc(s("hg_S"), 1)

            def gated(c):
                dve.wait_ge(s("hg_squares"), c + 1)
                dve.tensor_tensor(Wc[:, 0:4, c, :], Wc[:, 0:4, c, :], Wc[:, 12:16, c, :], ALU.mult).then_inc(s("hg_gated"), 1)

            def mixer2(c, odd, ahead=True):
                first = isinstance(c, int) and c == 0
                mask = const("swa_first" if first else "swa_rest", 256).rearrange("p (a t) -> p a t", a=1)
                if not first:
                    attention_low(c - 1)
                for g in range(2):
                    heads_g, of = slice(4 * g, 4 * g + 4), lambda n: small[:, n + 4 * g:n + 4 * g + 4]
                    dve.wait_ge(s("sw_scores"), 2 * c + (g + 1))
                    link(dve.scalar_tensor_tensor(pr[:, heads_g, :], s3[:, heads_g, :], 0.125,
                                                  mask.to_broadcast([P, 4, 256]), ALU.mult, ALU.min))
                    link(dve.tensor_reduce(of(0), pr[:, heads_g, :], AX, ALU.max))
                    link(dve.tensor_tensor(of(0), of(0), sinks[:, heads_g], ALU.max))
                    link(dve.tensor_tensor(of(32), sinks[:, heads_g], of(0), ALU.subtract))
                    dve.tensor_scalar(of(8), of(0), -1.0, None, ALU.mult).then_inc(s("sw_negmax"), 1)
                    if g == 0:
                        dve.wait_ge(s("hg_scores"), c + 1)
                        dve.memset(small[:, 60:61], 0.0)
                        dve.copy_predicated(AT, hmask, Gb[0]).then_inc(s("hg_masked"), 1)
                for g in range(2):
                    of = lambda n: small[:, n + 4 * g:n + 4 * g + 4]
                    dve.wait_ge(s("sw_exps"), 2 * c + (g + 1))
                    link(dve.tensor_tensor(of(16), of(16), of(24), ALU.add))
                    link(dve.reciprocal(of(16), of(16)))
                    pg = pr[:, 4 * g:4 * g + 4, :]
                    dve.tensor_tensor(pg, pg, of(16).rearrange("p (h m) -> p h m", m=1).to_broadcast([P, 4, 256]),
                                      ALU.mult).then_inc(s("sw_probs"), 1)
                state(c, odd, 0)
                if ahead:
                    decays(c + 1)
                if not first:
                    gated(c - 1)
                state(c, odd, 1)
                dve.tensor_scalar(Wc[:, 0:4, c, :], Nb[1], 1.0, None, ALU.mult).then_inc(s("hg_kept"), 1)
                if ahead:
                    weighted(c + 1, 1 - odd)

            decays(0)
            weighted(0, 0)
            mixer2(0, 0)
            with dve.Fori(0, NCH // 2 - 1) as i:
                chain.enter(i, 0, 26)
                for n in (1, 2):
                    mixer2(i * 2 + n, n % 2)
            chain.leave(NCH // 2 - 1)
            mixer2(NCH - 1, 1, False)
            attention_low(NCH - 1)
            gated(NCH - 1)
            dve.wait_ge(s("hg_gated"), NCH)
            for n in range(4):
                dve.wait_ge(s("hr_root"), n + 1)
                dve.tensor_tensor(W[:, n, :], W[:, n, :], W[:, 16 + n, :], ALU.mult).then_inc(s("hr_y"), 1)
                if n:
                    low("y2", 3 + n, W[:, n - 1, :], n)
            dve.wait_ge(s("hr_y"), 4)
            low("y2", 7, W[:, 3, :], 4)

            def normalised(name, k, gain):
                dve.scalar_tensor_tensor(W[:, 8 + k, :], W[:, 8 + k, :], col(gain, k), rstd[:, :], ALU.mult, ALU.mult)\
                   .then_inc(s(name + "_y"), 1)

            def post(name, nxt, post_gain, gain, loaded, beside):
                have_rstd(name)
                for k in range(KT):
                    dve.wait_ge(*loaded(k))
                    link(dve.scalar_tensor_tensor(root, W[:, 8 + k, :], col(post_gain, k), rstd[:, :], ALU.mult, ALU.mult))
                    dve.tensor_tensor(W[:, k, :], W[:, k, :], root, ALU.add).then_inc(s(name + "_h"), 1)
                    dve.wait_ge(s(name + "_h"), k + 1)
                    beside(k)
                    if k:
                        split_low(nxt, k - 1, h_tile, gain)
                        sums(nxt, k - 1)
                split_low(nxt, KT - 1, h_tile, gain)
                sums(nxt, KT - 1)

            to_tiles("out2", "pm", y_tile, False, None, lambda: memory("2"))
            post("pm", "q2", "post_mix", "x2", lambda k: (s(f"x_in{k}"), 48),
                 lambda k: key("2", k - 2) if k > 1 else None)
            last_keys_and_values("2")
            have_rstd("q2")
            query_tiles("2")
            cross("2")
            to_tiles("xo2", "px", y_tile, False)
            have_rstd("px")
            for k in range(KT):
                normalised("px", k, "post_x")
                if k > 1:
                    dve.wait_ge(s("px_h"), k - 1)
                    split_low("ffn2", k - 2, h_tile, "ffn2")
            for k in (KT - 2, KT - 1):
                dve.wait_ge(s("px_h"), k + 1)
                split_low("ffn2", k, h_tile, "ffn2")
            have_rstd("ffn2")
            link(dve.memset(W[:, 8:16, :], 0.0))
            ffn("ffn2", y_tile, False)
            last_down("ffn2", y_tile, "pf")
            have_rstd("pf")
            for k in range(KT):
                normalised("pf", k, "post_ffn")
                if k % 2 == 0:
                    dve.wait_ge(s("pf_y"), k + 1)
                    dve.tensor_tensor(W[:, k, :], W[:, k, :], W[:, 8 + k, :], ALU.add).then_inc(s("pf_h"), 1)


def packed(w):
    return w.reshape(KT, P, -1, P).transpose(2, 1, 0, 3).reshape(-1, P, KT * P)


def packed_values(w):
    return w.reshape(4, 2, P, 2, HALF).transpose(3, 0, 2, 1, 4).reshape(KT, P, KT * P)


def packed_down(w, c):
    w = w[2 * P * c:2 * P * (c + 1)].reshape(2, P, 2, 4, P)
    return w.transpose(2, 1, 3, 0, 4).reshape(2, P, KT * P)


def packed_ffn(gate, up, down):
    gate, up = packed(gate), packed(up)
    out = []
    for c in range(FC + 1):
        if c < FC:
            out += [gate[2 * c:2 * c + 2], up[2 * c:2 * c + 2]]
        if c:
            out.append(packed_down(down, c - 1))
    return out


def columns(v):
    return v.reshape(-1, P).T


def constants():
    c = np.zeros((P, NCONST), np.float32)

    def put(name, value):
        c[:value.shape[0], CST[name]:CST[name] + value.shape[1]] = value

    r = np.arange(P)
    put("ident", np.eye(P))
    put("ones", np.ones((P, P)))
    put("blk", (r[:, None] // 64 == r[None] // 64) * 1.0)
    put("ml_mask", np.where(r[:, None] <= r[None], BIG, NEG))
    key, query = np.arange(256)[None] // 64, r[:, None] // 64
    seen = (key >= query) & (key <= query + 2)
    put("swa_rest", np.where(seen, BIG, NEG))
    put("swa_first", np.where(seen & (key >= 2), BIG, NEG))
    put("hg_mask", ((r[:, None] // 64 == r[None] // 64) & (r[:, None] <= r[None])) * 1.0)
    put("hg_reset", np.tile((np.arange(512) % 64 != 0) * 1.0, (P, 1)))
    put("sel", np.repeat(np.eye(NH), P, axis=1))
    return c


def kernel(**inputs):
    import concourse.bacc as bacc
    from concourse.bass_utils import run_bass_kernel_spmd

    i = {name: np.asarray(a) for name, a in inputs.items()}
    v = {name: a[0] for name, a in i.items() if name not in ("final_g",)}
    w_in = v["w_in"]
    gates = np.zeros((D, P), np.float32)
    gates[:, 0:NH] = w_in[:, 2048:2052]
    gates[:, 32:32 + NH] = w_in[:, 2052:2056]
    z1 = np.concatenate([gates, w_in[:, 512:1024], w_in[:, 1024:1536], w_in[:, 0:512], w_in[:, 1536:2048]], 1)
    w2 = v["w_in_2"]
    pair = [64 * h + d for n in range(4) for h in (n, 4 + n) for d in range(64)]
    z2 = np.concatenate([w2[:, 768:2816], w2[:, 0:512][:, pair], w2[:, 512:768]], 1)
    w_out2 = np.concatenate([v["w_out_2"][0:512][pair], v["w_out_2"][512:]], 0)
    stream = [packed(z1), packed(v["w_out"]), packed(v["w_xkv"][:, :D]), packed_values(v["w_xkv"][:, D:]), packed(v["w_xq"]), packed(v["w_xo"]),
              *packed_ffn(v["w_up"][:, :FT * P], v["w_up"][:, FT * P:], v["w_down"]),
              packed(z2), packed(w_out2), packed(v["wk_x_2"]), packed_values(v["wv_x_2"]), packed(v["wq_x_2"]),
              packed(v["wo_x_2"]), *packed_ffn(v["w_gate_2"], v["w_up_2"], v["w_down_2"])]
    gate_b = np.zeros((P, 1), np.float32)
    gate_b[0:NH, 0], gate_b[32:32 + NH, 0] = v["b_igate"], v["b_fgate"]
    conv_f = np.concatenate([v["conv_f_w"], v["conv_f_b"][None]], 0)
    by = {"mix1": columns(v["norm_mix_g"]), "lna_g": columns(v["ln_a_g"]), "lna_b": columns(v["ln_a_b"]),
          "cb_w": columns(v["conv_b_w"].reshape(31, 2, P).transpose(1, 0, 2)),
          "cb_b": columns(v["conv_b_b"]), "gnb_g": columns(v["gn_b_g"]), "gnb_b": columns(v["gn_b_b"]),
          "cc_w": columns(v["conv_c_w"].reshape(4, 4, P).transpose(1, 0, 2)), "cc_b": columns(v["conv_c_b"]),
          "hn_g": columns(v["hn_c_g"]), "skip": columns(v["skip_c"]), "x1": columns(v["norm_x_g"]),
          "mem1": columns(v["norm_mem_g"]), "ffn1": columns(v["norm_ffn_g"]),
          "cf": columns(conv_f.reshape(4, FT, P).transpose(1, 0, 2)), "final": columns(i["final_g"]),
          "mix2": columns(v["g_mix_pre_2"]), "post_mix": columns(v["g_mix_post_2"]), "mem2": columns(v["g_mem_2"]),
          "x2": columns(v["g_x_pre_2"]), "post_x": columns(v["g_x_post_2"]), "ffn2": columns(v["g_ffn_pre_2"]),
          "post_ffn": columns(v["g_ffn_post_2"]), "lb": columns(i["hgrn_lb_2"]), "onorm": columns(v["hgrn_onorm_2"]),
          "sinks": np.broadcast_to(v["sinks_2"], (P, 8)), "gate_b": gate_b}
    tiles = lambda a: a.T.reshape(KT, P, -1).transpose(1, 0, 2)
    arrays = {
        "wstream": np.concatenate(stream, 0),
        "cols": np.concatenate([by[name] for name, _ in COLS], 1),
        "consts": constants(),
        "xT": tiles(v["x"]),
        "memT1": tiles(v["mem"]).reshape(P, 2, T),
        "memT2": tiles(v["mem_2"]).reshape(P, 2, T),
        "w_q": v["w_q_c"].transpose(1, 0, 2).reshape(P, -1),
        "w_k": v["w_k_c"].transpose(1, 0, 2).reshape(P, -1),
        "w_v": v["w_v_c"].transpose(1, 0, 2).reshape(P, -1),
        "w_sT": v["w_s"].transpose(2, 0, 1).reshape(P, -1),
        "b_s": np.repeat(v["b_s"].reshape(2, 2, 1, P), 64, axis=2).reshape(2, P, P).transpose(1, 0, 2).reshape(P, -1),
    }
    arrays = {name: np.ascontiguousarray(a, np.float32) for name, a in arrays.items()}
    nc = bacc.Bacc("TRN2", target_bir_lowering=False, num_devices=1)
    ap = {name: nc.dram_tensor(name, a.shape, F32, kind="ExternalInput").ap() for name, a in arrays.items()}
    ap["out"] = nc.dram_tensor("out", (P, KT, T), F32, kind="ExternalOutput").ap()
    ap["parked"] = nc.dram_tensor("parked", (P, KT, T), F32, kind="Internal").ap()
    program(nc, ap)
    result = run_bass_kernel_spmd(nc, [arrays], core_ids=[0]).results[0]["out"]
    return np.asarray(result).transpose(2, 1, 0).reshape(1, T, D)
```
